# Optimizing a Trainium2 kernel written in Bass

```python
import math
import jax, jax.numpy as jnp
from jax import lax
import numpy as np

D_MODEL = 1024
BATCH = 1
SEQ = 256
DEPTH = 1

MEM_LEN = 256
DA_HEADS = 8
DA_HEAD_DIM = 64
DA_QK = DA_HEADS * 2 * DA_HEAD_DIM
DA_V = DA_HEADS * 2 * DA_HEAD_DIM
Q_BLOCK = 128
SSD_EXPAND = 2
SSD_INNER = SSD_EXPAND * D_MODEL
SSD_HEAD_DIM = 64
SSD_HEADS = SSD_INNER // SSD_HEAD_DIM
SSD_GROUPS = 4
SSD_HEADS_PER_GROUP = SSD_HEADS // SSD_GROUPS
SSD_STATE = 128
SSD_CONV = 4
SSD_CHUNK = 128
SSD_CONV_DIM = SSD_INNER + 2 * SSD_GROUPS * SSD_STATE
XA_HEADS = 4
XA_HEAD_DIM = D_MODEL // XA_HEADS
D_FF = 2816
N_BRANCH = 2
IN_SIZES = (DA_QK, DA_QK, DA_V, SSD_INNER, SSD_CONV_DIM, SSD_HEADS, N_BRANCH * D_MODEL)
IN_WIDTH = DA_QK + DA_QK + DA_V + SSD_INNER + SSD_CONV_DIM + SSD_HEADS + N_BRANCH * D_MODEL
NORM_EPS = 1e-6
SUBLN_EPS = 1e-5


def _rmsnorm(x, g, eps=NORM_EPS):
    xf = x.astype(jnp.float32)
    y = xf * lax.rsqrt(jnp.mean(xf * xf, axis=-1, keepdims=True) + eps)
    return (y * g.astype(jnp.float32)).astype(x.dtype)

def _swiglu(h, w_gu, w_down):
    g, u = jnp.split(h @ w_gu, 2, axis=-1)
    return (jax.nn.silu(g) * u) @ w_down

def _diff_attention(q, k, v, lam):
    b, s = q.shape[0], q.shape[1]
    q1, q2 = q[:, :, :, 0].transpose(0, 2, 1, 3), q[:, :, :, 1].transpose(0, 2, 1, 3)
    k1, k2 = k[:, :, :, 0].transpose(0, 2, 1, 3), k[:, :, :, 1].transpose(0, 2, 1, 3)
    vh = v.transpose(0, 2, 1, 3)
    nblk = s // Q_BLOCK
    scale = DA_HEAD_DIM ** -0.5
    key_pos = jnp.arange(s)

    def blocks(t):
        return t.reshape(b, DA_HEADS, nblk, Q_BLOCK, DA_HEAD_DIM).transpose(2, 0, 1, 3, 4)

    def one_block(args):
        q1b, q2b, start = args
        mask = (start + jnp.arange(Q_BLOCK))[:, None] >= key_pos[None, :]

        def probs(qb, kk):
            sc = jnp.einsum('bhqd,bhkd->bhqk', qb, kk).astype(jnp.float32) * scale
            return jax.nn.softmax(jnp.where(mask, sc, -jnp.inf), axis=-1)

        p = probs(q1b, k1) - lam * probs(q2b, k2)
        return jnp.einsum('bhqk,bhke->bhqe', p.astype(vh.dtype), vh)

    out = lax.map(one_block, (blocks(q1), blocks(q2), jnp.arange(nblk, dtype=jnp.int32) * Q_BLOCK))
    return out.transpose(1, 2, 0, 3, 4).reshape(b, DA_HEADS, s, 2 * DA_HEAD_DIM)

def _segsum(a):
    t = a.shape[-1]
    cs = jnp.cumsum(a, axis=-1)
    seg = cs[..., :, None] - cs[..., None, :]
    return jnp.where(jnp.tril(jnp.ones((t, t), dtype=bool)), seg, -jnp.inf)

def _ssd_chunked(xdt, adt, bm, cm):
    b, s = xdt.shape[0], xdt.shape[1]
    c = s // SSD_CHUNK
    G, R, P, N, Lc = SSD_GROUPS, SSD_HEADS_PER_GROUP, SSD_HEAD_DIM, SSD_STATE, SSD_CHUNK
    X = xdt.astype(jnp.float32).reshape(b, c, Lc, G, R, P)
    A = adt.astype(jnp.float32).reshape(b, c, Lc, G, R).transpose(0, 3, 4, 1, 2)
    Bc = bm.astype(jnp.float32).reshape(b, c, Lc, G, N)
    Cc = cm.astype(jnp.float32).reshape(b, c, Lc, G, N)
    a_cs = jnp.cumsum(A, axis=-1)
    Lmat = jnp.exp(_segsum(A))
    cb = jnp.einsum('bclgn,bcsgn->bgcls', Cc, Bc)
    y_diag = jnp.einsum('bgrcls,bcsgrp->bclgrp', cb[:, :, None] * Lmat, X)
    decay_states = jnp.exp(a_cs[..., -1:] - a_cs)
    states = jnp.einsum('bclgn,bgrcl,bclgrp->bcgrpn', Bc, decay_states, X)
    chunk_end = jnp.pad(a_cs[..., -1], ((0, 0), (0, 0), (0, 0), (1, 0)))
    decay_chunk = jnp.exp(_segsum(chunk_end))
    states = jnp.concatenate([jnp.zeros_like(states[:, :1]), states], axis=1)
    prev_states = jnp.einsum('bgrzc,bcgrpn->bzgrpn', decay_chunk, states)[:, :-1]
    y_off = jnp.einsum('bclgn,bcgrpn,bgrcl->bclgrp', Cc, prev_states, jnp.exp(a_cs))
    return (y_diag + y_off).reshape(b, s, SSD_HEADS, P)

def _depthwise_causal_conv(u, w, bias):
    y = lax.conv_general_dilated(u, w.astype(u.dtype)[:, None, :], window_strides=(1,),
                                 padding=[(SSD_CONV - 1, 0)],
                                 dimension_numbers=('NWC', 'WIO', 'NWC'),
                                 feature_group_count=u.shape[-1])
    return y + bias.astype(u.dtype)

def _layer(x, mem, layer_idx,
           ffn1_pre_g, ffn1_post_g, ffn1_w_gu, ffn1_w_down,
           mix_pre_g, mix_post_g, w_in, b_gate,
           da_lambda_q1, da_lambda_k1, da_lambda_q2, da_lambda_k2, da_subln_g,
           ssd_conv_w, ssd_conv_b, ssd_dt_bias, ssd_A_log, ssd_D, ssd_norm_g,
           w_branch_attn, w_branch_ssd, w_mix_out,
           xa_pre_g, xa_post_g, mem_norm_g, xa_w_q, xa_w_kv, xa_w_o,
           ffn2_pre_g, ffn2_post_g, ffn2_w_gu, ffn2_w_down):
    b, s, _ = x.shape
    x = x + 0.5 * _rmsnorm(_swiglu(_rmsnorm(x, ffn1_pre_g), ffn1_w_gu, ffn1_w_down), ffn1_post_g)

    h = _rmsnorm(x, mix_pre_g)
    cuts = [sum(IN_SIZES[:i + 1]) for i in range(len(IN_SIZES) - 1)]
    q, k, v, z, xbc, dt_raw, gate_logits = jnp.split(h @ w_in, cuts, axis=-1)

    lam_init = 0.8 - 0.6 * math.exp(-0.3 * layer_idx)
    lam = (jnp.exp(jnp.sum(da_lambda_q1 * da_lambda_k1).astype(jnp.float32))
           - jnp.exp(jnp.sum(da_lambda_q2 * da_lambda_k2).astype(jnp.float32)) + lam_init)
    o = _diff_attention(q.reshape(b, s, DA_HEADS, 2, DA_HEAD_DIM),
                        k.reshape(b, s, DA_HEADS, 2, DA_HEAD_DIM),
                        v.reshape(b, s, DA_HEADS, 2 * DA_HEAD_DIM), lam)
    o = _rmsnorm(o, da_subln_g, SUBLN_EPS) * (1.0 - lam_init)
    attn_out = o.transpose(0, 2, 1, 3).reshape(b, s, DA_V) @ w_branch_attn

    xbc = jax.nn.silu(_depthwise_causal_conv(xbc, ssd_conv_w, ssd_conv_b))
    xs, bm, cm = jnp.split(xbc, [SSD_INNER, SSD_INNER + SSD_GROUPS * SSD_STATE], axis=-1)
    dt = jax.nn.softplus(dt_raw.astype(jnp.float32) + ssd_dt_bias.astype(jnp.float32))
    a = -jnp.exp(ssd_A_log.astype(jnp.float32))
    xh = xs.reshape(b, s, SSD_HEADS, SSD_HEAD_DIM)
    y = _ssd_chunked(xh * dt[..., None], a * dt,
                     bm.reshape(b, s, SSD_GROUPS, SSD_STATE), cm.reshape(b, s, SSD_GROUPS, SSD_STATE))
    y = (y + ssd_D.astype(jnp.float32)[:, None] * xh).astype(x.dtype).reshape(b, s, SSD_INNER)
    yg = (y * jax.nn.silu(z)).reshape(b, s, SSD_GROUPS, SSD_INNER // SSD_GROUPS)
    y = _rmsnorm(yg, ssd_norm_g.reshape(SSD_GROUPS, SSD_INNER // SSD_GROUPS), SUBLN_EPS)
    ssd_out = y.reshape(b, s, SSD_INNER) @ w_branch_ssd

    g_attn, g_ssd = jnp.split(jax.nn.sigmoid(gate_logits + b_gate), N_BRANCH, axis=-1)
    mixed = (g_attn * attn_out + g_ssd * ssd_out) @ w_mix_out
    x = x + _rmsnorm(mixed, mix_post_g)

    hq = _rmsnorm(x, xa_pre_g)
    qx = (hq @ xa_w_q).reshape(b, s, XA_HEADS, XA_HEAD_DIM)
    kx, vx = jnp.split(_rmsnorm(mem, mem_norm_g) @ xa_w_kv, 2, axis=-1)
    m = mem.shape[1]
    kx = kx.reshape(b, m, XA_HEADS, XA_HEAD_DIM)
    vx = vx.reshape(b, m, XA_HEADS, XA_HEAD_DIM)
    sc = jnp.einsum('bqhd,bkhd->bhqk', qx, kx).astype(jnp.float32) * (XA_HEAD_DIM ** -0.5)
    p = jax.nn.softmax(sc, axis=-1).astype(vx.dtype)
    xo = jnp.einsum('bhqk,bkhd->bqhd', p, vx).reshape(b, s, D_MODEL) @ xa_w_o
    x = x + _rmsnorm(xo, xa_post_g)

    x = x + 0.5 * _rmsnorm(_swiglu(_rmsnorm(x, ffn2_pre_g), ffn2_w_gu, ffn2_w_down), ffn2_post_g)
    return x

def first_inputs(seed: int = 0) -> dict:
    key = jax.random.key(seed)
    ks = iter(jax.random.split(key, 48))
    L = DEPTH

    def nrm(shape, scale):
        return scale * jax.random.normal(next(ks), shape, jnp.float32)

    def gain(n):
        return 1.0 + 0.02 * jax.random.normal(next(ks), (L, n), jnp.float32)

    inp = {}
    inp["x"] = nrm((BATCH, SEQ, D_MODEL), 1.0)
    inp["mem"] = nrm((BATCH, MEM_LEN, D_MODEL), 1.0)
    inp["ffn1_pre_g"] = gain(D_MODEL)
    inp["ffn1_post_g"] = gain(D_MODEL)
    inp["ffn1_w_gu"] = nrm((L, D_MODEL, 2 * D_FF), D_MODEL ** -0.5)
    inp["ffn1_w_down"] = nrm((L, D_FF, D_MODEL), D_FF ** -0.5)
    inp["mix_pre_g"] = gain(D_MODEL)
    inp["mix_post_g"] = gain(D_MODEL)
    inp["w_in"] = nrm((L, D_MODEL, IN_WIDTH), D_MODEL ** -0.5)
    inp["b_gate"] = nrm((L, N_BRANCH * D_MODEL), 0.02)
    inp["da_lambda_q1"] = nrm((L, DA_HEAD_DIM), 0.1)
    inp["da_lambda_k1"] = nrm((L, DA_HEAD_DIM), 0.1)
    inp["da_lambda_q2"] = nrm((L, DA_HEAD_DIM), 0.1)
    inp["da_lambda_k2"] = nrm((L, DA_HEAD_DIM), 0.1)
    inp["da_subln_g"] = gain(2 * DA_HEAD_DIM)
    inp["ssd_conv_w"] = nrm((L, SSD_CONV, SSD_CONV_DIM), SSD_CONV ** -0.5)
    inp["ssd_conv_b"] = nrm((L, SSD_CONV_DIM), 0.02)
    u = jax.random.uniform(next(ks), (L, SSD_HEADS), jnp.float32)
    dt0 = jnp.exp(u * (math.log(0.1) - math.log(0.001)) + math.log(0.001))
    inp["ssd_dt_bias"] = dt0 + jnp.log(-jnp.expm1(-dt0))
    inp["ssd_A_log"] = jnp.log(jax.random.uniform(next(ks), (L, SSD_HEADS), jnp.float32, 1.0, 16.0))
    inp["ssd_D"] = 1.0 + nrm((L, SSD_HEADS), 0.1)
    inp["ssd_norm_g"] = gain(SSD_INNER)
    inp["w_branch_attn"] = nrm((L, DA_V, D_MODEL), DA_V ** -0.5)
    inp["w_branch_ssd"] = nrm((L, SSD_INNER, D_MODEL), SSD_INNER ** -0.5)
    inp["w_mix_out"] = nrm((L, D_MODEL, D_MODEL), D_MODEL ** -0.5)
    inp["xa_pre_g"] = gain(D_MODEL)
    inp["xa_post_g"] = gain(D_MODEL)
    inp["mem_norm_g"] = gain(D_MODEL)
    inp["xa_w_q"] = nrm((L, D_MODEL, D_MODEL), D_MODEL ** -0.5)
    inp["xa_w_kv"] = nrm((L, D_MODEL, 2 * D_MODEL), D_MODEL ** -0.5)
    inp["xa_w_o"] = nrm((L, D_MODEL, D_MODEL), D_MODEL ** -0.5)
    inp["ffn2_pre_g"] = gain(D_MODEL)
    inp["ffn2_post_g"] = gain(D_MODEL)
    inp["ffn2_w_gu"] = nrm((L, D_MODEL, 2 * D_FF), D_MODEL ** -0.5)
    inp["ffn2_w_down"] = nrm((L, D_FF, D_MODEL), D_FF ** -0.5)
    return inp

def first_block(x, mem, ffn1_pre_g, ffn1_post_g, ffn1_w_gu, ffn1_w_down,
              mix_pre_g, mix_post_g, w_in, b_gate,
              da_lambda_q1, da_lambda_k1, da_lambda_q2, da_lambda_k2, da_subln_g,
              ssd_conv_w, ssd_conv_b, ssd_dt_bias, ssd_A_log, ssd_D, ssd_norm_g,
              w_branch_attn, w_branch_ssd, w_mix_out,
              xa_pre_g, xa_post_g, mem_norm_g, xa_w_q, xa_w_kv, xa_w_o,
              ffn2_pre_g, ffn2_post_g, ffn2_w_gu, ffn2_w_down):
    for l in range(DEPTH):
        x = _layer(x, mem, l,
                   ffn1_pre_g[l], ffn1_post_g[l], ffn1_w_gu[l], ffn1_w_down[l],
                   mix_pre_g[l], mix_post_g[l], w_in[l], b_gate[l],
                   da_lambda_q1[l], da_lambda_k1[l], da_lambda_q2[l], da_lambda_k2[l], da_subln_g[l],
                   ssd_conv_w[l], ssd_conv_b[l], ssd_dt_bias[l], ssd_A_log[l], ssd_D[l], ssd_norm_g[l],
                   w_branch_attn[l], w_branch_ssd[l], w_mix_out[l],
                   xa_pre_g[l], xa_post_g[l], mem_norm_g[l], xa_w_q[l], xa_w_kv[l], xa_w_o[l],
                   ffn2_pre_g[l], ffn2_post_g[l], ffn2_w_gu[l], ffn2_w_down[l])
    return x


HY_WIDTH = 512
HY_ORDER = 2
SHORT_CONV = 3
FILTER_EMB = 33
FILTER_HIDDEN = 64
DECAY_TARGET = 1e-2
FAST_DECAY = 0.3
SLOW_DECAY = 1.5
MIN_DECAY = math.log(DECAY_TARGET) / SLOW_DECAY
MAX_DECAY = math.log(DECAY_TARGET) / FAST_DECAY

MLA_HEADS = 8
QK_NOPE = 64
QK_ROPE = 32
QK_DIM = QK_NOPE + QK_ROPE
V_DIM = 64
Q_LORA = 384
KV_LORA = 256
ATTN_WIDTH = MLA_HEADS * V_DIM
ROPE_THETA = 10000.0

EPS = 1e-6
IN_COLS = 4 * HY_WIDTH + Q_LORA + KV_LORA + QK_ROPE + ATTN_WIDTH + 2 * D_MODEL


def rms_norm(x, g):
    xf = x.astype(jnp.float32)
    y = xf * lax.rsqrt(jnp.mean(xf * xf, axis=-1, keepdims=True) + EPS)
    return (y * g.astype(jnp.float32)).astype(x.dtype)

def short_conv(u, w, b):
    L = u.shape[1]
    pad = SHORT_CONV // 2
    up = jnp.pad(u, ((0, 0), (pad, pad), (0, 0)))
    return sum(up[:, j:j + L] * w[j] for j in range(SHORT_CONV)) + b

def hyena_filter_spectra(L, w_f1, b_f1, freq_1, w_f2, b_f2, freq_2, w_f3):
    t = jnp.linspace(0.0, 1.0, L, dtype=jnp.float32)[:, None]
    bands = (FILTER_EMB - 1) // 2
    f = jnp.linspace(1e-4, bands - 1, bands, dtype=jnp.float32)
    ang = (2.0 * jnp.pi / L) * jnp.arange(L, dtype=jnp.float32)[:, None] * f[None, :]
    z = jnp.concatenate([t, jnp.cos(ang), -jnp.sin(ang)], axis=-1)
    h = jnp.sin(freq_1 * (z @ w_f1 + b_f1))
    h = jnp.sin(freq_2 * (h @ w_f2 + b_f2))
    k = (h @ w_f3).reshape(L, HY_ORDER, 2, HY_WIDTH)
    deltas = jnp.abs(jnp.linspace(MIN_DECAY, MAX_DECAY, HY_WIDTH, dtype=jnp.float32))
    decay = jnp.exp(-t * deltas)
    k = k * decay[:, None, None, :]
    k_full = jnp.concatenate([k[:, :, 0], k[::-1, :, 1]], axis=0)
    return jnp.fft.rfft(k_full.astype(jnp.float32), axis=0)

def long_conv(u, k_spec, bias):
    L = u.shape[1]
    uf = u.astype(jnp.float32)
    y = jnp.fft.irfft(jnp.fft.rfft(uf, n=2 * L, axis=1) * k_spec[None], n=2 * L, axis=1)[:, :L]
    return (y + uf * bias.astype(jnp.float32)).astype(u.dtype)

def rotary(t, cos, sin):
    t1, t2 = jnp.split(t, 2, axis=-1)
    c = cos[:, None, :].astype(t.dtype)
    s = sin[:, None, :].astype(t.dtype)
    return jnp.concatenate([t1 * c - t2 * s, t1 * s + t2 * c], axis=-1)

def dense_bidirectional_attention(q, k, v):
    B, L, H, Dk = q.shape
    nb = L // Q_BLOCK
    scale = 1.0 / math.sqrt(Dk)
    kt = k.transpose(0, 2, 1, 3)
    vt = v.transpose(0, 2, 1, 3)
    qb = q.reshape(B, nb, Q_BLOCK, H, Dk).transpose(1, 0, 3, 2, 4)

    def one_block(qblk):
        s = jnp.einsum('bhqd,bhkd->bhqk', qblk, kt).astype(jnp.float32) * scale
        p = jax.nn.softmax(s, axis=-1).astype(vt.dtype)
        return jnp.einsum('bhqk,bhkd->bqhd', p, vt)

    o = lax.map(one_block, qb)
    return o.transpose(1, 0, 2, 3, 4).reshape(B, L, H * v.shape[-1])

def second_inputs(seed: int = 0) -> dict:
    key = jax.random.key(seed)
    ks = jax.random.split(key, 24)
    f32 = jnp.float32

    def nrm(k, shape, scale):
        return jax.random.normal(k, shape, f32) * scale

    n = DEPTH
    return {
        'x': nrm(ks[0], (BATCH, SEQ, D_MODEL), 1.0),
        'g_norm': 1.0 + nrm(ks[1], (n, D_MODEL), 0.02),
        'w_in': nrm(ks[2], (n, D_MODEL, IN_COLS), D_MODEL ** -0.5),
        'b_gate': nrm(ks[3], (n, 2 * D_MODEL), 0.02),
        'w_short': nrm(ks[4], (n, SHORT_CONV, 3 * HY_WIDTH), SHORT_CONV ** -0.5),
        'b_short': nrm(ks[5], (n, 3 * HY_WIDTH), 0.02),
        'w_f1': nrm(ks[6], (n, FILTER_EMB, FILTER_HIDDEN), FILTER_EMB ** -0.5),
        'b_f1': nrm(ks[7], (n, FILTER_HIDDEN), 0.02),
        'freq_1': 1.0 + nrm(ks[8], (n, FILTER_HIDDEN), 0.02),
        'w_f2': nrm(ks[9], (n, FILTER_HIDDEN, FILTER_HIDDEN), FILTER_HIDDEN ** -0.5),
        'b_f2': nrm(ks[10], (n, FILTER_HIDDEN), 0.02),
        'freq_2': 1.0 + nrm(ks[11], (n, FILTER_HIDDEN), 0.02),
        'w_f3': nrm(ks[12], (n, FILTER_HIDDEN, HY_ORDER * 2 * HY_WIDTH), 2.0 * (FILTER_HIDDEN * SEQ) ** -0.5),
        'hy_bias': nrm(ks[13], (n, HY_ORDER, HY_WIDTH), 0.1),
        'w_hy_out': nrm(ks[14], (n, HY_WIDTH, D_MODEL), HY_WIDTH ** -0.5),
        'g_cq': 1.0 + nrm(ks[15], (n, Q_LORA), 0.02),
        'w_uq': nrm(ks[16], (n, Q_LORA, MLA_HEADS * QK_DIM), Q_LORA ** -0.5),
        'g_ckv': 1.0 + nrm(ks[17], (n, KV_LORA), 0.02),
        'w_ukv': nrm(ks[18], (n, KV_LORA, MLA_HEADS * (QK_NOPE + V_DIM)), KV_LORA ** -0.5),
        'g_qn': 1.0 + nrm(ks[19], (n, QK_DIM), 0.02),
        'g_kn': 1.0 + nrm(ks[20], (n, QK_DIM), 0.02),
        'w_attn_out': nrm(ks[21], (n, ATTN_WIDTH, D_MODEL), ATTN_WIDTH ** -0.5),
        'w_out': nrm(ks[22], (n, D_MODEL, D_MODEL), D_MODEL ** -0.5),
    }

def second_block(x, g_norm, w_in, b_gate, w_short, b_short, w_f1, b_f1, freq_1, w_f2, b_f2, freq_2,
              w_f3, hy_bias, w_hy_out, g_cq, w_uq, g_ckv, w_ukv, g_qn, g_kn, w_attn_out, w_out):
    B, L, _ = x.shape
    pos = jnp.arange(L, dtype=jnp.float32)
    inv_freq = ROPE_THETA ** (-jnp.arange(0, QK_ROPE, 2, dtype=jnp.float32) / QK_ROPE)
    ang = pos[:, None] * inv_freq[None, :]
    cos, sin = jnp.cos(ang), jnp.sin(ang)

    split_at = list(np.cumsum([3 * HY_WIDTH, HY_WIDTH, Q_LORA, KV_LORA, QK_ROPE, ATTN_WIDTH, D_MODEL]))

    for l in range(DEPTH):
        h = rms_norm(x, g_norm[l])
        proj = h @ w_in[l]
        hy_in, z_hy, c_q, c_kv, k_rope, z_attn, gate_hy, gate_attn = jnp.split(proj, split_at, axis=-1)

        u = short_conv(hy_in, w_short[l], b_short[l])
        v_h, x1, x2 = jnp.split(u, 3, axis=-1)
        k_spec = hyena_filter_spectra(L, w_f1[l], b_f1[l], freq_1[l], w_f2[l], b_f2[l], freq_2[l], w_f3[l])
        zc = v_h
        for o, gate in enumerate((x1, x2)):
            zc = gate * long_conv(zc, k_spec[:, o], hy_bias[l, o])
        u_hy = (zc * jax.nn.silu(z_hy)) @ w_hy_out[l]

        q = (rms_norm(c_q, g_cq[l]) @ w_uq[l]).reshape(B, L, MLA_HEADS, QK_DIM)
        kv = (rms_norm(c_kv, g_ckv[l]) @ w_ukv[l]).reshape(B, L, MLA_HEADS, QK_NOPE + V_DIM)
        k_nope, v_a = kv[..., :QK_NOPE], kv[..., QK_NOPE:]
        k_r = jnp.broadcast_to(k_rope[:, :, None, :], (B, L, MLA_HEADS, QK_ROPE))
        k = jnp.concatenate([k_nope, k_r], axis=-1)
        q = rms_norm(q, g_qn[l])
        k = rms_norm(k, g_kn[l])
        q = jnp.concatenate([q[..., :QK_NOPE], rotary(q[..., QK_NOPE:], cos, sin)], axis=-1)
        k = jnp.concatenate([k[..., :QK_NOPE], rotary(k[..., QK_NOPE:], cos, sin)], axis=-1)
        attn = dense_bidirectional_attention(q, k, v_a)
        u_attn = (attn * jax.nn.silu(z_attn)) @ w_attn_out[l]

        gates = jax.nn.sigmoid(jnp.concatenate([gate_hy, gate_attn], axis=-1) + b_gate[l])
        g_hy, g_at = jnp.split(gates, 2, axis=-1)
        merged = g_hy * u_hy + g_at * u_attn
        x = x + merged @ w_out[l]
    return x


def setup_inputs(seed=0):
    out = dict(first_inputs(seed))
    for name, value in second_inputs(seed + 1).items():
        if name != "x":
            out[name + "_2"] = value
    return out


def reference(
    x, mem, ffn1_pre_g, ffn1_post_g, ffn1_w_gu, ffn1_w_down, mix_pre_g, mix_post_g, w_in,
    b_gate, da_lambda_q1, da_lambda_k1, da_lambda_q2, da_lambda_k2, da_subln_g, ssd_conv_w,
    ssd_conv_b, ssd_dt_bias, ssd_A_log, ssd_D, ssd_norm_g, w_branch_attn, w_branch_ssd,
    w_mix_out, xa_pre_g, xa_post_g, mem_norm_g, xa_w_q, xa_w_kv, xa_w_o, ffn2_pre_g,
    ffn2_post_g, ffn2_w_gu, ffn2_w_down, g_norm_2, w_in_2, b_gate_2, w_short_2, b_short_2,
    w_f1_2, b_f1_2, freq_1_2, w_f2_2, b_f2_2, freq_2_2, w_f3_2, hy_bias_2, w_hy_out_2, g_cq_2,
    w_uq_2, g_ckv_2, w_ukv_2, g_qn_2, g_kn_2, w_attn_out_2, w_out_2,
):
    x = first_block(
        x, mem, ffn1_pre_g, ffn1_post_g, ffn1_w_gu, ffn1_w_down, mix_pre_g, mix_post_g, w_in,
        b_gate, da_lambda_q1, da_lambda_k1, da_lambda_q2, da_lambda_k2, da_subln_g, ssd_conv_w,
        ssd_conv_b, ssd_dt_bias, ssd_A_log, ssd_D, ssd_norm_g, w_branch_attn, w_branch_ssd,
        w_mix_out, xa_pre_g, xa_post_g, mem_norm_g, xa_w_q, xa_w_kv, xa_w_o, ffn2_pre_g,
        ffn2_post_g, ffn2_w_gu, ffn2_w_down,
    )
    return second_block(
        x, g_norm_2, w_in_2, b_gate_2, w_short_2, b_short_2, w_f1_2, b_f1_2, freq_1_2, w_f2_2,
        b_f2_2, freq_2_2, w_f3_2, hy_bias_2, w_hy_out_2, g_cq_2, w_uq_2, g_ckv_2, w_ukv_2,
        g_qn_2, g_kn_2, w_attn_out_2, w_out_2,
    )


_drawn_inputs = setup_inputs


def setup_inputs(seed=0):
    import zlib

    import numpy as np

    out = dict(_drawn_inputs(seed))
    spreads = {}
    factors = {'ffn1_pre_g': 3.074,
     'ffn1_post_g': 4.753,
     'mix_post_g': 4.131,
     'b_gate': 8.0,
     'da_lambda_q1': 8.0,
     'da_subln_g': 6.563,
     'ssd_conv_b': 4.035,
     'ssd_norm_g': 5.479,
     'xa_pre_g': 4.973,
     'xa_post_g': 4.904,
     'mem_norm_g': 3.29,
     'ffn2_pre_g': 7.162,
     'ffn2_post_g': 8.0,
     'g_norm_2': 8.0,
     'b_gate_2': 21.402,
     'b_short_2': 8.0,
     'b_f1_2': 8.0,
     'freq_1_2': 8.0,
     'b_f2_2': 8.0,
     'freq_2_2': 8.0,
     'hy_bias_2': 5.097,
     'g_cq_2': 64.0,
     'w_uq_2': 3.772,
     'g_ckv_2': 64.0,
     'g_qn_2': 64.0,
     'g_kn_2': 64.0}
    for name, (base, spread) in spreads.items():
        noise = np.random.default_rng([zlib.crc32(name.encode()), seed]).standard_normal(out[name].shape)
        drawn = base * np.exp(spread * noise) if base else spread * noise
        out[name] = __import__('jax').numpy.asarray(drawn.astype(out[name].dtype))
    for name, factor in factors.items():
        out[name] = (out[name] * factor).astype(out[name].dtype)
    return out
```

```python
import math
from contextlib import ExitStack

import numpy as np

import concourse.bass as bass
from concourse import mybir

F32 = mybir.dt.float32
F32R = mybir.dt.float32r
I32 = mybir.dt.int32
ALU = mybir.AluOpType
ACT = mybir.ActivationFunctionType
AX = mybir.AxisListType

P = 128
SEQ = 256
TOK = SEQ // P
D = 1024
KD = D // P
D_FF = 2816
FF_TILES = D_FF // P
EPS = 1e-6
SUB_EPS = 1e-5

DA_HEADS = 8
DA_DIM = 64
SSD_INNER = 2048
SSD_HEADS = 32
SSD_GROUPS = 4
SSD_CONV = 4
XBC = 3072
XA_HEADS = 4
XA_DIM = 256
LAM_INIT = 0.8 - 0.6 * math.exp(-0.3 * 0)

HY = 512
HY_TILES = HY // P
FILTER_EMB = 33
FILTER_HIDDEN = 64
MLA_HEADS = 8
QK_NOPE, QK_ROPE, V_DIM = 64, 32, 64
QK_DIM = QK_NOPE + QK_ROPE
Q_LORA, KV_LORA = 384, 256

ROUND = 1.5 * 2 ** 23
TURN_HI = 6.28125
TURN_MID = float(np.float32(round((2 * math.pi - TURN_HI) * 2 ** 20) / 2 ** 20))
TURN_LO = 2 * math.pi - TURN_HI - TURN_MID
PI_BELOW = 3.1415925

BLOCK = 2048
RING = 3
STAGES = 3

W_IN_AT = {"q": 0, "k": 1024, "v": 2048, "z": 3072, "xbc": 5120, "dt": 8192, "gate": 8224}
W_IN2_AT = {"hy": 0, "z_hy": 1536, "cq": 2048, "ckv": 2432, "rope": 2688, "z_at": 2720, "gate": 3232}


def weight_blocks():
    out = []

    def add(stage, w, cols, kt=KD, row=0):
        out.append((stage, w, row, kt, cols))

    def ffn(n):
        for j in range(FF_TILES):
            add(f"ffn{n}_up", f"ffn{n}_w_gu", [(j * P, P), (D_FF + j * P, P)])
        for c in range(FF_TILES // 2):
            add(f"ffn{n}_down", f"ffn{n}_w_down", [(0, D)], 2, 2 * c * P)

    def plain(stage, w, at, n, width=256, kt=KD):
        for i in range(n):
            add(stage, w, [(at + i * width, width)], kt)

    ffn(1)
    plain("xa_kv", "xa_w_kv", 0, 8)
    add("dt", "w_in", [(W_IN_AT["dt"], SSD_HEADS)])
    plain("xbc", "w_in", W_IN_AT["xbc"], 12)
    plain("qkv", "w_in", W_IN_AT["q"], 12)
    plain("z", "w_in", W_IN_AT["z"], 8)
    plain("gate", "w_in", W_IN_AT["gate"], 8)
    plain("ssd_out", "w_branch_ssd", 0, 8, 128, 16)
    plain("attn_out", "w_branch_attn", 0, 4)
    plain("mix_out", "w_mix_out", 0, 4)
    plain("xa_q", "xa_w_q", 0, 4)
    plain("xa_o", "xa_w_o", 0, 4)
    ffn(2)
    add("cq", "w_in_2", [(W_IN2_AT["cq"], 256)])
    add("ckv", "w_in_2", [(W_IN2_AT["ckv"], 256)])
    add("cq_rope", "w_in_2", [(W_IN2_AT["cq"] + 256, P), (W_IN2_AT["rope"], QK_ROPE)])
    plain("z_hy", "w_in_2", W_IN2_AT["z_hy"], 2)
    plain("z_at", "w_in_2", W_IN2_AT["z_at"], 2)
    add("uq", "w_uq_2", [(0, 512)], 3)
    add("uq", "w_uq_2", [(512, 256)], 3)
    add("ukv", "w_ukv_2", [(0, 1024)], 2)
    plain("hy", "w_in_2", W_IN2_AT["hy"], 6)
    plain("gate2", "w_in_2", W_IN2_AT["gate"], 8)
    plain("hy_out", "w_hy_out_2", 0, 2, 512, 4)
    plain("at_out", "w_attn_out_2", 0, 2, 512, 4)
    plain("out", "w_out_2", 0, 4)
    return out


BLOCKS = weight_blocks()
NBLOCK = len(BLOCKS)
assert NBLOCK % RING == 0
FIRST = {}
for _n, _b in enumerate(BLOCKS):
    FIRST.setdefault(_b[0], _n)

COLS = {}
for _name, _len in [("ffn1_pre_g", 8), ("mix_pre_g", 8), ("xa_pre_g", 8), ("mem_norm_g", 8), ("ffn2_pre_g", 8),
                    ("g_norm_2", 8), ("b_gate", 16), ("da_subln_g", 1), ("ssd_conv_w", 96), ("ssd_conv_b", 24),
                    ("ssd_norm_g", 16), ("b_gate_2", 16), ("w_short_2", 36), ("b_short_2", 12), ("g_cq_2", 3),
                    ("g_ckv_2", 2)]:
    COLS[_name] = (sum(v[1] for v in COLS.values()), _len)
NCOLS = sum(v[1] for v in COLS.values())

ROWS = {}
for _name, _len in [("ssd_dt_bias", 32), ("ssd_A_log", 32), ("ssd_D", 32), ("da_lambda_q1", 64), ("da_lambda_k1", 64),
                    ("da_lambda_q2", 64), ("da_lambda_k2", 64), ("g_qn_2", QK_DIM), ("g_kn_2", QK_DIM)]:
    ROWS[_name] = (sum(v[1] for v in ROWS.values()), _len)
NROWS = sum(v[1] for v in ROWS.values())
X_READY = [2, 4, 6, 8]
POST_SSQ = [4, 8, 12, 16]
Y_TURNS = [4, 5, 6, 7, 0, 1, 2, 3]
POST = ["ffn1_post_g", "mix_post_g", "xa_post_g", "ffn2_post_g"]


def shape_constants():
    i = np.arange(P)
    upper = (i[:, None] <= i[None, :]).astype(np.float32)
    strict = (i[:, None] > i[None, :]).astype(np.float32)
    causal = np.where(strict.T > 0, np.float32(-1e30), np.float32(0))
    mask = np.concatenate([causal, np.zeros((P, P), np.float32), causal], axis=1)
    square = np.concatenate([np.eye(P, dtype=np.float32), upper, strict, mask], axis=1)

    w = 2 * np.pi * (np.arange(SEQ) + 0.5) / (2 * SEQ)
    s = np.arange(SEQ)

    def tiles(m):
        return np.ascontiguousarray(m.reshape(-1, P, m.shape[1]).transpose(1, 0, 2).astype(np.float32))

    ahead = np.concatenate([np.cos(s[:, None] * w), -np.sin(s[:, None] * w)], axis=1)
    behind = np.concatenate([np.cos((s[:, None] + 1) * w), np.sin((s[:, None] + 1) * w)], axis=1)
    back = np.concatenate([np.cos(w[:, None] * s), -np.sin(w[:, None] * s)], axis=0) / SEQ
    dft = np.concatenate([tiles(ahead).reshape(P, -1), tiles(behind).reshape(P, -1), tiles(back).reshape(P, -1)], axis=1)

    t = np.linspace(0.0, 1.0, SEQ, dtype=np.float32)[:, None]
    bands = (FILTER_EMB - 1) // 2
    f = np.linspace(1e-4, bands - 1, bands, dtype=np.float32)
    ang = np.float32(2.0 * np.pi / SEQ) * np.arange(SEQ, dtype=np.float32)[:, None] * f[None, :]
    emb = np.concatenate([t, np.cos(ang), -np.sin(ang)], axis=-1).astype(np.float32)
    deltas = np.abs(np.linspace(math.log(1e-2) / 1.5, math.log(1e-2) / 0.3, HY, dtype=np.float32))
    decay = tiles(np.exp(-t * deltas))

    inv = np.float32(10000.0) ** (-np.arange(0, QK_ROPE, 2, dtype=np.float32) / np.float32(QK_ROPE))
    rot = s.astype(np.float32)[:, None] * inv[None, :]
    rope = tiles(np.concatenate([np.cos(rot), np.sin(rot)], axis=1))
    return {"c_square": square, "c_dft": dft, "c_emb": np.ascontiguousarray(emb.T), "c_decay": decay, "c_rope": rope}


def program(nc, a, out):
    with ExitStack() as ctx:
        def sb(name, shape, dt=F32, scope=ctx):
            return scope.enter_context(nc.sbuf_tensor("sb_" + name, shape, dt))

        sems = {}

        def S(name):
            if name not in sems:
                sems[name] = ctx.enter_context(nc.semaphore("s_" + name))
            return sems[name]

        w_raw = [sb(f"w_raw{i}", [P, BLOCK]) for i in range(RING)]
        w_hi = [sb(f"w_hi{i}", [P, BLOCK], F32R) for i in range(STAGES)]
        w_lo = [sb(f"w_lo{i}", [P, BLOCK], F32R) for i in range(STAGES)]
        x = sb("x", [P, TOK, D])
        square = sb("square", [P, 6 * P])
        ident, upper, strict, causal = square[:, 0:P], square[:, P:2 * P], square[:, 2 * P:3 * P], square[:, 3 * P:]
        cols = sb("cols", [P, NCOLS])
        fcols = sb("fcols", [FILTER_HIDDEN, 4])
        rows = sb("rows", [P, NROWS])
        sub_g = sb("sub_g", [P, 1])
        nt = sb("newton", [P, 5, 16])
        ssq = sb("ssq", [P, 4])
        post_ssq = sb("post_ssq", [P, TOK, 4])
        post_sum = sb("post_sum", [P, TOK])
        ssd_ssq = sb("ssd_ssq", [P, TOK, SSD_GROUPS])
        c_ssq = sb("c_ssq", [P, 2, TOK])
        m_ssq = sb("m_ssq", [P, TOK * MLA_HEADS])
        rstd = sb("rstd", [P, 16])
        hT_hi = sb("hT_hi", [P, KD, SEQ], F32R)
        hT_lo = sb("hT_lo", [P, KD, SEQ], F32R)

        def col(name, i=0, n=1):
            at = COLS[name][0] + i
            return cols[:, at:at + n]

        def row(name):
            at, n = ROWS[name]
            return rows[:, at:at + n]

        places = [0]

        def place(at, name, shape, dt=F32):
            with ExitStack() as here:
                places[0] += 1
                if at:
                    sb(f"before{places[0]}", [P, int(at * 256)], F32, here)
                return sb(name, shape, dt, here)

        post_g = place(100, "post_g", [P, D])
        ffn = {}
        for n in (1, 2):
            ffn[n] = {
                "xn": place(16, f"ffn{n}_xn", [P, TOK, D]),
                "gate": place(16, f"ffn{n}_gate", [P, 2, SEQ]),
                "act": place(18, f"ffn{n}_act", [P, 2, SEQ]),
                "hi": place(24, f"ffn{n}_hi", [P, FF_TILES, SEQ], F32R),
                "lo": place(46, f"ffn{n}_lo", [P, FF_TILES, SEQ], F32R),
                "junk": place(24, f"ffn{n}_junk", [P, 512]),
            }

        mem_xn = place(72, "mem_xn", [P, TOK, D])
        mem_junk = place(68, "mem_junk", [P, 1, D])
        mem_hi = place(82, "mem_hi", [P, KD, SEQ], F32R)
        mem_lo = place(90, "mem_lo", [P, KD, SEQ], F32R)
        xa_k = place(0, "xa_k", [P, KD, SEQ])
        xa_v = place(8, "xa_v", [P, TOK, D])

        mix_xn = place(48, "mix_xn", [P, TOK, D])
        ssd_y = place(16, "ssd_y", [P, TOK, SSD_INNER])
        da_q = place(32, "da_q", [P, DA_HEADS, SEQ])
        da_o = place(32, "da_o", [P, DA_HEADS, TOK, P])
        da_k = place(40, "da_k", [P, DA_HEADS, SEQ])
        ssd_bF = place(48, "ssd_bF", [P, SSD_GROUPS, SEQ])
        ssd_cF = place(52, "ssd_cF", [P, SSD_GROUPS, SEQ])
        ssd_bT = place(56, "ssd_bT", [P, SSD_GROUPS, P])
        ssd_dtt = place(58, "ssd_dtt", [P, 6, TOK * SSD_HEADS])
        ssd_dt = place(59.5, "ssd_dt", [P, TOK, SSD_HEADS])
        ssd_A = place(59.75, "ssd_A", [P, TOK, SSD_HEADS])
        ssd_conv = place(60, "ssd_conv", [P, 2, 2, SEQ])
        ssd_xF = place(64, "ssd_xF", [P, 2, 2, SEQ])
        ssd_xdd = place(60, "ssd_xdd", [P, SSD_INNER])
        ssd_xdt = place(68, "ssd_xdt", [P, SSD_INNER])
        ssd_state = place(76, "ssd_state", [P, SSD_GROUPS, 512])
        ssd_cb = place(84, "ssd_cb", [P, P])
        ssd_uA = place(85, "ssd_uA", [P, 2, 512])
        ssd_L = place(89, "ssd_L", [P, 2, 512])
        ssd_M = place(93, "ssd_M", [P, 2, 512])
        ssd_t = place(97, "ssd_t", [P, 512])
        ssd_eA = place(99, "ssd_eA", [P, SSD_HEADS])
        ssd_decay = place(99.25, "ssd_decay", [P, SSD_HEADS])
        ssd_ecs = place(99.5, "ssd_ecs", [P, SSD_HEADS])
        da_v = place(60, "da_v", [P, TOK, D])
        mix_gate = place(68, "mix_gate", [P, 16, SEQ])
        ssd_z = place(84, "ssd_z", [P, TOK, SSD_INNER])
        da_s = place(48, "da_s", [P, 2, 384])
        da_p = place(51, "da_p", [P, 2, 384])
        da_P = place(54, "da_P", [P, 384])
        da_PT = place(55.5, "da_PT", [P, 384])
        da_st = place(57, "da_st", [P, 4, 4])
        da_lam = place(57.25, "da_lam", [P, 4])
        da_ssq = place(57.5, "da_ssq", [P, TOK, DA_HEADS])
        da_junk = place(58, "da_junk", [P, P])
        da_junk2 = place(58.5, "da_junk2", [P, 2, DA_DIM])
        y2_hi = place(84, "y2_hi", [P, KD, SEQ], F32R)
        y2_lo = place(92, "y2_lo", [P, KD, SEQ], F32R)
        o_hi = place(40, "o_hi", [P, KD, SEQ], F32R)
        o_lo = place(60, "o_lo", [P, KD, SEQ], F32R)
        mg = place(48, "mg", [P, KD, SEQ])
        mixed_hi = place(16, "mixed_hi", [P, KD, SEQ], F32R)
        mixed_lo = place(24, "mixed_lo", [P, KD, SEQ], F32R)

        xa_q = place(16, "xa_q", [P, KD, SEQ])
        xa_xn = place(24, "xa_xn", [P, TOK, D])
        xa_p = place(24, "xa_p", [P, 2, 2, SEQ])
        xa_PT = place(28, "xa_PT", [P, 2, SEQ])
        xa_st = place(30, "xa_st", [P, 4, 2])
        xa_hi = place(32, "xa_hi", [P, KD, SEQ], F32R)
        xa_lo = place(40, "xa_lo", [P, KD, SEQ], F32R)
        post_tmp = place(56, "post_tmp", [P, 512])
        mg_T = mg[:].rearrange("p k t -> p (k t)").rearrange("p (t d) -> p t d", t=TOK)

        decay = place(60, "decay", [P, TOK, HY])
        bias_row = place(64, "bias_row", [1, 2, HY])
        kfil = place(68, "kfil", [P, TOK, 4 * HY])
        w_f3 = place(84, "w_f3", [FILTER_HIDDEN, 4 * HY])
        hid = place(92, "hid", [FILTER_HIDDEN, 4, SEQ])
        fil_t = place(96, "fil_t", [FILTER_HIDDEN, 2, SEQ])
        emb = place(98, "emb", [FILTER_EMB, SEQ])
        w_f12 = place(99, "w_f12", [FILTER_HIDDEN, 2, FILTER_HIDDEN])
        dft_f = place(0, "dft_f", [P, 2, TOK, 512])
        spec = place(84, "spec", [P, 2, 4, HY])

        gate2 = place(0, "gate2", [P, 16, SEQ])
        z_hy = place(16, "z_hy", [P, HY_TILES, SEQ])
        z_at = place(20, "z_at", [P, HY_TILES, SEQ])
        sec_xn = place(24, "sec_xn", [P, TOK, D])
        mv = place(24, "mv", [P, TOK, MLA_HEADS, V_DIM])
        dft_b = place(28, "dft_b", [P, 4, SEQ])
        cq = place(32, "cq", [P, TOK, Q_LORA])
        ckv = place(35, "ckv", [P, TOK, KV_LORA])
        c_junk = place(37, "c_junk", [P, Q_LORA])
        cq_hi = place(39, "cq_hi", [P, 3, SEQ], F32R)
        cq_lo = place(42, "cq_lo", [P, 3, SEQ], F32R)
        ckv_hi = place(45, "ckv_hi", [P, 2, SEQ], F32R)
        ckv_lo = place(47, "ckv_lo", [P, 2, SEQ], F32R)
        hyF = place(32, "hyF", [P, 12, SEQ])
        uT = place(44, "uT", [P, TOK, HY])
        mq = place(49, "mq", [P, 2, TOK, MLA_HEADS, QK_DIM])
        at_hi = place(49, "at_hi", [P, HY_TILES, SEQ], F32R)
        at_lo = place(53, "at_lo", [P, HY_TILES, SEQ], F32R)
        m_p = place(57, "m_p", [P, 2, 2, SEQ])
        k_rope = place(61, "k_rope", [P, TOK, QK_ROPE])
        m_ropeT = place(61.25, "m_ropeT", [P, TOK, QK_ROPE])
        m_st = place(61.5, "m_st", [P, 4, 2])
        msq = place(62, "msq", [P, TOK, MLA_HEADS, QK_DIM])
        m_t = place(70, "m_t", [P, 4, TOK, MLA_HEADS, 16])
        mqT = place(62, "mqT", [QK_DIM, 2, MLA_HEADS, SEQ])
        dft_a = place(78, "dft_a", [P, TOK, 512])
        m_PT = place(82, "m_PT", [P, 2, SEQ])
        yt = place(100, "yt", [P, 2, HY])
        hy_hi = place(84, "hy_hi", [P, HY_TILES, SEQ], F32R)
        hy_lo = place(88, "hy_lo", [P, HY_TILES, SEQ], F32R)
        mg2 = place(92, "mg2", [P, KD, SEQ])
        mq_rows = mq[:].rearrange("p s t h d -> p s t (h d)")
        banks = [ctx.enter_context(nc.psum_tensor(f"bank{i}", [P, 512], F32)) for i in range(8)]
        block_done, w_hi_in, w_lo_in = S("block_done"), S("w_hi_in"), S("w_lo_in")
        w_landed = [S(f"w_landed{i}") for i in range(RING)]
        bank_full = [S(f"bank_full{i}") for i in range(8)]
        bank_read = [S(f"bank_read{i}") for i in range(8)]

        fills = {}
        used = [0] * 8
        filled = [0] * 8

        def full(eng, key):
            bank, _, n, b = fills[key]
            if b is None:
                eng.wait_ge(bank_full[bank], n)
            else:
                eng.wait_ge(block_done, b + 1)
            return banks[bank]

        def read(ins, key):
            ins.then_inc(bank_read[fills[key][0]], 1)

        def wait_read(eng, key):
            eng.wait_ge(bank_read[fills[key][0]], fills[key][1])

        block = ctx.enter_context(nc.Block())

        @block.tensor
        def _(pe):
            def claim(key, bank, b=None):
                if used[bank]:
                    pe.wait_ge(bank_read[bank], used[bank])
                used[bank] += 1
                if b is None:
                    filled[bank] += 1
                fills[key] = (bank, used[bank], filled[bank], b)
                return banks[bank]

            def ends(ins, key):
                ins.then_inc(bank_full[fills[key][0]], 1)

            def product(o, a_hi, a_lo, b_hi, b_lo, first, last):
                pe.matmul(o, a_hi, b_hi, start=first, stop=False)
                pe.matmul(o, a_hi, b_lo, start=False, stop=False)
                return pe.matmul(o, a_lo, b_hi, start=False, stop=last)

            def weights(b, kt, width):
                pe.wait_ge(w_lo_in, b + 1)
                return [w[b % STAGES][:, 0:kt * width].rearrange("p (k c) -> p k c", k=kt) for w in (w_hi, w_lo)]

            def feature_block(key, b, tiles, a_hi, a_lo, kt=KD, width=256, bank=None, at=0, last=True, ready=None):
                hi, lo = weights(b, kt, width)
                o = claim(key, b % 3 if bank is None else bank, b if last else None)
                for i in range(tiles):
                    c = slice(at + i * P, at + (i + 1) * P)
                    for k in range(kt):
                        if ready and i == 0:
                            ready(k)
                        mm = product(o[:, i * SEQ:(i + 1) * SEQ], hi[:, k, c], lo[:, k, c],
                                     a_hi[:, k, :], a_lo[:, k, :], k == 0, k == kt - 1)
                if last:
                    mm.then_inc(block_done, 1)
                else:
                    ends(mm, key)

            def token_block(key, b, width, a_hi, a_lo, kt=KD, stride=256, bank=None, ready=None):
                hi, lo = weights(b, kt, width)
                o = claim(key, b % 3 if bank is None else bank, b)
                for t in range(TOK):
                    c = slice(t * P, (t + 1) * P)
                    for k in range(kt):
                        if ready and t == 0:
                            ready(k)
                        mm = product(o[:, t * stride:t * stride + width], a_hi[:, k, c], a_lo[:, k, c],
                                     hi[:, k, :], lo[:, k, :], k == 0, k == kt - 1)
                mm.then_inc(block_done, 1)

            def turn(o, src):
                return pe.transpose(o, src, ident)

            def norm_turn(n, src, at=(3, 4, 5, 6)):
                pe.wait_ge(S("xn_ready"), 2 * n + 2)
                for kp in range(KD // 2):
                    o = claim(f"norm{n}.{kp}", at[kp])
                    for kk in range(2):
                        for t in range(TOK):
                            k = 2 * kp + kk
                            mm = turn(o[:, kk * SEQ + t * P:kk * SEQ + (t + 1) * P], src[:, t, k * P:(k + 1) * P])
                    ends(mm, f"norm{n}.{kp}")

            def norm_done(n):
                def ready(k):
                    if k % 2 == 0:
                        wait_read(pe, f"norm{n}.{k // 2}")
                return ready

            def ffn_part(n, norm, between=None):
                up, down = FIRST[f"ffn{n}_up"], FIRST[f"ffn{n}_down"]
                f = ffn[n]
                for j in range(FF_TILES):
                    feature_block(f"up{n}.{j}", up + j, 2, hT_hi, hT_lo, ready=None if j else norm_done(norm))
                for c in range(FF_TILES // 2):
                    hi, lo = weights(down + c, 2, D)
                    if c == 0:
                        o = [claim(f"down{n}.{i}", 3 + i, down + FF_TILES // 2 - 1) for i in range(4)]
                    pe.wait_ge(S("ffn_lo"), FF_TILES * (n - 1) + 2 * c + 2)
                    for kk in range(2):
                        k = 2 * c + kk
                        for i in range(4):
                            t, h = slice(i // 2 * P, (i // 2 + 1) * P), slice(i % 2 * 512, (i % 2 + 1) * 512)
                            mm = product(o[i][:], f["hi"][:, k, t], f["lo"][:, k, t], hi[:, kk, h], lo[:, kk, h],
                                         k == 0, k == FF_TILES - 1)
                    mm.then_inc(block_done, 1)
                    if n == 1 and c == 6:
                        norm_turn(1, mem_xn, (7, 0, 1, 2))

            pe.wait_ge(S("square_in"), 16)
            norm_turn(0, ffn[1]["xn"])
            ffn_part(1, 0)

            for i in range(8):
                if i < 4:
                    feature_block(f"kv{i}", FIRST["xa_kv"] + i, 2, mem_hi, mem_lo, ready=None if i else norm_done(1))
                else:
                    token_block(f"kv{i}", FIRST["xa_kv"] + i, 256, mem_hi, mem_lo)
                if i == 4:
                    norm_turn(2, mix_xn)

            token_block("dt", FIRST["dt"], SSD_HEADS, hT_hi, hT_lo, ready=norm_done(2))
            xbc, qkv, zb, gb = FIRST["xbc"], FIRST["qkv"], FIRST["z"], FIRST["gate"]

            def xbc_turn(i):
                pe.wait_ge(S("xbc_silu"), i + 1)
                o = claim(f"xT{i}", 3 + i % 2)
                for c in range(2):
                    if i < 8:
                        for t in range(TOK):
                            mm = turn(o[:, t * 256 + c * P:t * 256 + (c + 1) * P], ssd_xF[:, i % 2, c, t * P:(t + 1) * P])
                    else:
                        mm = turn(o[:, c * P:(c + 1) * P], ssd_bF[:, 2 * (i - 8) + c, 0:P])
                ends(mm, f"xT{i}")

            for i in range(12):
                feature_block(f"xbc{i}", xbc + i, 2, hT_hi, hT_lo)
                if 1 <= i <= 10:
                    xbc_turn(i - 1)

            def ssd_sums():
                pe.wait_ge(S("ssd_A"), 2)
                o = claim("sums", 3)
                pe.matmul(o[:, 0:SSD_HEADS], upper, ssd_A[:, 1, :], start=True, stop=True)
                ends(pe.matmul(o[:, SSD_HEADS:2 * SSD_HEADS], strict, ssd_A[:, 0, :], start=True, stop=True), "sums")

            def ssd_unit(u):
                c, g = divmod(u, SSD_GROUPS)
                o = claim(f"cb{u}", 3)
                ends(pe.matmul(o[:, 0:P], ssd_bF[:, g, c * P:(c + 1) * P], ssd_cF[:, g, c * P:(c + 1) * P],
                               start=True, stop=True), f"cb{u}")
                for q in range(2):
                    pe.wait_ge(S("ssd_uA"), 2 * u + q + 1)
                    o = claim(f"seg{u}.{q}", 4 + q)
                    ends(pe.matmul(o[:], strict, ssd_uA[:, q, :], start=True, stop=True), f"seg{u}.{q}")
                if c == 0:
                    pe.wait_ge(S("ssd_xdd"), 1)
                    o = claim(f"state{g}", 6)
                    ends(pe.matmul(o[:], ssd_bT[:, g, :], ssd_xdd[:, g * 512:(g + 1) * 512], start=True, stop=True),
                         f"state{g}")

            def ssd_diag(u):
                c, g = divmod(u, SSD_GROUPS)
                pe.wait_ge(S("ssd_xdt"), c + 1)
                pe.wait_ge(S("ssd_M"), 2 * u + 2)
                o = claim(f"diag{u}", 7)
                for r in range(8):
                    mm = pe.matmul(o[:, r * 64:(r + 1) * 64], ssd_M[:, r // 4, r % 4 * P:(r % 4 + 1) * P],
                                   ssd_xdt[:, (8 * g + r) * 64:(8 * g + r + 1) * 64], start=True, stop=True)
                ends(mm, f"diag{u}")
                if c:
                    wait_read(pe, f"state{g}")
                    o = claim(f"yoff{g}", 6)
                    ends(pe.matmul(o[:], ssd_cF[:, g, P:2 * P], ssd_state[:, g, :], start=True, stop=True), f"yoff{g}")

            for i in range(12):
                if i < 8:
                    feature_block(f"qkv{i}", qkv + i, 2, hT_hi, hT_lo)
                else:
                    token_block(f"qkv{i}", qkv + i, 256, hT_hi, hT_lo)
                if i == 0:
                    ssd_sums()
                    for j in range(10):
                        wait_read(pe, f"xT{j}")
                if 1 <= i <= 8:
                    ssd_unit(i - 1)
                if 2 <= i <= 9:
                    ssd_diag(i - 2)

            def da_scores(h):
                for j in range(2):
                    o = claim(f"das{h}.{j}", 3 + j)
                    r = slice(j * DA_DIM, (j + 1) * DA_DIM)
                    pe.matmul(o[:, 0:P], da_q[r, h, 0:P], da_k[r, h, 0:P], start=True, stop=True)
                    mm = pe.matmul(o[:, P:P + SEQ], da_q[r, h, P:SEQ], da_k[r, h, :], start=True, stop=True)
                    ends(mm, f"das{h}.{j}")

            def da_turn(h):
                pe.wait_ge(S("da_P"), 2 * h + 2)
                o = claim(f"daT{h}", 5)
                for j in range(3):
                    mm = turn(o[:, j * P:(j + 1) * P], da_P[:, j * P:(j + 1) * P])
                ends(mm, f"daT{h}")

            def da_out(h):
                wait_read(pe, f"daT{h}")
                o = claim(f"dao{h}", 6)
                e = slice(h * P, (h + 1) * P)
                pe.matmul(o[:, 0:P], da_PT[:, 0:P], da_v[:, 0, e], start=True, stop=True)
                pe.matmul(o[:, P:2 * P], da_PT[:, P:2 * P], da_v[:, 0, e], start=True, stop=False)
                ends(pe.matmul(o[:, P:2 * P], da_PT[:, 2 * P:3 * P], da_v[:, 1, e], start=False, stop=True), f"dao{h}")

            def y_turn(kp):
                o = claim(f"yT{kp}", 7 if kp >= 4 else 3 + kp)
                for i in range(2):
                    for t in range(TOK):
                        k = 2 * kp + i
                        mm = turn(o[:, i * SEQ + t * P:i * SEQ + (t + 1) * P], ssd_y[:, t, k * P:(k + 1) * P])
                ends(mm, f"yT{kp}")

            for i in range(12):
                wait_read(pe, f"qkv{i}")
            for i in range(16):
                if i < 8:
                    token_block(f"z{i}", zb + i, 256, hT_hi, hT_lo)
                else:
                    feature_block(f"gate{i - 8}", gb + i - 8, 2, hT_hi, hT_lo)
                if i % 2 == 0:
                    if i:
                        da_turn(i // 2 - 1)
                    da_scores(i // 2)
                elif i > 1:
                    da_out(i // 2 - 1)
                if i >= 13:
                    if i == 13:
                        pe.wait_ge(S("ssd_yn"), 8)
                    y_turn(i - 9)
            y_turn(7)
            da_turn(DA_HEADS - 1)

            for kp in range(4):
                y_turn(kp)
            da_out(DA_HEADS - 1)
            y_order = [*range(8, 16), *range(8)]

            def ssd_block(i):
                b = FIRST["ssd_out"] + i
                hi, lo = weights(b, 16, P)
                o = claim(f"ssd{i}", b % 3, b)
                for n, k in enumerate(y_order):
                    if i == 0 and k % 2 == 0:
                        wait_read(pe, f"yT{k // 2}")
                    c_hi, c_lo = (hT_hi, hT_lo) if k < 8 else (y2_hi, y2_lo)
                    mm = product(o[:, 0:SEQ], hi[:, k, :], lo[:, k, :], c_hi[:, k % 8, :], c_lo[:, k % 8, :], n == 0, n == 15)
                mm.then_inc(block_done, 1)

            for i in range(8):
                ssd_block(i)
                if i == 4:
                    pe.wait_ge(S("da_on"), 2)
                    for hp in range(4):
                        o = claim(f"oT{hp}", 3 + hp)
                        for j in range(2):
                            for t in range(TOK):
                                mm = turn(o[:, j * SEQ + t * P:j * SEQ + (t + 1) * P], da_o[:, 2 * hp + j, t, :])
                        ends(mm, f"oT{hp}")
            for hp in range(4):
                wait_read(pe, f"oT{hp}")
            for i in range(4):
                feature_block(f"attn{i}", FIRST["attn_out"] + i, 2, o_hi, o_lo)

            def filter_hidden(i):
                o = claim(f"hid{i}", 7)
                if i == 0:
                    pe.wait_ge(S("filter_in"), 5 * 16)
                    mm = pe.matmul(o[0:FILTER_HIDDEN, 0:SEQ], w_f12[0:FILTER_EMB, 0, :], emb[:, :], start=True, stop=True)
                else:
                    pe.wait_ge(S("hid_sin"), 1)
                    mm = pe.matmul(o[0:FILTER_HIDDEN, 0:SEQ], w_f12[:, 1, :], hid[:, 1, :], start=True, stop=True)
                ends(mm, f"hid{i}")

            def filter_taps(i):
                t, c = divmod(i, 4)
                if i == 0:
                    pe.wait_ge(S("hid_sin"), 2)
                o = claim(f"taps{i}", 3 + i % 4)
                ends(pe.matmul(o[:], hid[:, 3, t * P:(t + 1) * P], w_f3[:, c * HY:(c + 1) * HY], start=True, stop=True),
                     f"taps{i}")

            def filter_spectrum(i, bank):
                n, f = divmod(i, 4)
                if i == 0:
                    pe.wait_ge(S("kfil_bias"), 2)
                    pe.wait_ge(S("dft_f_in"), 16)
                o = claim(f"spec{i}", bank)
                for way in range(2):
                    for t in range(TOK):
                        mm = pe.matmul(o[:], dft_f[:, way, t, f * P:(f + 1) * P],
                                       kfil[:, t, (2 * n + way) * HY:(2 * n + way + 1) * HY],
                                       start=way == 0 and t == 0, stop=way == 1 and t == 1)
                ends(mm, f"spec{i}")

            def mixed_ready(k):
                if k % 2 == 0:
                    pe.wait_ge(S("mixed_lo"), k // 2 + 1)

            for i in range(4):
                token_block(f"mix{i}", FIRST["mix_out"] + i, 256, mixed_hi, mixed_lo, ready=None if i else mixed_ready)
                if i in (0, 2):
                    filter_hidden(i // 2)
            for i in range(8):
                filter_taps(i)

            norm_turn(3, xa_xn)
            for i in range(8):
                wait_read(pe, f"kv{i}")

            def xa_scores(h):
                wait_read(pe, f"xaq{h}")
                o = claim(f"xas{h}", 3 + h % 2)
                for q in range(2):
                    for kk in range(2):
                        k = 2 * h + kk
                        mm = pe.matmul(o[:, q * SEQ:(q + 1) * SEQ], xa_q[:, k, q * P:(q + 1) * P], xa_k[:, k, :],
                                       start=kk == 0, stop=kk == 1)
                ends(mm, f"xas{h}")

            def xa_turn(h):
                pe.wait_ge(S("xa_P"), 2 * h + 2)
                o = claim(f"xaT{h}", 5)
                for kb in range(2):
                    for q in range(2):
                        mm = turn(o[:, kb * SEQ + q * P:kb * SEQ + (q + 1) * P], xa_p[:, h % 2, q, kb * P:(kb + 1) * P])
                ends(mm, f"xaT{h}")

            def xa_out(h):
                wait_read(pe, f"xaT{h}")
                o = claim(f"xao{h}", 6)
                for f in range(2):
                    for kb in range(2):
                        mm = pe.matmul(o[:, f * SEQ:(f + 1) * SEQ], xa_v[:, kb, (2 * h + f) * P:(2 * h + f + 1) * P],
                                       xa_PT[:, kb, :], start=kb == 0, stop=kb == 1)
                ends(mm, f"xao{h}")

            for i in range(XA_HEADS + 3):
                if i < XA_HEADS:
                    feature_block(f"xaq{i}", FIRST["xa_q"] + i, 2, hT_hi, hT_lo, ready=None if i else norm_done(3))
                if 1 <= i <= XA_HEADS:
                    xa_scores(i - 1)
                if i >= 3:
                    xa_out(i - 3)
                if 2 <= i <= XA_HEADS + 1:
                    xa_turn(i - 2)
            for h in range(XA_HEADS):
                wait_read(pe, f"xao{h}")
            for i in range(4):
                token_block(f"xo{i}", FIRST["xa_o"] + i, 256, xa_hi, xa_lo)

            for i in range(4):
                filter_spectrum(i, (3, 4, 5, 7)[i])
            norm_turn(4, ffn[2]["xn"])
            ffn_part(2, 4)
            for i in range(4):
                filter_spectrum(4 + i, (0, 1, 2, 7)[i])

            norm_turn(5, sec_xn)
            token_block("cq0", FIRST["cq"], 256, hT_hi, hT_lo, ready=norm_done(5))
            token_block("ckv", FIRST["ckv"], 256, hT_hi, hT_lo)
            token_block("cq1", FIRST["cq_rope"], P + QK_ROPE, hT_hi, hT_lo)
            for i in range(4):
                feature_block(f"zz{i}", FIRST["z_hy"] + i, 2, hT_hi, hT_lo)
                if i == 2:
                    pe.wait_ge(S("c_ready"), 4)
                    for k in range(5):
                        if k % 2 == 0:
                            o = claim(f"cT{k // 2}", 3 + k // 2)
                        for t in range(TOK):
                            src = cq[:, t, k * P:(k + 1) * P] if k < 3 else ckv[:, t, (k - 3) * P:(k - 2) * P]
                            mm = turn(o[:, k % 2 * SEQ + t * P:k % 2 * SEQ + (t + 1) * P], src)
                        if k % 2 or k == 4:
                            ends(mm, f"cT{k // 2}")
            for k in range(3):
                wait_read(pe, f"cT{k}")

            def token_wide(key, b, kt, width, a_hi, a_lo, at):
                hi, lo = weights(b, kt, width)
                for t in range(TOK):
                    for h in range(0, width, 512):
                        n = min(512, width - h)
                        o = claim(f"{key}.{t}.{h}", at + t * (width // 512 or 1) + h // 512, b)
                        for k in range(kt):
                            mm = product(o[:, 0:n], a_hi[:, k, t * P:(t + 1) * P], a_lo[:, k, t * P:(t + 1) * P],
                                         hi[:, k, h:h + n], lo[:, k, h:h + n], k == 0, k == kt - 1)
                mm.then_inc(block_done, 1)

            uq, ukv = FIRST["uq"], FIRST["ukv"]
            token_wide("uq0", uq, 3, 512, cq_hi, cq_lo, 6)
            token_wide("uq1", uq + 1, 3, 256, cq_hi, cq_lo, 3)
            token_wide("ukv", ukv, 2, 1024, ckv_hi, ckv_lo, 4)

            def hyena_turn(n):
                if n == 0:
                    wait_read(pe, "hy0")
                    wait_read(pe, "hy1")
                for t in range(TOK):
                    o = claim(f"uT{n}.{t}", 6 + t)
                    for c in range(HY_TILES):
                        if n and c % 2 == 0:
                            wait_read(pe, f"yt0.{c // 2}")
                        mm = turn(o[:, c * P:(c + 1) * P], hyF[:, c, t * P:(t + 1) * P])
                    ends(mm, f"uT{n}.{t}")

            def hyena_ahead(n, f):
                if n == 0 and f == 0:
                    pe.wait_ge(S("dft_ab_in"), 32)
                for t in range(TOK):
                    wait_read(pe, f"uT{n}.{t}")
                for i in (f, f + 2):
                    o = claim(f"uf{n}.{i}", 6 + i // 2)
                    for t in range(TOK):
                        mm = pe.matmul(o[:], dft_a[:, t, i * P:(i + 1) * P], uT[:, t, :], start=t == 0, stop=t == 1)
                    ends(mm, f"uf{n}.{i}")

            def hyena_back(n):
                pe.wait_ge(S("hy_yf"), 4 * (n + 1))
                for cp in range(2):
                    o = claim(f"yt{n}.{cp}", 6 + cp)
                    for i in range(2):
                        c = 2 * cp + i
                        for f in range(4):
                            mm = pe.matmul(o[:, i * SEQ:(i + 1) * SEQ], spec[:, n, f, c * P:(c + 1) * P], dft_b[:, f, :],
                                           start=f == 0, stop=f == 3)
                    ends(mm, f"yt{n}.{cp}")

            def head_turn(s, hp):
                o = claim(f"mT{s}.{hp}", 3 + (4 * s + hp) % 3)
                for i in range(2):
                    for t in range(TOK):
                        mm = turn(o[0:QK_DIM, i * SEQ + t * P:i * SEQ + (t + 1) * P], mq[:, s, t, 2 * hp + i, :])
                ends(mm, f"mT{s}.{hp}")

            def mla_scores(h):
                if h == 0:
                    for s in range(2):
                        for hp in range(4):
                            wait_read(pe, f"mT{s}.{hp}")
                o = claim(f"ms{h}", 3)
                for q in range(2):
                    mm = pe.matmul(o[:, q * SEQ:(q + 1) * SEQ], mqT[:, 0, h, q * P:(q + 1) * P], mqT[:, 1, h, :],
                                   start=True, stop=True)
                ends(mm, f"ms{h}")

            def mla_turn(h):
                pe.wait_ge(S("m_P"), 2 * h + 2)
                o = claim(f"mPT{h}", 4)
                for kb in range(2):
                    for q in range(2):
                        mm = turn(o[:, kb * SEQ + q * P:kb * SEQ + (q + 1) * P], m_p[:, h % 2, q, kb * P:(kb + 1) * P])
                ends(mm, f"mPT{h}")

            def mla_out(h):
                wait_read(pe, f"mPT{h}")
                if h % 2 == 0:
                    claim(f"mo{h // 2}", 5)
                r = slice(h % 2 * V_DIM, (h % 2 + 1) * V_DIM)
                for kb in range(2):
                    mm = pe.matmul(banks[5][r, 0:SEQ], mv[:, kb, h, :], m_PT[:, kb, :], start=kb == 0, stop=kb == 1)
                if h % 2:
                    ends(mm, f"mo{h // 2}")

            def wide_out(key, b, hi, lo):
                feature_block(f"{key}.0", b, 2, hi, lo, HY_TILES, 512, last=False)
                feature_block(f"{key}.1", b, 2, hi, lo, HY_TILES, 512, bank=(b + 1) % 3, at=256)

            for i in range(6):
                feature_block(f"hy{i}", FIRST["hy"] + i, 2, hT_hi, hT_lo)
            hyena_turn(0)
            for s in range(2):
                pe.wait_ge(S("mla_qk"), s + 1)
                for hp in range(4):
                    head_turn(s, hp)
            for i in range(MLA_HEADS + 2):
                if i < 8:
                    feature_block(f"gg{i}", FIRST["gate2"] + i, 2, hT_hi, hT_lo)
                if i >= 2:
                    mla_out(i - 2)
                if i == 8:
                    pe.wait_ge(S("hy_lo"), 4)
                if i >= 8:
                    wide_out(f"hyo{i - 8}", FIRST["hy_out"] + i - 8, hy_hi, hy_lo)
                if 1 <= i <= MLA_HEADS:
                    mla_turn(i - 1)
                if i < MLA_HEADS:
                    mla_scores(i)
                if i in (0, 1):
                    hyena_ahead(0, i)
                elif i in (2, 6):
                    hyena_back(i // 4)
                elif i == 3:
                    hyena_turn(1)
                elif i in (4, 5):
                    hyena_ahead(1, i - 4)
            pe.wait_ge(S("at_lo"), 4)
            for i in range(2):
                wide_out(f"ato{i}", FIRST["at_out"] + i, at_hi, at_lo)

            def fin_ready(k):
                if k % 2 == 0:
                    pe.wait_ge(S("fin_lo"), k // 2 + 1)

            for i in range(4):
                token_block(f"out{i}", FIRST["out"] + i, 256, hT_hi, hT_lo, bank=3 + i, ready=None if i else fin_ready)

        @block.scalar
        def _(act):
            rounded = [0]
            step = [0]

            def link(ins):
                step[0] += 1
                ins.then_inc(S("scalar_step"), 1)
                act.wait_ge(S("scalar_step"), step[0])

            def round_to(n):
                for b in range(rounded[0], min(n, NBLOCK)):
                    act.wait_ge(w_landed[b % RING], 16 * (b // RING + 1))
                    if b >= STAGES:
                        act.wait_ge(block_done, b - STAGES + 1)
                    act.activation(w_hi[b % STAGES][:], w_raw[b % RING][:], ACT.Copy).then_inc(w_hi_in, 1)
                rounded[0] = max(rounded[0], min(n, NBLOCK))

            def after(b):
                round_to(b + 1 + STAGES)

            def copy(key, dst, src):
                read(act.activation(dst, src, ACT.Copy), key)

            def two(bank, n=2):
                return bank[:].rearrange("p (t c) -> p t c", t=n)

            def norm_squares(src, junk):
                act.activation(junk[:, 0, :], src[:, 0, :], ACT.Square, accum_out=ssq[:, 0:1]).then_inc(S("norm_ssq"), 1)

            def norm_high(n, gain, hi):
                for kp in range(KD // 2):
                    o = full(act, f"norm{n}.{kp}")
                    for kk in range(2):
                        k = 2 * kp + kk
                        ins = act.activation(hi[:, k, :], o[:, kk * SEQ:(kk + 1) * SEQ], ACT.Copy, scale=col(gain, k))
                    ins.then_inc(S("norm_hi"), 1)

            def post_gain(i, name):
                if i:
                    act.wait_ge(S("x_ready"), X_READY[i - 1] - 1)
                act.dma_start(post_g[:], a[name].partition_broadcast(P)[:, 0, :]).then_inc(S("post_g_in"), 16)

            def ffn_part(n):
                f, up, down = ffn[n], FIRST[f"ffn{n}_up"], FIRST[f"ffn{n}_down"]

                def high(j):
                    wait_read(act, f"up{n}.{j}")
                    act.activation(f["hi"][:, j, :], f["act"][:, j % 2, :], ACT.Copy).then_inc(S("ffn_hi"), 1)

                for j in range(FF_TILES):
                    o = full(act, f"up{n}.{j}")
                    if j >= 2:
                        wait_read(act, f"up{n}.{j - 2}")
                    act.activation(f["gate"][:, j % 2, :], o[:, 0:SEQ], ACT.Silu).then_inc(S("ffn_gate"), 1)
                    after(up + j)
                    if j:
                        high(j - 1)
                high(FF_TILES - 1)
                if n == 1:
                    act.wait_ge(S("mem_in"), 16)
                    norm_squares(mem_xn, mem_junk)
                for c in range(FF_TILES // 2):
                    after(down + c)
                    if n == 1 and c == 6:
                        norm_high(1, "mem_norm_g", mem_hi)
                for i in range(4):
                    o = full(act, f"down{n}.{i}")
                    if i >= 2:
                        wait_read(act, f"down{n}.{i}")
                    if i:
                        act.wait_ge(S("post_ssq"), (0 if n == 1 else POST_SSQ[2]) + i)
                    act.activation(f["junk"][:], o[:], ACT.Square, accum_out=post_ssq[:, i // 2, i % 2:i % 2 + 1])\
                       .then_inc(S("post_ssq"), 1)

            def out_part(stage, key, i_post, between=None):
                for i in range(4):
                    o = full(act, f"{key}{i}")
                    act.wait_ge(S("post_ssq"), POST_SSQ[i_post - 1] + i)
                    for t in range(TOK):
                        ins = act.activation(post_tmp[:, t * 256:(t + 1) * 256], o[:, t * 256:(t + 1) * 256], ACT.Square,
                                             accum_out=post_ssq[:, t, i:i + 1])
                    ins.then_inc(S("post_ssq"), 1)
                    after(FIRST[stage] + i)
                    if between:
                        between(i)

            act.dma_start(fcols[:], a["fcols"]).then_inc(S("rows_in"), 16)
            act.dma_start(rows[:], a["rows"].partition_broadcast(P)[:, 0, :]).then_inc(S("rows_in"), 16)
            post_gain(0, POST[0])

            act.wait_ge(S("x_in"), 16)
            norm_squares(x, ffn[1]["xn"])
            round_to(1)
            act.wait_ge(S("cols_in"), 16)
            norm_high(0, "ffn1_pre_g", hT_hi)
            round_to(STAGES)
            act.dma_start(mem_xn[:], a["mem"].rearrange("(t p) d -> p t d", p=P)).then_inc(S("mem_in"), 16)
            ffn_part(1)

            post_gain(1, POST[1])
            norm_squares(x, mix_xn)
            for i in range(8):
                o = full(act, f"kv{i}")
                if i < 4:
                    copy(f"kv{i}", xa_k[:, 2 * i:2 * i + 2, :], two(o))
                else:
                    copy(f"kv{i}", xa_v[:, :, (i - 4) * 256:(i - 3) * 256], two(o))
                after(FIRST["xa_kv"] + i)
                if i == 4:
                    norm_high(2, "mix_pre_g", hT_hi)

            after(FIRST["dt"])
            act.wait_ge(S("rows_in"), 32)
            act.activation(ssd_eA[:], row("ssd_A_log"), ACT.Exp).then_inc(S("dt_exp"), 1)

            def softplus():
                act.wait_ge(S("dt_abs"), 1)
                act.activation(ssd_dtt[:, 2], ssd_dtt[:, 1], ACT.Exp).then_inc(S("dt_exp"), 1)
                act.wait_ge(S("dt_one"), 1)
                act.activation(ssd_dtt[:, 4], ssd_dtt[:, 3], ACT.Ln).then_inc(S("dt_ln"), 1)

            softplus()
            for i in range(12):
                wait_read(act, f"xbc{i}")
                dst = ssd_xF[:, i % 2] if i < 8 else (ssd_bF if i < 10 else ssd_cF)[:, 2 * (i % 2):2 * (i % 2) + 2]
                act.activation(dst, ssd_conv[:, i % 2], ACT.Silu).then_inc(S("xbc_silu"), 1)
                after(FIRST["xbc"] + i)
                if 1 <= i <= 10:
                    o = full(act, f"xT{i - 1}")
                    if i <= 8:
                        copy(f"xT{i - 1}", ssd_y[:, :, (i - 1) * 256:i * 256], two(o))
                    else:
                        copy(f"xT{i - 1}", ssd_bT[:, 2 * (i - 9):2 * (i - 9) + 2, :], two(o)[:, 0, :].rearrange("p (c l) -> p c l", c=2))

            for i in range(12):
                o = full(act, f"qkv{i}")
                h = i % 4
                if i < 8:
                    copy(f"qkv{i}", (da_q if i < 4 else da_k)[:, 2 * h:2 * h + 2, :], two(o))
                else:
                    copy(f"qkv{i}", da_v[:, :, h * 256:(h + 1) * 256], two(o))
                after(FIRST["qkv"] + i)
                if i == 0:
                    o = full(act, "sums")
                    act.activation(ssd_ecs[:], o[:, 0:SSD_HEADS], ACT.Exp).then_inc(S("ssd_ecs"), 1)
                    read(act.activation(ssd_decay[:], o[:, SSD_HEADS:2 * SSD_HEADS], ACT.Exp), "sums")
                if 1 <= i <= 8:
                    u = i - 1
                    for q in range(2):
                        o = full(act, f"seg{u}.{q}")
                        if u:
                            act.wait_ge(S("ssd_M"), 2 * (u - 1) + q + 1)
                        read(act.activation(ssd_L[:, q, :], o[:], ACT.Exp), f"seg{u}.{q}")
                    if u < SSD_GROUPS:
                        o = full(act, f"state{u}")
                        copy(f"state{u}", ssd_state[:, u, :], o[:])

            act.wait_ge(S("lam_dot"), 2)
            act.activation(da_lam[:, 2:4], da_lam[:, 0:2], ACT.Exp).then_inc(S("lam_exp"), 1)

            def da_exps(h):
                act.wait_ge(S("da_max"), h + 1)
                if h:
                    act.wait_ge(S("da_P"), 2 * h)
                for j in range(2):
                    for q in range(2):
                        c = slice(0, P) if q == 0 else slice(P, P + SEQ)
                        ins = act.activation(da_p[:, j, c], da_s[:, j, c], ACT.Exp, bias=da_st[:, 1, 2 * j + q:2 * j + q + 1],
                                             scale=DA_DIM ** -0.5, accum_out=da_st[:, 2, 2 * j + q:2 * j + q + 1])
                        ins.then_inc(S("da_exp"), 1)

            def da_rows(h):
                o = full(act, f"dao{h}")
                for t in range(TOK):
                    if h or t:
                        act.wait_ge(S("da_ssq"), TOK * h + t)
                    act.activation(da_junk[:], o[:, t * P:(t + 1) * P], ACT.Square, accum_out=da_ssq[:, t, h:h + 1])\
                       .then_inc(S("da_ssq"), 1)
                copy(f"dao{h}", da_o[:, h, :, :], o[:, 0:SEQ].rearrange("p (t c) -> p t c", t=TOK))

            def da_columns(h):
                o = full(act, f"daT{h}")
                copy(f"daT{h}", da_PT[:], o[:, 0:384])

            def y_columns(k):
                return (hT_hi, hT_lo) if k < 8 else (y2_hi, y2_lo)

            def y_high(kp):
                o = full(act, f"yT{kp}")
                for i in range(2):
                    k = 2 * kp + i
                    ins = act.activation(y_columns(k)[0][:, k % 8, :], o[:, i * SEQ:(i + 1) * SEQ], ACT.Copy,
                                         scale=col("ssd_norm_g", k))
                ins.then_inc(S("y_hi"), 1)

            for i in range(16):
                after(FIRST["z"] + i)
                if i % 2 == 0:
                    if i:
                        da_columns(i // 2 - 1)
                    da_exps(i // 2)
                elif i > 1:
                    da_rows(i // 2 - 1)
                if i == 8:
                    for j in range(8):
                        wait_read(act, f"z{j}")
                    for t in range(TOK):
                        act.activation(ssd_z[:, t, :], ssd_z[:, t, :], ACT.Silu).then_inc(S("z_silu"), 1)
                if i in (10, 11):
                    t = i - 10
                    act.wait_ge(S("ssd_yg"), t + 1)
                    for g in range(SSD_GROUPS):
                        act.activation(ssd_z[:, t, g * 512:(g + 1) * 512], ssd_y[:, t, g * 512:(g + 1) * 512], ACT.Square,
                                       accum_out=ssd_ssq[:, t, g:g + 1]).then_inc(S("ssd_ssq"), 1)
                if i >= 13:
                    y_high(i - 9)
            y_high(7)
            da_columns(DA_HEADS - 1)

            for kp in range(4):
                y_high(kp)
            da_rows(DA_HEADS - 1)
            for i in range(8):
                wait_read(act, f"gate{i}")
            for c in (1, 0):
                act.activation(mix_gate[:, 8 * c:8 * c + 8, :], mix_gate[:, 8 * c:8 * c + 8, :], ACT.Sigmoid)\
                   .then_inc(S("mix_gate"), 1)
            act.wait_ge(S("sub_g"), 1)
            for i in range(8):
                after(FIRST["ssd_out"] + i)
                if i == 4:
                    for hp in range(4):
                        o = full(act, f"oT{hp}")
                        act.activation(o_hi[:, 2 * hp:2 * hp + 2, :], two(o), ACT.Copy, scale=sub_g[:, 0:1]).then_inc(S("o_hi"), 1)
            for i in range(4):
                after(FIRST["attn_out"] + i)
                act.wait_ge(S("mixed"), i + 1)
                act.activation(mixed_hi[:, 2 * i:2 * i + 2, :], mg[:, 2 * i:2 * i + 2, :], ACT.Copy).then_inc(S("mixed_hi"), 1)

            act.dma_start(w_f12[0:FILTER_EMB, 0, :], a["w_f1_2"]).then_inc(S("filter_in"), 16)
            act.dma_start(w_f12[:, 1, :], a["w_f2_2"]).then_inc(S("filter_in"), 16)
            act.dma_start(emb[:], a["c_emb"]).then_inc(S("filter_in"), 16)
            act.dma_start(w_f3[:], a["w_f3_2"]).then_inc(S("filter_in"), 16)
            act.dma_start(decay[:], a["c_decay"]).then_inc(S("filter_in"), 16)
            act.dma_start(bias_row[:], a["hy_bias"].unsqueeze(0)).then_inc(S("bias_in"), 16)

            def hidden_sin(i):
                act.wait_ge(S("hid_arg"), i + 1)
                act.activation(hid[:, 2 * i + 1, :], hid[:, 2 * i, :], ACT.Sin).then_inc(S("hid_sin"), 1)

            def mix_between(i):
                if i in (1, 2):
                    hidden_sin(i - 1)

            out_part("mix_out", "mix", 1, mix_between)

            def taps(i):
                t, c = divmod(i, 4)
                o = full(act, f"taps{i}")
                copy(f"taps{i}", kfil[:, t, c * HY:(c + 1) * HY], o[:])

            def spectrum(i):
                n, f = divmod(i, 4)
                o = full(act, f"spec{i}")
                copy(f"spec{i}", spec[:, n, f, :], o[:])

            for i in range(5):
                taps(i)
            post_gain(2, POST[2])
            norm_squares(x, xa_xn)
            for i in range(5, 8):
                taps(i)
            norm_high(3, "xa_pre_g", hT_hi)

            def xa_exps(h):
                act.wait_ge(S("xa_max"), h + 1)
                o = banks[fills[f"xas{h}"][0]]
                if h >= 2:
                    full(act, f"xaT{h - 2}")
                for q in range(2):
                    ins = act.activation(xa_p[:, h % 2, q, :], o[:, q * SEQ:(q + 1) * SEQ], ACT.Exp, bias=xa_st[:, 1, q:q + 1],
                                         scale=XA_DIM ** -0.5, accum_out=xa_st[:, 2, q:q + 1])
                read(ins, f"xas{h}")

            for i in range(XA_HEADS + 3):
                if i < XA_HEADS:
                    o = full(act, f"xaq{i}")
                    copy(f"xaq{i}", xa_q[:, 2 * i:2 * i + 2, :], two(o))
                    after(FIRST["xa_q"] + i)
                if 1 <= i <= XA_HEADS:
                    xa_exps(i - 1)
                if i >= 3:
                    h = i - 3
                    o = full(act, f"xao{h}")
                    act.activation(xa_hi[:, 2 * h:2 * h + 2, :], two(o), ACT.Copy).then_inc(S("xo_hi"), 1)
                if 2 <= i <= XA_HEADS + 1:
                    o = full(act, f"xaT{i - 2}")
                    copy(f"xaT{i - 2}", xa_PT[:], two(o))
            act.dma_start(dft_f[:].rearrange("p w t f -> p (w t f)"), a["c_dft"][:, 0:2048]).then_inc(S("dft_f_in"), 16)
            out_part("xa_o", "xo", 2)

            for i in range(4):
                spectrum(i)
            post_gain(3, POST[3])
            norm_squares(x, ffn[2]["xn"])
            norm_high(4, "ffn2_pre_g", hT_hi)
            ffn_part(2)

            for i in range(4, 8):
                spectrum(i)
            act.dma_start(dft_a[:].rearrange("p t f -> p (t f)"), a["c_dft"][:, 0:1024]).then_inc(S("dft_ab_in"), 16)
            act.dma_start(m_ropeT[:], a["c_rope"]).then_inc(S("rope_in"), 16)
            act.wait_ge(S("x_ready"), X_READY[3] - 1)
            norm_squares(x, sec_xn)
            norm_high(5, "g_norm_2", hT_hi)
            act.dma_start(dft_b[:].rearrange("p f t -> p (f t)"), a["c_dft"][:, 2048:3072]).then_inc(S("dft_ab_in"), 16)

            o = full(act, "cq0")
            copy("cq0", cq[:, :, 0:256], two(o))
            after(FIRST["cq"])
            o = full(act, "ckv")
            copy("ckv", ckv[:], two(o))
            after(FIRST["ckv"])
            o = full(act, "cq1")
            act.activation(cq[:, :, 256:384], two(o)[:, :, 0:P], ACT.Copy).then_inc(S("cq1_in"), 1)
            copy("cq1", k_rope[:], two(o)[:, :, P:P + QK_ROPE])
            for t in range(TOK):
                if t == 0:
                    wait_read(act, "cq0")
                    wait_read(act, "ckv")
                    act.wait_ge(S("cq1_in"), 1)
                else:
                    act.wait_ge(S("c_ssq"), 2)
                act.activation(c_junk[:, 0:Q_LORA], cq[:, t, :], ACT.Square, accum_out=c_ssq[:, 0, t:t + 1]).then_inc(S("c_ssq"), 1)
                act.wait_ge(S("c_ssq"), 2 * t + 1)
                act.activation(c_junk[:, 0:KV_LORA], ckv[:, t, :], ACT.Square, accum_out=c_ssq[:, 1, t:t + 1]).then_inc(S("c_ssq"), 1)
            after(FIRST["cq_rope"])
            for i in range(4):
                o = full(act, f"zz{i}")
                read(act.activation((z_hy if i < 2 else z_at)[:, 2 * (i % 2):2 * (i % 2) + 2, :], two(o), ACT.Silu), f"zz{i}")
                after(FIRST["z_hy"] + i)
                if i == 2:
                    for k in range(5):
                        o = full(act, f"cT{k // 2}")
                        dst = cq_hi[:, k, :] if k < 3 else ckv_hi[:, k - 3, :]
                        g = col("g_cq_2", k) if k < 3 else col("g_ckv_2", k - 3)
                        act.activation(dst, o[:, k % 2 * SEQ:(k % 2 + 1) * SEQ], ACT.Copy, scale=g).then_inc(S("c_hi"), 1)
            for t in range(TOK):
                o = full(act, f"uq0.{t}.0")
                copy(f"uq0.{t}.0", mq_rows[:, 0, t, 0:512], o[:])
            after(FIRST["uq"])
            for t in range(TOK):
                o = full(act, f"uq1.{t}.0")
                copy(f"uq1.{t}.0", mq_rows[:, 0, t, 512:768], o[:, 0:256])
            after(FIRST["uq"] + 1)
            for t in range(TOK):
                for h in range(0, 1024, 512):
                    o = full(act, f"ukv.{t}.{h}")[:].rearrange("p (h c) -> p h c", h=4)
                    heads = slice(h // P, h // P + 4)
                    act.activation(mq[:, 1, t, heads, 0:QK_NOPE], o[:, :, 0:QK_NOPE], ACT.Copy)
                    copy(f"ukv.{t}.{h}", mv[:, t, heads, :], o[:, :, QK_NOPE:])
            after(FIRST["ukv"])

            def centre_tap(i):
                o = full(act, f"hy{i}")
                for c in range(2):
                    ch = 2 * i + c
                    act.activation(hyF[:, ch, :], o[:, c * SEQ:(c + 1) * SEQ], ACT.Identity, scale=col("w_short_2", 3 * ch + 1),
                                   bias=col("b_short_2", ch)).then_inc(S("hy_mid"), 1)

            def hyena_rows(n):
                for t in range(TOK):
                    o = full(act, f"uT{n}.{t}")
                    copy(f"uT{n}.{t}", uT[:, t, :], o[:])

            for i in range(6):
                centre_tap(i)
                after(FIRST["hy"] + i)
            hyena_rows(0)
            for s in range(2):
                for hp in range(4):
                    o = full(act, f"mT{s}.{hp}")
                    copy(f"mT{s}.{hp}", mqT[:, s, 2 * hp:2 * hp + 2, :], o[0:QK_DIM, :].rearrange("p (h c) -> p h c", h=2))

            def mla_exps(h):
                act.wait_ge(S("m_max"), h + 1)
                o = banks[fills[f"ms{h}"][0]]
                if h >= 2:
                    full(act, f"mPT{h - 2}")
                for q in range(2):
                    ins = act.activation(m_p[:, h % 2, q, :], o[:, q * SEQ:(q + 1) * SEQ], ACT.Exp, bias=m_st[:, 1, q:q + 1],
                                         scale=QK_DIM ** -0.5, accum_out=m_st[:, 2, q:q + 1])
                read(ins, f"ms{h}")

            for i in range(MLA_HEADS + 2):
                if i < 8:
                    o = full(act, f"gg{i}")
                    for c in range(2):
                        ins = act.activation(gate2[:, 2 * i + c, :], o[:, c * SEQ:(c + 1) * SEQ], ACT.Identity,
                                             bias=col("b_gate_2", 2 * i + c))
                    read(ins, f"gg{i}")
                    after(FIRST["gate2"] + i)
                if 1 <= i <= MLA_HEADS:
                    o = full(act, f"mPT{i - 1}")
                    copy(f"mPT{i - 1}", m_PT[:], two(o))
                if i < MLA_HEADS:
                    mla_exps(i)
                if i >= 3 and i % 2:
                    c = (i - 3) // 2
                    wait_read(act, f"mo{c}")
                    act.activation(at_hi[:, c, :], z_at[:, c, :], ACT.Copy).then_inc(S("at_hi"), 1)
                if i == 3:
                    hyena_rows(1)
                if i == 7:
                    for c in range(HY_TILES):
                        wait_read(act, f"yt1.{c // 2}")
                        act.activation(hy_hi[:, c, :], hyF[:, c, :], ACT.Copy).then_inc(S("hy_hi"), 1)
                if i == 8:
                    for j in range(8):
                        wait_read(act, f"gg{j}")
                    for c in range(2):
                        act.activation(gate2[:, 8 * c:8 * c + 8, :], gate2[:, 8 * c:8 * c + 8, :], ACT.Sigmoid)\
                           .then_inc(S("gate2"), 1)
                if i >= 8:
                    after(FIRST["hy_out"] + i - 8)
            for i in range(4):
                act.wait_ge(S("fin"), i + 1)
                act.activation(hT_hi[:, 2 * i:2 * i + 2, :], mg2[:, 2 * i:2 * i + 2, :], ACT.Copy).then_inc(S("fin_hi"), 1)
                if i % 2:
                    after(FIRST["at_out"] + i // 2)
            for i in range(4):
                after(FIRST["out"] + i)

        @block.vector
        def _(dve):
            step = [0]

            def link(ins):
                step[0] += 1
                ins.then_inc(S("vector_step"), 1)
                dve.wait_ge(S("vector_step"), step[0])

            ts, tt, stt = dve.tensor_scalar, dve.tensor_tensor, dve.scalar_tensor_tensor

            def f32(t):
                return t.bitcast(F32)

            def two(bank, n=2):
                return bank[:].rearrange("p (t c) -> p t c", t=n)

            def inverse_root(dst, sums, n, width, eps):
                v, half, bits, t = (nt[:, i, 0:n] for i in range(4))
                link(ts(v, sums, 1.0 / width, eps, ALU.mult, ALU.add))
                link(ts(bits.bitcast(I32), v.bitcast(I32), 1, None, ALU.logical_shift_right))
                link(ts(dst.bitcast(I32), bits.bitcast(I32), -1.0, float(0x5F3759DF), ALU.mult, ALU.add))
                link(ts(half, v, -0.5, None, ALU.mult))
                for _ in range(3):
                    link(tt(t, dst, dst, ALU.mult))
                    link(tt(t, t, half, ALU.mult))
                    link(stt(dst, t, 1.5, dst, ALU.add, ALU.mult))

            def square_sum(junk, src, acc):
                return dve.tensor_tensor_reduce(junk, src, src, 1.0, 0.0, ALU.mult, ALU.add, acc)

            def norm_rows(n, src, dst, junk):
                link(square_sum(junk[:, 1, :], src[:, 1, :], ssq[:, 1:2]))
                dve.wait_ge(S("norm_ssq"), n + 1)
                inverse_root(rstd[:, 0:2], ssq[:, 0:2], 2, D, EPS)
                for t in range(TOK):
                    ts(dst[:, t, :], src[:, t, :], rstd[:, t:t + 1], None, ALU.mult).then_inc(S("xn_ready"), 1)

            def norm_low(n, gain, hi, lo):
                for kp in range(KD // 2):
                    dve.wait_ge(S("norm_hi"), 4 * n + kp + 1)
                    o = banks[fills[f"norm{n}.{kp}"][0]]
                    for kk in range(2):
                        k = 2 * kp + kk
                        ins = stt(lo[:, k, :], o[:, kk * SEQ:(kk + 1) * SEQ], col(gain, k), f32(hi[:, k, :]),
                                  ALU.mult, ALU.subtract)
                    read(ins, f"norm{n}.{kp}")

            def ffn_part(n):
                f = ffn[n]

                def low(j):
                    dve.wait_ge(S("ffn_hi"), FF_TILES * (n - 1) + j + 1)
                    tt(f["lo"][:, j, :], f["act"][:, j % 2, :], f32(f["hi"][:, j, :]), ALU.subtract).then_inc(S("ffn_lo"), 1)

                for j in range(FF_TILES):
                    dve.wait_ge(S("ffn_gate"), FF_TILES * (n - 1) + j + 1)
                    if j >= 2:
                        dve.wait_ge(S("ffn_lo"), FF_TILES * (n - 1) + j - 1)
                    o = banks[fills[f"up{n}.{j}"][0]]
                    read(tt(f["act"][:, j % 2, :], o[:, SEQ:2 * SEQ], f["gate"][:, j % 2, :], ALU.mult), f"up{n}.{j}")
                    if j:
                        low(j - 1)
                low(FF_TILES - 1)
                if n == 1:
                    dve.wait_ge(S("mem_in"), 16)
                    norm_rows(1, mem_xn, mem_xn, f["xn"])
                    norm_low(1, "mem_norm_g", mem_hi, mem_lo)
                i_post = 0 if n == 1 else 3
                dve.wait_ge(S("post_g_in"), 16 * (i_post + 1))
                for i in (2, 3, 0, 1):
                    t, h = i // 2, slice(i % 2 * 512, (i % 2 + 1) * 512)
                    key = f"down{n}.{i}"
                    o = full(dve, key)
                    if t == 0:
                        dve.wait_ge(S("post_ssq"), POST_SSQ[i_post] - 3 + i)
                    read(stt(f["xn"][:, t, h], o[:], 0.5, post_g[:, h], ALU.mult, ALU.mult), key)
                dve.wait_ge(S("post_ssq"), POST_SSQ[i_post])
                link(tt(post_sum[:], post_ssq[:, :, 0], post_ssq[:, :, 1], ALU.add))
                residual(i_post, [f"down{n}.{i}" for i in range(4)], f["xn"])

            def residual(i_post, keys, y):
                inverse_root(rstd[:, 2:4], post_sum[:], 2, D, EPS)
                for key in keys:
                    wait_read(dve, key)
                for t in range(TOK):
                    stt(x[:, t, :], y[:, t, :], rstd[:, 2 + t:3 + t], x[:, t, :], ALU.mult, ALU.add).then_inc(S("x_ready"), 1)
                dve.wait_ge(S("x_ready"), X_READY[i_post])

            def out_part(key, i_post, between=None):
                dve.wait_ge(S("post_g_in"), 16 * (i_post + 1))
                for i in range(4):
                    dve.wait_ge(S("post_ssq"), POST_SSQ[i_post - 1] + i + 1)
                    o = banks[fills[f"{key}{i}"][0]]
                    c = slice(i * 256, (i + 1) * 256)
                    read(tt(mg_T[:, :, c], two(o), post_g[:, c].unsqueeze(1).to_broadcast([P, TOK, 256]), ALU.mult), f"{key}{i}")
                    if between:
                        between(i)
                link(dve.tensor_reduce(post_sum[:], post_ssq[:], AX.X, ALU.add))
                residual(i_post, [f"{key}{i}" for i in range(4)], mg_T)

            def each(src, reps):
                return src.unsqueeze(2).to_broadcast([P, src.shape[1], reps])

            dve.wait_ge(S("x_in"), 16)
            norm_rows(0, x, ffn[1]["xn"], ffn[1]["xn"])
            dve.wait_ge(S("cols_in"), 16)
            norm_low(0, "ffn1_pre_g", hT_hi, hT_lo)
            ffn_part(1)

            norm_rows(2, x, mix_xn, mix_xn)
            norm_low(2, "mix_pre_g", hT_hi, hT_lo)
            dve.wait_ge(S("rows_in"), 32)
            o = full(dve, "dt")
            for t in range(TOK):
                ins = tt(ssd_dtt[:, 0, t * 32:(t + 1) * 32], o[:, t * 256:t * 256 + 32], row("ssd_dt_bias"), ALU.add)
            read(ins, "dt")
            wait_read(dve, "dt")
            link(ts(ssd_dtt[:, 1], ssd_dtt[:, 0], -1.0, None, ALU.mult))
            tt(ssd_dtt[:, 1], ssd_dtt[:, 1], ssd_dtt[:, 0], ALU.min).then_inc(S("dt_abs"), 1)

            dve.wait_ge(S("dt_exp"), 2)
            e, u, ln, c5 = ssd_dtt[:, 2], ssd_dtt[:, 3], ssd_dtt[:, 4], ssd_dtt[:, 5]
            ts(u, e, 1.0, None, ALU.add).then_inc(S("dt_one"), 1)
            dve.wait_ge(S("dt_one"), 1)
            link(ts(c5, u, -1.0, None, ALU.add))
            link(tt(c5, e, c5, ALU.subtract))
            link(dve.reciprocal(ssd_dtt[:, 1], u))
            link(tt(c5, c5, ssd_dtt[:, 1], ALU.mult))
            dve.wait_ge(S("dt_ln"), 1)
            link(tt(ln, ln, c5, ALU.add))
            link(stt(ssd_dt[:].rearrange("p t h -> p (t h)"), ssd_dtt[:, 0], 0.0, ln, ALU.max, ALU.add))
            dve.wait_ge(S("dt_exp"), 2)
            for t in range(TOK):
                stt(ssd_A[:, t, :], ssd_dt[:, t, :], -1.0, ssd_eA[:], ALU.mult, ALU.mult).then_inc(S("ssd_A"), 1)
            dve.wait_ge(S("ssd_A"), 2)

            def causal_conv(key, i, dst, w, b, first, taps):
                o = full(dve, key)
                for c in range(2):
                    ch = first + c
                    u, v = o[:, c * SEQ:(c + 1) * SEQ], dst[:, c, :]
                    link(ts(v, u, col(w, taps * ch + taps - 1), col(b, ch), ALU.mult, ALU.add))
                    for j in range(1, taps):
                        ins = stt(v[:, j:SEQ], u[:, 0:SEQ - j], col(w, taps * ch + taps - 1 - j), v[:, j:SEQ], ALU.mult, ALU.add)
                        if c == 0 or j < taps - 1:
                            link(ins)
                read(ins, key)

            for i in range(12):
                if i >= 2:
                    dve.wait_ge(S("xbc_silu"), i - 1)
                causal_conv(f"xbc{i}", i, ssd_conv[:, i % 2], "ssd_conv_w", "ssd_conv_b", 2 * i, SSD_CONV)

            def ssd_inputs(c):
                tt(ssd_xdt[:].rearrange("p (h d) -> p h d", d=64), ssd_y[:, c, :].rearrange("p (h d) -> p h d", d=64),
                   each(ssd_dt[:, c, :], 64), ALU.mult).then_inc(S("ssd_xdt"), 1)

            def ssd_steps(u):
                c, g = divmod(u, SSD_GROUPS)
                for q in range(2):
                    h = 8 * g + 4 * q
                    tt(ssd_uA[:, q, :].rearrange("p (h l) -> p h l", h=4), upper.unsqueeze(1).to_broadcast([P, 4, P]),
                       each(ssd_A[:, c, h:h + 4], P), ALU.mult).then_inc(S("ssd_uA"), 1)

            def ssd_rows(u):
                c, g = divmod(u, SSD_GROUPS)
                ys = ssd_y[:, c, g * 512:(g + 1) * 512]
                yh, th = ys.rearrange("p (h d) -> p h d", d=64), ssd_t[:].rearrange("p (h d) -> p h d", d=64)
                link(tt(th, yh, each(row("ssd_D")[:, 8 * g:8 * g + 8], 64), ALU.mult))
                o = full(dve, f"diag{u}")
                if c == 0:
                    read(tt(ys, o[:], ssd_t[:], ALU.add), f"diag{u}")
                    wait_read(dve, f"diag{u}")
                else:
                    read(tt(ys, o[:], ssd_t[:], ALU.add), f"diag{u}")
                    wait_read(dve, f"diag{u}")
                    o = full(dve, f"yoff{g}")
                    read(tt(th, o[:].rearrange("p (h d) -> p h d", d=64), each(ssd_ecs[:, 8 * g:8 * g + 8], 64), ALU.mult),
                         f"yoff{g}")
                    wait_read(dve, f"yoff{g}")
                    link(tt(ys, ys, ssd_t[:], ALU.add))

            for i in range(10):
                wait_read(dve, f"xT{i}")
            ssd_inputs(0)
            ssd_steps(0)
            dve.wait_ge(S("ssd_xdt"), 1)
            wait_read(dve, "sums")
            tt(ssd_xdd[:].rearrange("p (h d) -> p h d", d=64), ssd_xdt[:].rearrange("p (h d) -> p h d", d=64),
               each(ssd_decay[:], 64), ALU.mult).then_inc(S("ssd_xdd"), 1)
            dve.wait_ge(S("ssd_ecs"), 1)
            for i in range(1, 10):
                if i <= 8:
                    u = i - 1
                    if u:
                        dve.wait_ge(S("ssd_M"), 2 * u)
                    o = full(dve, f"cb{u}")
                    read(tt(ssd_cb[:], o[:, 0:P], upper, ALU.mult), f"cb{u}")
                    wait_read(dve, f"cb{u}")
                if i >= 2:
                    ssd_rows(i - 2)
                if i == 5:
                    ssd_inputs(1)
                if i <= 8:
                    for q in range(2):
                        wait_read(dve, f"seg{u}.{q}")
                        tt(ssd_M[:, q, :].rearrange("p (h l) -> p h l", h=4), ssd_L[:, q, :].rearrange("p (h l) -> p h l", h=4),
                           ssd_cb[:].unsqueeze(1).to_broadcast([P, 4, P]), ALU.mult).then_inc(S("ssd_M"), 1)
                    if u < 7:
                        ssd_steps(u + 1)

            for j in range(2):
                dve.tensor_tensor_reduce(da_junk2[:, j, :], row(f"da_lambda_q{j + 1}"), row(f"da_lambda_k{j + 1}"), 1.0, 0.0,
                                         ALU.mult, ALU.add, da_lam[:, j:j + 1]).then_inc(S("lam_dot"), 1)
            ts(sub_g[:], col("da_subln_g"), 1.0 - LAM_INIT, None, ALU.mult).then_inc(S("sub_g"), 1)
            dve.wait_ge(S("lam_exp"), 1)
            link(tt(da_lam[:, 0:1], da_lam[:, 3:4], da_lam[:, 2:3], ALU.subtract))
            link(ts(da_lam[:, 0:1], da_lam[:, 0:1], -LAM_INIT, None, ALU.add))

            def da_max(h):
                for j in range(2):
                    key = f"das{h}.{j}"
                    o = full(dve, key)
                    read(tt(da_s[:, j, :], o[:, 0:384], causal, ALU.add), key)
                for j in range(2):
                    wait_read(dve, f"das{h}.{j}")
                st = da_st[:, 0, :].rearrange("p (j q) -> p j q", j=2)
                link(dve.tensor_reduce(st[:, :, 0], da_s[:, :, 0:P], AX.X, ALU.max))
                link(dve.tensor_reduce(st[:, :, 1], da_s[:, :, P:P + SEQ], AX.X, ALU.max))
                ts(da_st[:, 1, :], da_st[:, 0, :], -DA_DIM ** -0.5, None, ALU.mult).then_inc(S("da_max"), 1)

            def da_probs(h):
                dve.wait_ge(S("da_exp"), 4 * h + 4)
                link(dve.reciprocal(da_st[:, 3, :], da_st[:, 2, :]))
                link(ts(da_st[:, 3, 2:4], da_st[:, 3, 2:4], da_lam[:, 0:1], None, ALU.mult))
                if h:
                    full(dve, f"daT{h - 1}")
                for q in range(2):
                    c = slice(0, P) if q == 0 else slice(P, P + SEQ)
                    link(ts(da_P[:, c], da_p[:, 0, c], da_st[:, 3, q:q + 1], None, ALU.mult))
                    stt(da_P[:, c], da_p[:, 1, c], da_st[:, 3, 2 + q:3 + q], da_P[:, c], ALU.mult, ALU.add)\
                        .then_inc(S("da_P"), 1)

            def gate_bias(key, i, dst, b):
                o = full(dve, key)
                for c in range(2):
                    ins = ts(dst[:, 2 * i + c, :], o[:, c * SEQ:(c + 1) * SEQ], col(b, 2 * i + c), None, ALU.add)
                read(ins, key)

            def y_low(kp):
                dve.wait_ge(S("y_hi"), Y_TURNS.index(kp) + 1)
                o = banks[fills[f"yT{kp}"][0]]
                for i in range(2):
                    k = 2 * kp + i
                    hi, lo = (hT_hi, hT_lo) if k < 8 else (y2_hi, y2_lo)
                    ins = stt(lo[:, k % 8, :], o[:, i * SEQ:(i + 1) * SEQ], col("ssd_norm_g", k), f32(hi[:, k % 8, :]),
                              ALU.mult, ALU.subtract)
                read(ins, f"yT{kp}")

            for i in range(16):
                if i < 8:
                    o = full(dve, f"z{i}")
                    read(dve.tensor_copy(ssd_z[:, :, i * 256:(i + 1) * 256], two(o)), f"z{i}")
                else:
                    gate_bias(f"gate{i - 8}", i - 8, mix_gate, "b_gate")
                if i % 2 == 0:
                    da_max(i // 2)
                    da_probs(i // 2)
                if i == 9:
                    for t in range(TOK):
                        dve.wait_ge(S("z_silu"), t + 1)
                        tt(ssd_y[:, t, :], ssd_y[:, t, :], ssd_z[:, t, :], ALU.mult).then_inc(S("ssd_yg"), 1)
                if i == 12:
                    dve.wait_ge(S("ssd_ssq"), TOK * SSD_GROUPS)
                    inverse_root(rstd[:, 0:8], ssd_ssq[:].rearrange("p t g -> p (t g)"), 8, SSD_INNER // SSD_GROUPS, SUB_EPS)
                    for t in range(TOK):
                        for g in range(SSD_GROUPS):
                            c = slice(g * 512, (g + 1) * 512)
                            ts(ssd_y[:, t, c], ssd_y[:, t, c], rstd[:, 4 * t + g:4 * t + g + 1], None, ALU.mult)\
                                .then_inc(S("ssd_yn"), 1)
                if i >= 13:
                    y_low(i - 9)
            y_low(7)

            for kp in range(4):
                y_low(kp)
            wait_read(dve, f"dao{DA_HEADS - 1}")
            dve.wait_ge(S("da_ssq"), TOK * DA_HEADS)
            dve.wait_ge(S("ssd_yn"), TOK * SSD_GROUPS)
            inverse_root(rstd[:], da_ssq[:].rearrange("p t h -> p (t h)"), TOK * DA_HEADS, 2 * DA_DIM, SUB_EPS)
            for t in range(TOK):
                oh = da_o[:, :, t, :]
                tt(oh, oh, each(rstd[:, t * DA_HEADS:(t + 1) * DA_HEADS], P), ALU.mult).then_inc(S("da_on"), 1)
            dve.wait_ge(S("mix_gate"), 1)
            for i in range(8):
                o = full(dve, f"ssd{i}")
                read(tt(mg[:, i, :], o[:, 0:SEQ], mix_gate[:, 8 + i, :], ALU.mult), f"ssd{i}")
                if i == 4:
                    for hp in range(4):
                        dve.wait_ge(S("o_hi"), hp + 1)
                        o = banks[fills[f"oT{hp}"][0]]
                        c = slice(2 * hp, 2 * hp + 2)
                        read(stt(o_lo[:, c, :], two(o), sub_g[:, 0:1], f32(o_hi[:, c, :]), ALU.mult, ALU.subtract), f"oT{hp}")
            dve.wait_ge(S("mix_gate"), 2)
            for i in range(8):
                wait_read(dve, f"ssd{i}")
            for i in range(4):
                o = full(dve, f"attn{i}")
                c = slice(2 * i, 2 * i + 2)
                read(tt(mix_gate[:, c, :], two(o), mix_gate[:, c, :], ALU.mult), f"attn{i}")
                wait_read(dve, f"attn{i}")
                tt(mg[:, c, :], mg[:, c, :], mix_gate[:, c, :], ALU.add).then_inc(S("mixed"), 1)
                dve.wait_ge(S("mixed_hi"), i + 1)
                tt(mixed_lo[:, c, :], mg[:, c, :], f32(mixed_hi[:, c, :]), ALU.subtract).then_inc(S("mixed_lo"), 1)

            def hidden_arg(i):
                arg, turns, r = hid[:, 2 * i, :], fil_t[:, 0, :], fil_t[:, 1, :]
                o = full(dve, f"hid{i}")
                read(ts(arg, o[0:FILTER_HIDDEN, 0:SEQ], fcols[:, 2 * i:2 * i + 1], fcols[:, 2 * i + 1:2 * i + 2], ALU.add, ALU.mult),
                     f"hid{i}")
                wait_read(dve, f"hid{i}")
                link(ts(turns, arg, 1.0 / (2 * math.pi), ROUND, ALU.mult, ALU.add))
                link(ts(turns, turns, -ROUND, None, ALU.add))
                link(stt(r, turns, -TURN_HI, arg, ALU.mult, ALU.add))
                link(stt(r, turns, -TURN_MID, r, ALU.mult, ALU.add))
                link(stt(r, turns, -TURN_LO, r, ALU.mult, ALU.add))
                ts(arg, r, PI_BELOW, -PI_BELOW, ALU.min, ALU.max).then_inc(S("hid_arg"), 1)

            def mix_between(i):
                if i in (0, 2):
                    hidden_arg(i // 2)

            out_part("mix", 1, mix_between)

            norm_rows(3, x, xa_xn, xa_xn)
            norm_low(3, "xa_pre_g", hT_hi, hT_lo)

            def softmax_max(key, st, scale, sem):
                o = full(dve, key)
                link(dve.tensor_reduce(st[:, 0, :], two(o), AX.X, ALU.max))
                ts(st[:, 1, :], st[:, 0, :], -scale, None, ALU.mult).then_inc(S(sem), 1)

            def softmax_scale(key, st, p, sem):
                wait_read(dve, key)
                link(dve.reciprocal(st[:, 3, :], st[:, 2, :]))
                for q in range(2):
                    ts(p[:, q, :], p[:, q, :], st[:, 3, q:q + 1], None, ALU.mult).then_inc(S(sem), 1)

            def filter_decay():
                for i in range(8):
                    wait_read(dve, f"taps{i}")
                for t in range(TOK):
                    k = kfil[:, t, :].rearrange("p (c d) -> p c d", c=4)
                    ins = tt(k, k, decay[:, t, :].unsqueeze(1).to_broadcast([P, 4, HY]), ALU.mult)
                link(ins)
                dve.wait_ge(S("bias_in"), 16)
                for n in range(2):
                    k = kfil[0:1, 0, 2 * n * HY:(2 * n + 1) * HY]
                    tt(k, k, bias_row[:, n, :], ALU.add).then_inc(S("kfil_bias"), 1)

            for i in range(XA_HEADS + 3):
                if i == 0:
                    filter_decay()
                if 1 <= i <= XA_HEADS:
                    h = i - 1
                    softmax_max(f"xas{h}", xa_st, XA_DIM ** -0.5, "xa_max")
                    softmax_scale(f"xas{h}", xa_st, xa_p[:, h % 2], "xa_P")
                if i >= 3:
                    h = i - 3
                    dve.wait_ge(S("xo_hi"), h + 1)
                    o = banks[fills[f"xao{h}"][0]]
                    read(tt(xa_lo[:, 2 * h:2 * h + 2, :], two(o), f32(xa_hi[:, 2 * h:2 * h + 2, :]), ALU.subtract), f"xao{h}")
            out_part("xo", 2)

            norm_rows(4, x, ffn[2]["xn"], ffn[2]["xn"])
            norm_low(4, "ffn2_pre_g", hT_hi, hT_lo)
            ffn_part(2)

            norm_rows(5, x, sec_xn, sec_xn)
            norm_low(5, "g_norm_2", hT_hi, hT_lo)

            dve.wait_ge(S("c_ssq"), 4)
            inverse_root(rstd[:, 4:6], c_ssq[:, 0, :], 2, Q_LORA, EPS)
            inverse_root(rstd[:, 6:8], c_ssq[:, 1, :], 2, KV_LORA, EPS)
            for t in range(TOK):
                ts(cq[:, t, :], cq[:, t, :], rstd[:, 4 + t:5 + t], None, ALU.mult).then_inc(S("c_ready"), 1)
                ts(ckv[:, t, :], ckv[:, t, :], rstd[:, 6 + t:7 + t], None, ALU.mult).then_inc(S("c_ready"), 1)

            for k in range(5):
                dve.wait_ge(S("c_hi"), min(2 * (k // 2) + 2, 5))
                o = banks[fills[f"cT{k // 2}"][0]]
                hi, lo, g = (cq_hi[:, k, :], cq_lo[:, k, :], col("g_cq_2", k)) if k < 3 else \
                    (ckv_hi[:, k - 3, :], ckv_lo[:, k - 3, :], col("g_ckv_2", k - 3))
                ins = stt(lo, o[:, k % 2 * SEQ:(k % 2 + 1) * SEQ], g, f32(hi), ALU.mult, ALU.subtract)
                if k % 2 or k == 4:
                    read(ins, f"cT{k // 2}")

            dve.wait_ge(S("rope_in"), 16)

            def head_rows(s):
                r = mq[:, s].rearrange("p t h d -> p (t h) d")
                n = TOK * MLA_HEADS
                sq = msq[:].rearrange("p t h d -> p (t h) d")
                link(tt(sq, r, r, ALU.mult))
                link(dve.tensor_reduce(m_ssq[:], sq, AX.X, ALU.add))
                inverse_root(rstd[:], m_ssq[:], n, QK_DIM, EPS)
                link(tt(r, r, each(rstd[:], QK_DIM), ALU.mult))
                g = row("g_qn_2" if s == 0 else "g_kn_2")
                link(tt(r, r, g.unsqueeze(1).to_broadcast([P, n, QK_DIM]), ALU.mult))
                for t in range(TOK):
                    cos, sin = (m_ropeT[:, t, i * 16:(i + 1) * 16].unsqueeze(1).to_broadcast([P, MLA_HEADS, 16]) for i in range(2))
                    a1, a2 = mq[:, s, t, :, 64:80], mq[:, s, t, :, 80:96]
                    parts = [m_t[:, i, t] for i in range(4)]
                    tt(parts[0], a1, cos, ALU.mult)
                    tt(parts[1], a2, sin, ALU.mult)
                    tt(parts[2], a1, sin, ALU.mult)
                    link(tt(parts[3], a2, cos, ALU.mult))
                    link(tt(a1, parts[0], parts[1], ALU.subtract))
                    ins = tt(a2, parts[2], parts[3], ALU.add)
                    if t == 0:
                        link(ins)
                ins.then_inc(S("mla_qk"), 1)

            def centred_conv(i):
                key = f"hy{i}"
                dve.wait_ge(S("hy_mid"), 2 * i + 2)
                o = banks[fills[key][0]]
                for c in range(2):
                    ch = 2 * i + c
                    u, v = o[:, c * SEQ:(c + 1) * SEQ], hyF[:, ch, :]
                    link(stt(v[:, 1:SEQ], u[:, 0:SEQ - 1], col("w_short_2", 3 * ch), v[:, 1:SEQ], ALU.mult, ALU.add))
                    ins = stt(v[:, 0:SEQ - 1], u[:, 1:SEQ], col("w_short_2", 3 * ch + 2), v[:, 0:SEQ - 1], ALU.mult, ALU.add)
                read(ins, key)

            for t in range(TOK):
                wait_read(dve, f"uq0.{t}.0")
                wait_read(dve, f"uq1.{t}.0")
            head_rows(0)
            for t in range(TOK):
                for h in (0, 512):
                    wait_read(dve, f"ukv.{t}.{h}")
            wait_read(dve, "cq1")
            for t in range(TOK):
                ins = dve.tensor_copy(mq[:, 1, t, :, QK_NOPE:], k_rope[:, t, :].unsqueeze(1).to_broadcast([P, MLA_HEADS, QK_ROPE]))
            link(ins)
            centred_conv(0)
            centred_conv(1)
            head_rows(1)
            for i in range(2, 6):
                centred_conv(i)
            for j in range(8):
                wait_read(dve, f"spec{j}")
            for i in range(6):
                wait_read(dve, f"hy{i}")

            def hyena_product(n, f):
                kr, ki = spec[:, n, f, :], spec[:, n, f + 2, :]
                if n or f:
                    dve.wait_ge(S("hy_yf"), 4 * n + 2 * f)
                ur, ui = full(dve, f"uf{n}.{f}"), full(dve, f"uf{n}.{f + 2}")
                tt(yt[:, 0, :], ui[:], ki, ALU.mult)
                read(tt(yt[:, 1, :], ui[:], kr, ALU.mult), f"uf{n}.{f + 2}")
                wait_read(dve, f"uf{n}.{f + 2}")
                tt(ki, ur[:], ki, ALU.mult)
                read(tt(kr, ur[:], kr, ALU.mult), f"uf{n}.{f}")
                wait_read(dve, f"uf{n}.{f}")
                tt(kr, kr, yt[:, 0, :], ALU.subtract).then_inc(S("hy_yf"), 1)
                tt(ki, ki, yt[:, 1, :], ALU.add).then_inc(S("hy_yf"), 1)

            def hyena_gate(n):
                for cp in range(2):
                    key = f"yt{n}.{cp}"
                    o = full(dve, key)
                    k = 4 * (n + 1) + 2 * cp
                    read(tt(hyF[:, 2 * cp:2 * cp + 2, :], two(o), hyF[:, k:k + 2, :], ALU.mult), key)

            def softmax_rows(h):
                softmax_max(f"ms{h}", m_st, QK_DIM ** -0.5, "m_max")
                softmax_scale(f"ms{h}", m_st, m_p[:, h % 2], "m_P")

            def at_low(c):
                dve.wait_ge(S("at_hi"), c + 1)
                tt(at_lo[:, c, :], z_at[:, c, :], f32(at_hi[:, c, :]), ALU.subtract).then_inc(S("at_lo"), 1)

            def fin_low(i):
                dve.wait_ge(S("fin_hi"), i + 1)
                tt(hT_lo[:, 2 * i:2 * i + 2, :], mg2[:, 2 * i:2 * i + 2, :], f32(hT_hi[:, 2 * i:2 * i + 2, :]), ALU.subtract)\
                    .then_inc(S("fin_lo"), 1)

            def wide_gate(i, first):
                for p in range(2):
                    key = f"{'hyo' if first else 'ato'}{i}.{p}"
                    o = full(dve, key)
                    k = 4 * i + 2 * p
                    m, g = mg2[:, k:k + 2, :], gate2[:, (0 if first else 8) + k:(0 if first else 8) + k + 2, :]
                    if first:
                        read(tt(m, two(o), g, ALU.mult), key)
                    else:
                        read(tt(g, two(o), g, ALU.mult), key)
                        wait_read(dve, key)
                        tt(m, m, g, ALU.add).then_inc(S("fin"), 1)
                        fin_low(2 * i + p)

            for i in range(MLA_HEADS + 2):
                c = (i - 3) // 2
                if i >= 3 and i % 2:
                    o = full(dve, f"mo{c}")
                    read(tt(z_at[:, c, :], o[:, 0:SEQ], z_at[:, c, :], ALU.mult), f"mo{c}")
                if i < MLA_HEADS:
                    softmax_rows(i)
                if i >= 3 and i % 2:
                    at_low(c)
                if i in (0, 1, 4, 5):
                    hyena_product(i // 4, i % 4)
                elif i in (2, 6):
                    hyena_gate(i // 4)
                elif i == 3:
                    link(tt(hyF[:, 8:12, :], hyF[:, 8:12, :], z_hy[:], ALU.mult))
                elif i == 7:
                    for j in range(HY_TILES):
                        dve.wait_ge(S("hy_hi"), j + 1)
                        tt(hy_lo[:, j, :], hyF[:, j, :], f32(hy_hi[:, j, :]), ALU.subtract).then_inc(S("hy_lo"), 1)
                elif i == 8:
                    dve.wait_ge(S("gate2"), 2)
                if i >= 8:
                    wide_gate(i - 8, True)
            for i in range(2):
                for p in range(2):
                    wait_read(dve, f"hyo{i}.{p}")
            for i in range(2):
                wide_gate(i, False)
            for i in range(4):
                o = full(dve, f"out{i}")
                c = slice(i * 256, (i + 1) * 256)
                tt(x[:, :, c], two(o), x[:, :, c], ALU.add).then_inc(S("out_ready"), 1)

        @block.gpsimd
        def _(pool):
            for b in range(NBLOCK):
                pool.wait_ge(w_hi_in, b + 1)
                pool.tensor_tensor(w_lo[b % STAGES][:], w_raw[b % RING][:], w_hi[b % STAGES][:].bitcast(F32), ALU.subtract)\
                    .then_inc(w_lo_in, 1)

        @block.sync
        def _(sp):
            sp.dma_start(x[:], a["x"].rearrange("(t p) d -> p t d", p=P)).then_inc(S("x_in"), 16)
            for b in range(NBLOCK):
                if b >= RING:
                    sp.wait_ge(w_lo_in, b - RING + 1)
                sp.dma_start(w_raw[b % RING][:], a["w"][b]).then_inc(w_landed[b % RING], 16)
                if b == 0:
                    sp.dma_start(square[:], a["c_square"]).then_inc(S("square_in"), 16)
                    sp.dma_start(cols[:], a["cols"]).then_inc(S("cols_in"), 16)
            for i in range(4):
                sp.wait_ge(S("out_ready"), i + 1)
                c = slice(i * 256, (i + 1) * 256)
                sp.dma_start(out.rearrange("(t p) d -> p t d", p=P)[:, :, c], x[:, :, c]).then_inc(S("out_in"), 16)
            sp.wait_ge(S("out_in"), 64)


def kernel(**inputs):
    import concourse.bacc as bacc
    from concourse.bass_utils import run_bass_kernel_spmd

    given = {name: np.asarray(value) for name, value in inputs.items()}
    arrays = {"x": given["x"][0], "mem": given["mem"][0]}

    stream = np.zeros((NBLOCK, P, BLOCK), np.float32)
    for n, (_, w, first, kt, columns) in enumerate(BLOCKS):
        rows = given[w][0][first:first + kt * P].reshape(kt, P, -1).transpose(1, 0, 2)
        width = sum(c for _, c in columns)
        part = stream[n, :, 0:kt * width].reshape(P, kt, width)
        at = 0
        for c, m in columns:
            part[:, :, at:at + m] = rows[:, :, c:c + m]
            at += m
    arrays["w"] = stream

    def over_partitions(v):
        v = v.reshape(-1, v.shape[-1])
        return v.reshape(v.shape[0], -1, P).transpose(2, 1, 0).reshape(P, -1)

    arrays["cols"] = np.concatenate([over_partitions(given[n][0]) for n in COLS], axis=1)
    arrays["rows"] = np.concatenate([given[n][0].reshape(1, -1) for n in ROWS], axis=1)
    arrays["fcols"] = np.stack([given[n][0] for n in ("b_f1_2", "freq_1_2", "b_f2_2", "freq_2_2")], axis=1)
    for n in POST + ["w_f1_2", "w_f2_2", "w_f3_2"]:
        arrays[n] = given[n][0].reshape(1, -1) if n in POST else given[n][0]
    arrays["hy_bias"] = given["hy_bias_2"][0]
    arrays.update(shape_constants())
    arrays = {n: np.ascontiguousarray(v) for n, v in arrays.items()}

    nc = bacc.Bacc("TRN2", target_bir_lowering=False, num_devices=1)
    a = {n: nc.dram_tensor(f"in_{n}", v.shape, mybir.dt.from_np(v.dtype), kind="ExternalInput").ap()
         for n, v in arrays.items()}
    out = nc.dram_tensor("out", (SEQ, D), F32, kind="ExternalOutput").ap()
    program(nc, a, out)
    r = run_bass_kernel_spmd(nc, [{f"in_{n}": v for n, v in arrays.items()}], core_ids=[0])
    return r.results[0]["out"].reshape(1, SEQ, D)
```

```python
import math
from contextlib import ExitStack

import numpy as np

import concourse.bass as bass
from concourse import mybir

F32 = mybir.dt.float32
F32R = mybir.dt.float32r
I32 = mybir.dt.int32
ALU = mybir.AluOpType
ACT = mybir.ActivationFunctionType
AX = mybir.AxisListType

P = 128
SEQ = 256
TOK = SEQ // P
D = 1024
KD = D // P
D_FF = 2816
FF_TILES = D_FF // P
EPS = 1e-6
SUB_EPS = 1e-5

DA_HEADS = 8
DA_DIM = 64
SSD_INNER = 2048
SSD_HEADS = 32
SSD_GROUPS = 4
SSD_CONV = 4
XBC = 3072
XA_HEADS = 4
XA_DIM = 256
LAM_INIT = 0.8 - 0.6 * math.exp(-0.3 * 0)

HY = 512
HY_TILES = HY // P
FILTER_EMB = 33
FILTER_HIDDEN = 64
MLA_HEADS = 8
QK_NOPE, QK_ROPE, V_DIM = 64, 32, 64
QK_DIM = QK_NOPE + QK_ROPE
Q_LORA, KV_LORA = 384, 256

ROUND = 1.5 * 2 ** 23
TURN_HI = 6.28125
TURN_MID = float(np.float32(round((2 * math.pi - TURN_HI) * 2 ** 20) / 2 ** 20))
TURN_LO = 2 * math.pi - TURN_HI - TURN_MID
PI_BELOW = 3.1415925

BLOCK = 2048
RING = 3
STAGES = 3

TURN = 3
assert RING == STAGES == TURN
PAIRS = FF_TILES // 2
PAIR_TURNS = PAIRS - 2

W_IN_AT = {"q": 0, "k": 1024, "v": 2048, "z": 3072, "xbc": 5120, "dt": 8192, "gate": 8224}
W_IN2_AT = {"hy": 0, "z_hy": 1536, "cq": 2048, "ckv": 2432, "rope": 2688, "z_at": 2720, "gate": 3232}


def weight_blocks():
    out = []

    def add(stage, w, cols, kt=KD, row=0):
        out.append((stage, w, row, kt, cols))

    def ffn(n):
        for j in range(FF_TILES):
            if j % 2 and j > 1:
                add(f"ffn{n}", f"ffn{n}_w_down", [(0, D)], 2, (j - 3) * P)
            add(f"ffn{n}", f"ffn{n}_w_gu", [(j * P, P), (D_FF + j * P, P)])
        add(f"ffn{n}", f"ffn{n}_w_down", [(0, D)], 2, (FF_TILES - 2) * P)

    def plain(stage, w, at, n, width=256, kt=KD):
        for i in range(n):
            add(stage, w, [(at + i * width, width)], kt)

    ffn(1)
    plain("xa_kv", "xa_w_kv", 0, 8)
    add("dt", "w_in", [(W_IN_AT["dt"], SSD_HEADS)])
    plain("xbc", "w_in", W_IN_AT["xbc"], 12)
    plain("qkv", "w_in", W_IN_AT["q"], 12)
    plain("z", "w_in", W_IN_AT["z"], 8)
    plain("gate", "w_in", W_IN_AT["gate"], 8)
    plain("ssd_out", "w_branch_ssd", 0, 8, 128, 16)
    plain("attn_out", "w_branch_attn", 0, 4)
    plain("mix_out", "w_mix_out", 0, 4)
    plain("xa_q", "xa_w_q", 0, 4)
    plain("xa_o", "xa_w_o", 0, 4)
    ffn(2)
    add("cq", "w_in_2", [(W_IN2_AT["cq"], 256)])
    add("ckv", "w_in_2", [(W_IN2_AT["ckv"], 256)])
    add("cq_rope", "w_in_2", [(W_IN2_AT["cq"] + 256, P), (W_IN2_AT["rope"], QK_ROPE)])
    plain("z_hy", "w_in_2", W_IN2_AT["z_hy"], 2)
    plain("z_at", "w_in_2", W_IN2_AT["z_at"], 2)
    add("uq", "w_uq_2", [(0, 512)], 3)
    add("uq", "w_uq_2", [(512, 256)], 3)
    add("ukv", "w_ukv_2", [(0, 1024)], 2)
    plain("hy", "w_in_2", W_IN2_AT["hy"], 6)
    plain("gate2", "w_in_2", W_IN2_AT["gate"], 8)
    plain("hy_out", "w_hy_out_2", 0, 2, 512, 4)
    plain("at_out", "w_attn_out_2", 0, 2, 512, 4)
    plain("out", "w_out_2", 0, 4)
    return out


def up_at(n, j):
    return FIRST[f"ffn{n}"] + (j if j < 2 else 2 + 3 * (j // 2 - 1) + 2 * (j % 2))


def down_at(n, c):
    return FIRST[f"ffn{n}"] + (3 * c + 3 if c < PAIRS - 1 else 3 * PAIRS - 1)


BLOCKS = weight_blocks()
NBLOCK = len(BLOCKS)
assert NBLOCK % RING == 0
FIRST = {}
for _n, _b in enumerate(BLOCKS):
    FIRST.setdefault(_b[0], _n)

COLS = {}
for _name, _len in [("ffn1_pre_g", 8), ("mix_pre_g", 8), ("xa_pre_g", 8), ("mem_norm_g", 8), ("ffn2_pre_g", 8),
                    ("g_norm_2", 8), ("b_gate", 16), ("da_subln_g", 1), ("ssd_conv_w", 96), ("ssd_conv_b", 24),
                    ("ssd_norm_g", 16), ("b_gate_2", 16), ("w_short_2", 36), ("b_short_2", 12), ("g_cq_2", 3),
                    ("g_ckv_2", 2)]:
    COLS[_name] = (sum(v[1] for v in COLS.values()), _len)
NCOLS = sum(v[1] for v in COLS.values())

ROWS = {}
for _name, _len in [("ssd_dt_bias", 32), ("ssd_A_log", 32), ("ssd_D", 32), ("da_lambda_q1", 64), ("da_lambda_k1", 64),
                    ("da_lambda_q2", 64), ("da_lambda_k2", 64), ("g_qn_2", QK_DIM), ("g_kn_2", QK_DIM)]:
    ROWS[_name] = (sum(v[1] for v in ROWS.values()), _len)
NROWS = sum(v[1] for v in ROWS.values())
X_READY = [2, 4, 6, 8]
POST_SSQ = [4, 8, 12, 16]
MIXED = [slice(0, 2), slice(2, 4), slice(4, 6), slice(6, 7), slice(7, 8)]
Y_TURNS = [4, 5, 6, 7, 0, 1, 2, 3]
POST = ["ffn1_post_g", "mix_post_g", "xa_post_g", "ffn2_post_g"]


def shape_constants():
    i = np.arange(P)
    upper = (i[:, None] <= i[None, :]).astype(np.float32)
    strict = (i[:, None] > i[None, :]).astype(np.float32)
    causal = np.where(strict.T > 0, np.float32(-1e30), np.float32(0))
    mask = np.concatenate([causal, np.zeros((P, P), np.float32), causal], axis=1)
    square = np.concatenate([np.eye(P, dtype=np.float32), upper, strict, mask], axis=1)

    w = 2 * np.pi * (np.arange(SEQ) + 0.5) / (2 * SEQ)
    s = np.arange(SEQ)

    def tiles(m):
        return np.ascontiguousarray(m.reshape(-1, P, m.shape[1]).transpose(1, 0, 2).astype(np.float32))

    ahead = np.concatenate([np.cos(s[:, None] * w), -np.sin(s[:, None] * w)], axis=1)
    behind = np.concatenate([np.cos((s[:, None] + 1) * w), np.sin((s[:, None] + 1) * w)], axis=1)
    back = np.concatenate([np.cos(w[:, None] * s), -np.sin(w[:, None] * s)], axis=0) / SEQ
    dft = np.concatenate([tiles(ahead).reshape(P, -1), tiles(behind).reshape(P, -1), tiles(back).reshape(P, -1)], axis=1)

    t = np.linspace(0.0, 1.0, SEQ, dtype=np.float32)[:, None]
    bands = (FILTER_EMB - 1) // 2
    f = np.linspace(1e-4, bands - 1, bands, dtype=np.float32)
    ang = np.float32(2.0 * np.pi / SEQ) * np.arange(SEQ, dtype=np.float32)[:, None] * f[None, :]
    emb = np.concatenate([t, np.cos(ang), -np.sin(ang)], axis=-1).astype(np.float32)
    deltas = np.abs(np.linspace(math.log(1e-2) / 1.5, math.log(1e-2) / 0.3, HY, dtype=np.float32))
    decay = tiles(np.exp(-t * deltas))

    inv = np.float32(10000.0) ** (-np.arange(0, QK_ROPE, 2, dtype=np.float32) / np.float32(QK_ROPE))
    rot = s.astype(np.float32)[:, None] * inv[None, :]
    rope = tiles(np.concatenate([np.cos(rot), np.sin(rot)], axis=1))
    return {"c_square": square, "c_dft": dft, "c_emb": np.ascontiguousarray(emb.T), "c_decay": decay, "c_rope": rope}


def program(nc, a, out):
    with ExitStack() as ctx:
        def sb(name, shape, dt=F32, scope=ctx):
            return scope.enter_context(nc.sbuf_tensor("sb_" + name, shape, dt))

        sems = {}

        def S(name):
            if name not in sems:
                sems[name] = ctx.enter_context(nc.semaphore("s_" + name))
            return sems[name]

        w_raw = [sb(f"w_raw{i}", [P, BLOCK]) for i in range(RING)]
        w_hi = [sb(f"w_hi{i}", [P, BLOCK], F32R) for i in range(STAGES)]
        w_lo = [sb(f"w_lo{i}", [P, BLOCK], F32R) for i in range(STAGES)]
        x = sb("x", [P, TOK, D])
        square = sb("square", [P, 6 * P])
        ident, upper, strict, causal = square[:, 0:P], square[:, P:2 * P], square[:, 2 * P:3 * P], square[:, 3 * P:]
        cols = sb("cols", [P, NCOLS])
        strict_r = sb("strict_r", [P, P], F32R)
        fcols = sb("fcols", [FILTER_HIDDEN, 4])
        rows = sb("rows", [P, NROWS])
        sub_g = sb("sub_g", [P, 1])
        nt = sb("newton", [P, 5, 16])
        ssq = sb("ssq", [P, 4])
        post_ssq = sb("post_ssq", [P, TOK, 4])
        post_sum = sb("post_sum", [P, TOK])
        ssd_ssq = sb("ssd_ssq", [P, TOK, SSD_GROUPS])
        c_ssq = sb("c_ssq", [P, 2, TOK])
        m_ssq = sb("m_ssq", [P, TOK * MLA_HEADS])
        rstd = sb("rstd", [P, 16])
        hT_hi = sb("hT_hi", [P, KD, SEQ], F32R)
        hT_lo = sb("hT_lo", [P, KD, SEQ], F32R)

        def col(name, i=0, n=1):
            at = COLS[name][0] + i
            return cols[:, at:at + n]

        def row(name):
            at, n = ROWS[name]
            return rows[:, at:at + n]

        places = [0]

        def place(at, name, shape, dt=F32):
            with ExitStack() as here:
                places[0] += 1
                if at:
                    sb(f"before{places[0]}", [P, int(at * 256)], F32, here)
                return sb(name, shape, dt, here)

        post_g = place(100, "post_g", [P, D])
        ffn = {}
        for n in (1, 2):
            ffn[n] = {
                "xn": place(16, f"ffn{n}_xn", [P, TOK, D]),
                "gate": place(16, f"ffn{n}_gate", [P, 2, SEQ]),
                "act": place(18, f"ffn{n}_act", [P, 2, SEQ]),
                "hi": place(24, f"ffn{n}_hi", [P, 2, SEQ], F32R),
                "lo": place(26, f"ffn{n}_lo", [P, 2, SEQ], F32R),
                "junk": place(28, f"ffn{n}_junk", [P, 512]),
            }

        mem_xn = place(72, "mem_xn", [P, TOK, D])
        mem_junk = place(68, "mem_junk", [P, 1, D])
        mem_hi = place(82, "mem_hi", [P, KD, SEQ], F32R)
        mem_lo = place(90, "mem_lo", [P, KD, SEQ], F32R)
        xa_k = place(0, "xa_k", [P, KD, SEQ])
        xa_v = place(8, "xa_v", [P, TOK, D])

        mix_xn = place(48, "mix_xn", [P, TOK, D])
        ssd_y = place(16, "ssd_y", [P, TOK, SSD_INNER])
        da_q = place(32, "da_q", [P, DA_HEADS, SEQ])
        da_o = place(32, "da_o", [P, DA_HEADS, TOK, P])
        da_k = place(40, "da_k", [P, DA_HEADS, SEQ])
        ssd_bF = place(48, "ssd_bF", [P, SSD_GROUPS, SEQ])
        ssd_cF = place(52, "ssd_cF", [P, SSD_GROUPS, SEQ])
        ssd_bT = place(56, "ssd_bT", [P, SSD_GROUPS, P])
        ssd_dtt = place(58, "ssd_dtt", [P, 6, TOK * SSD_HEADS])
        ssd_dt = place(59.5, "ssd_dt", [P, TOK, SSD_HEADS])
        ssd_A = place(59.75, "ssd_A", [P, TOK, SSD_HEADS])
        ssd_conv = place(60, "ssd_conv", [P, 2, 2, SEQ])
        ssd_xF = place(64, "ssd_xF", [P, 2, 2, SEQ])
        ssd_xdd = place(60, "ssd_xdd", [P, SSD_INNER])
        ssd_xdt = place(68, "ssd_xdt", [P, SSD_INNER])
        ssd_state = place(76, "ssd_state", [P, SSD_GROUPS, 512])
        ssd_cb = place(84, "ssd_cb", [P, P])
        ssd_uA_hi = place(85, "ssd_uA_hi", [P, 2, 512], F32R)
        ssd_uA_lo = place(100, "ssd_uA_lo", [P, 2, 512], F32R)
        ssd_A_hi = place(84.5, "ssd_A_hi", [P, TOK, SSD_HEADS], F32R)
        ssd_A_lo = place(84.75, "ssd_A_lo", [P, TOK, SSD_HEADS])
        ssd_dtF = place(97, "ssd_dtF", [SSD_HEADS, SEQ])
        ssd_L = place(89, "ssd_L", [P, 2, 512])
        ssd_M = place(93, "ssd_M", [P, 2, 512])
        ssd_t = place(97, "ssd_t", [P, 512])
        ssd_eA = place(99, "ssd_eA", [P, SSD_HEADS])
        ssd_decay = place(99.25, "ssd_decay", [P, SSD_HEADS])
        ssd_ecs = place(99.5, "ssd_ecs", [P, SSD_HEADS])
        da_v = place(60, "da_v", [P, TOK, D])
        mix_gate = place(68, "mix_gate", [P, 16, SEQ])
        ssd_z = place(84, "ssd_z", [P, TOK, SSD_INNER])
        da_s = place(48, "da_s", [P, 2, 384])
        da_p = place(51, "da_p", [P, 2, 384])
        da_P = place(54, "da_P", [P, 384])
        da_PT = place(55.5, "da_PT", [P, 384])
        da_st = place(57, "da_st", [P, 4, 4])
        da_lam = place(57.25, "da_lam", [P, 4])
        da_ssq = place(57.5, "da_ssq", [P, TOK, DA_HEADS])
        da_junk = place(58, "da_junk", [P, P])
        da_junk2 = place(58.5, "da_junk2", [P, 2, DA_DIM])
        y2_hi = place(84, "y2_hi", [P, KD, SEQ], F32R)
        y2_lo = place(92, "y2_lo", [P, KD, SEQ], F32R)
        o_hi = place(40, "o_hi", [P, KD, SEQ], F32R)
        o_lo = place(60, "o_lo", [P, KD, SEQ], F32R)
        mg = place(48, "mg", [P, KD, SEQ])
        mixed_hi = place(16, "mixed_hi", [P, KD, SEQ], F32R)
        mixed_lo = place(24, "mixed_lo", [P, KD, SEQ], F32R)

        xa_q = place(16, "xa_q", [P, KD, SEQ])
        xa_xn = place(24, "xa_xn", [P, TOK, D])
        xa_p = place(24, "xa_p", [P, 2, 2, SEQ])
        xa_PT = place(28, "xa_PT", [P, 2, SEQ])
        xa_st = place(30, "xa_st", [P, 4, 2])
        xa_hi = place(32, "xa_hi", [P, KD, SEQ], F32R)
        xa_lo = place(40, "xa_lo", [P, KD, SEQ], F32R)
        post_tmp = place(56, "post_tmp", [P, 512])
        mg_T = mg[:].rearrange("p k t -> p (k t)").rearrange("p (t d) -> p t d", t=TOK)

        decay = place(60, "decay", [P, TOK, HY])
        bias_row = place(64, "bias_row", [1, 2, HY])
        kfil = place(68, "kfil", [P, TOK, 4 * HY])
        w_f3 = place(84, "w_f3", [FILTER_HIDDEN, 4 * HY])
        hid = place(92, "hid", [FILTER_HIDDEN, 4, SEQ])
        fil_t = place(96, "fil_t", [FILTER_HIDDEN, 2, SEQ])
        emb = place(98, "emb", [FILTER_EMB, SEQ])
        w_f12 = place(99, "w_f12", [FILTER_HIDDEN, 2, FILTER_HIDDEN])
        dft_f = place(0, "dft_f", [P, 2, TOK, 512])
        spec = place(84, "spec", [P, 2, 4, HY])

        gate2 = place(0, "gate2", [P, 16, SEQ])
        z_hy = place(16, "z_hy", [P, HY_TILES, SEQ])
        z_at = place(20, "z_at", [P, HY_TILES, SEQ])
        sec_xn = place(24, "sec_xn", [P, TOK, D])
        mv = place(24, "mv", [P, TOK, MLA_HEADS, V_DIM])
        dft_b = place(28, "dft_b", [P, 4, SEQ])
        cq = place(32, "cq", [P, TOK, Q_LORA])
        ckv = place(35, "ckv", [P, TOK, KV_LORA])
        c_junk = place(37, "c_junk", [P, Q_LORA])
        cq_hi = place(39, "cq_hi", [P, 3, SEQ], F32R)
        cq_lo = place(42, "cq_lo", [P, 3, SEQ], F32R)
        ckv_hi = place(45, "ckv_hi", [P, 2, SEQ], F32R)
        ckv_lo = place(47, "ckv_lo", [P, 2, SEQ], F32R)
        hyF = place(32, "hyF", [P, 12, SEQ])
        uT = place(44, "uT", [P, TOK, HY])
        mq = place(49, "mq", [P, 2, TOK, MLA_HEADS, QK_DIM])
        at_hi = place(49, "at_hi", [P, HY_TILES, SEQ], F32R)
        at_lo = place(53, "at_lo", [P, HY_TILES, SEQ], F32R)
        m_p = place(57, "m_p", [P, 2, 2, SEQ])
        k_rope = place(61, "k_rope", [P, TOK, QK_ROPE])
        m_ropeT = place(61.25, "m_ropeT", [P, TOK, QK_ROPE])
        m_st = place(61.5, "m_st", [P, 4, 2])
        msq = place(72, "msq", [P, TOK, MLA_HEADS, QK_DIM])
        m_t = place(100, "m_t", [P, 4, TOK, MLA_HEADS, 16])
        mqT = place(62, "mqT", [QK_DIM, 2, MLA_HEADS, SEQ])
        dft_a = place(78, "dft_a", [P, TOK, 512])
        m_PT = place(82, "m_PT", [P, 2, SEQ])
        yt = place(100, "yt", [P, 2, HY])
        hy_hi = place(84, "hy_hi", [P, HY_TILES, SEQ], F32R)
        hy_lo = place(88, "hy_lo", [P, HY_TILES, SEQ], F32R)
        mg2 = place(92, "mg2", [P, KD, SEQ])
        mq_rows = mq[:].rearrange("p s t h d -> p s t (h d)")
        banks = [ctx.enter_context(nc.psum_tensor(f"bank{i}", [P, 512], F32)) for i in range(8)]
        block_done, w_hi_in, w_lo_in = S("block_done"), S("w_hi_in"), S("w_lo_in")
        w_landed = [S(f"w_landed{i}") for i in range(RING)]
        bank_full = [S(f"bank_full{i}") for i in range(8)]
        bank_read = [S(f"bank_read{i}") for i in range(8)]

        fills = {}
        used = [0] * 8
        filled = [0] * 8

        def full(eng, key, turn=0):
            bank, _, n, b = fills[key]
            if b is None:
                eng.wait_ge(bank_full[bank], n)
            else:
                eng.wait_ge(block_done, b + 1 + TURN * turn)
            return banks[bank]

        def read(ins, key):
            ins.then_inc(bank_read[fills[key][0]], 1)

        def wait_read(eng, key, turn=0):
            eng.wait_ge(bank_read[fills[key][0]], fills[key][1] + turn)

        block = ctx.enter_context(nc.Block())

        @block.tensor
        def _(pe):
            def claim(key, bank, b=None):
                if used[bank]:
                    pe.wait_ge(bank_read[bank], used[bank])
                used[bank] += 1
                if b is None:
                    filled[bank] += 1
                fills[key] = (bank, used[bank], filled[bank], b)
                return banks[bank]

            def claim_turns(keys, bank, b, turn):
                pe.wait_ge(bank_read[bank], used[bank] + turn)
                for i, key in enumerate(keys):
                    used[bank] += 1
                    fills[key] = (bank, used[bank], filled[bank], b + TURN * i)
                return banks[bank]

            def ends(ins, key):
                ins.then_inc(bank_full[fills[key][0]], 1)

            def product(o, a_hi, a_lo, b_hi, b_lo, first, last):
                pe.matmul(o, a_hi, b_hi, start=first, stop=False)
                pe.matmul(o, a_hi, b_lo, start=False, stop=False)
                return pe.matmul(o, a_lo, b_hi, start=False, stop=last)

            def halves(b, kt, width):
                return [w[b % STAGES][:, 0:kt * width].rearrange("p (k c) -> p k c", k=kt) for w in (w_hi, w_lo)]

            def weights(b, kt, width):
                pe.wait_ge(w_lo_in, b + 1)
                return halves(b, kt, width)

            def feature_products(o, b, tiles, a_hi, a_lo, kt=KD, width=256, at=0, ready=None):
                hi, lo = halves(b, kt, width)
                for i in range(tiles):
                    c = slice(at + i * P, at + (i + 1) * P)
                    for k in range(kt):
                        if ready and i == 0:
                            ready(k)
                        mm = product(o[:, i * SEQ:(i + 1) * SEQ], hi[:, k, c], lo[:, k, c],
                                     a_hi[:, k, :], a_lo[:, k, :], k == 0, k == kt - 1)
                return mm

            def feature_block(key, b, tiles, a_hi, a_lo, kt=KD, width=256, bank=None, at=0, last=True, ready=None):
                pe.wait_ge(w_lo_in, b + 1)
                o = claim(key, b % 3 if bank is None else bank, b if last else None)
                mm = feature_products(o, b, tiles, a_hi, a_lo, kt, width, at, ready)
                if last:
                    mm.then_inc(block_done, 1)
                else:
                    ends(mm, key)

            def token_block(key, b, width, a_hi, a_lo, kt=KD, stride=256, bank=None, ready=None):
                hi, lo = weights(b, kt, width)
                o = claim(key, b % 3 if bank is None else bank, b)
                for t in range(TOK):
                    c = slice(t * P, (t + 1) * P)
                    for k in range(kt):
                        if ready and t == 0:
                            ready(k)
                        mm = product(o[:, t * stride:t * stride + width], a_hi[:, k, c], a_lo[:, k, c],
                                     hi[:, k, :], lo[:, k, :], k == 0, k == kt - 1)
                mm.then_inc(block_done, 1)

            def turn(o, src):
                return pe.transpose(o, src, ident)

            def norm_turn(n, src, at=(3, 4, 5, 6)):
                pe.wait_ge(S("xn_ready"), 2 * n + 2)
                for kp in range(KD // 2):
                    o = claim(f"norm{n}.{kp}", at[kp])
                    for kk in range(2):
                        for t in range(TOK):
                            k = 2 * kp + kk
                            mm = turn(o[:, kk * SEQ + t * P:kk * SEQ + (t + 1) * P], src[:, t, k * P:(k + 1) * P])
                    ends(mm, f"norm{n}.{kp}")

            def norm_done(n):
                def ready(k):
                    if k % 2 == 0:
                        wait_read(pe, f"norm{n}.{k // 2}")
                return ready

            def ffn_part(n, norm):
                f = ffn[n]

                def up_block(j, turn=None):
                    b = up_at(n, j)
                    if turn is None:
                        feature_block(f"up{n}.{j}", b, 2, hT_hi, hT_lo, ready=None if j else norm_done(norm))
                        return
                    pe.wait_ge(w_lo_in, b + 1 + TURN * turn)
                    o = claim_turns([f"up{n}.{j + 2 * i}" for i in range(PAIR_TURNS)], b % 3, b, turn)
                    feature_products(o, b, 2, hT_hi, hT_lo).then_inc(block_done, 1)

                def down_block(c, turn=0):
                    b = down_at(n, c)
                    pe.wait_ge(w_lo_in, b + 1 + TURN * turn)
                    hi, lo = halves(b, 2, D)
                    pe.wait_ge(S("ffn_lo"), FF_TILES * (n - 1) + 2 * c + 2 + 2 * turn)
                    for k in range(2):
                        for i in range(4):
                            t, h = slice(i // 2 * P, (i // 2 + 1) * P), slice(i % 2 * 512, (i % 2 + 1) * 512)
                            mm = product(o[i][:], f["hi"][:, k, t], f["lo"][:, k, t], hi[:, k, h], lo[:, k, h],
                                         c == 0 and k == 0, c == PAIRS - 1 and k == 1)
                    mm.then_inc(block_done, 1)

                for j in range(3):
                    if n == 1 and j < 2:
                        pe.wait_ge(S("first_lo"), j + 1)
                    up_block(j)
                o = [claim(f"down{n}.{i}", 3 + i, down_at(n, PAIRS - 1)) for i in range(4)]
                down_block(0)
                up_block(3)
                with pe.Fori(0, PAIR_TURNS) as turn:
                    up_block(4, turn)
                    down_block(1, turn)
                    up_block(5, turn)
                if n == 1:
                    norm_turn(1, mem_xn, (7, 0, 1, 2))
                else:
                    filter_spectrum(3, 7)
                down_block(PAIRS - 1)

            pe.wait_ge(S("square_in"), 16)
            norm_turn(0, ffn[1]["xn"])
            ffn_part(1, 0)

            for i in range(8):
                if i < 4:
                    feature_block(f"kv{i}", FIRST["xa_kv"] + i, 2, mem_hi, mem_lo, ready=None if i else norm_done(1))
                else:
                    token_block(f"kv{i}", FIRST["xa_kv"] + i, 256, mem_hi, mem_lo)
                if i == 4:
                    norm_turn(2, mix_xn)

            pe.wait_ge(w_lo_in, FIRST["dt"] + 1)
            hi, lo = halves(FIRST["dt"], KD, SSD_HEADS)
            o, ready = claim("dt", FIRST["dt"] % 3, FIRST["dt"]), norm_done(2)
            for k in range(KD):
                ready(k)
                mm = product(o[0:SSD_HEADS, 0:SEQ], hi[:, k, :], lo[:, k, :], hT_hi[:, k, :], hT_lo[:, k, :], k == 0, k == KD - 1)
            mm.then_inc(block_done, 1)

            def dt_turn():
                wait_read(pe, "dt")
                o = claim("dtT", 5)
                for t in range(TOK):
                    mm = pe.transpose(o[:, t * SSD_HEADS:(t + 1) * SSD_HEADS], ssd_dtF[:, t * P:(t + 1) * P],
                                      ident[0:SSD_HEADS, 0:SSD_HEADS])
                ends(mm, "dtT")

            xbc, qkv, zb, gb = FIRST["xbc"], FIRST["qkv"], FIRST["z"], FIRST["gate"]

            def xbc_turn(i):
                pe.wait_ge(S("xbc_silu"), i + 1)
                o = claim(f"xT{i}", 3 + i % 2)
                for c in range(2):
                    if i < 8:
                        for t in range(TOK):
                            mm = turn(o[:, t * 256 + c * P:t * 256 + (c + 1) * P], ssd_xF[:, i % 2, c, t * P:(t + 1) * P])
                    else:
                        mm = turn(o[:, c * P:(c + 1) * P], ssd_bF[:, 2 * (i - 8) + c, 0:P])
                ends(mm, f"xT{i}")

            for i in range(12):
                feature_block(f"xbc{i}", xbc + i, 2, hT_hi, hT_lo)
                if i == 0:
                    dt_turn()
                if 1 <= i <= 10:
                    xbc_turn(i - 1)

            def ssd_sums():
                pe.wait_ge(S("ssd_A"), 2)
                o = claim("sums", 3)
                pe.matmul(o[:, 0:SSD_HEADS], upper, ssd_A[:, 1, :], start=True, stop=True)
                ends(pe.matmul(o[:, SSD_HEADS:2 * SSD_HEADS], strict, ssd_A[:, 0, :], start=True, stop=True), "sums")

            def ssd_unit(u):
                c, g = divmod(u, SSD_GROUPS)
                o = claim(f"cb{u}", 3)
                ends(pe.matmul(o[:, 0:P], ssd_bF[:, g, c * P:(c + 1) * P], ssd_cF[:, g, c * P:(c + 1) * P],
                               start=True, stop=True), f"cb{u}")
                for q in range(2):
                    pe.wait_ge(S("ssd_uA"), 2 * u + q + 1)
                    o = claim(f"seg{u}.{q}", 4 + q)
                    pe.matmul(o[:], strict_r[:], ssd_uA_hi[:, q, :], start=True, stop=False)
                    ends(pe.matmul(o[:], strict_r[:], ssd_uA_lo[:, q, :], start=False, stop=True), f"seg{u}.{q}")
                if c == 0:
                    pe.wait_ge(S("ssd_xdd"), 1)
                    o = claim(f"state{g}", 6)
                    ends(pe.matmul(o[:], ssd_bT[:, g, :], ssd_xdd[:, g * 512:(g + 1) * 512], start=True, stop=True),
                         f"state{g}")

            def ssd_diag(u):
                c, g = divmod(u, SSD_GROUPS)
                pe.wait_ge(S("ssd_xdt"), c + 1)
                pe.wait_ge(S("ssd_M"), 2 * u + 2)
                o = claim(f"diag{u}", 7)
                for r in range(8):
                    mm = pe.matmul(o[:, r * 64:(r + 1) * 64], ssd_M[:, r // 4, r % 4 * P:(r % 4 + 1) * P],
                                   ssd_xdt[:, (8 * g + r) * 64:(8 * g + r + 1) * 64], start=True, stop=True)
                ends(mm, f"diag{u}")
                if c:
                    wait_read(pe, f"state{g}")
                    o = claim(f"yoff{g}", 6)
                    ends(pe.matmul(o[:], ssd_cF[:, g, P:2 * P], ssd_state[:, g, :], start=True, stop=True), f"yoff{g}")

            for i in range(12):
                if i < 8:
                    feature_block(f"qkv{i}", qkv + i, 2, hT_hi, hT_lo)
                else:
                    token_block(f"qkv{i}", qkv + i, 256, hT_hi, hT_lo)
                if i == 0:
                    ssd_sums()
                    for j in range(10):
                        wait_read(pe, f"xT{j}")
                if 1 <= i <= 8:
                    ssd_unit(i - 1)
                if 2 <= i <= 9:
                    ssd_diag(i - 2)

            def da_scores(h):
                for j in range(2):
                    o = claim(f"das{h}.{j}", 3 + j)
                    r = slice(j * DA_DIM, (j + 1) * DA_DIM)
                    pe.matmul(o[:, 0:P], da_q[r, h, 0:P], da_k[r, h, 0:P], start=True, stop=True)
                    mm = pe.matmul(o[:, P:P + SEQ], da_q[r, h, P:SEQ], da_k[r, h, :], start=True, stop=True)
                    ends(mm, f"das{h}.{j}")

            def da_turn(h):
                pe.wait_ge(S("da_P"), 2 * h + 2)
                o = claim(f"daT{h}", 5)
                for j in range(3):
                    mm = turn(o[:, j * P:(j + 1) * P], da_P[:, j * P:(j + 1) * P])
                ends(mm, f"daT{h}")

            def da_out(h):
                wait_read(pe, f"daT{h}")
                o = claim(f"dao{h}", 6)
                e = slice(h * P, (h + 1) * P)
                pe.matmul(o[:, 0:P], da_PT[:, 0:P], da_v[:, 0, e], start=True, stop=True)
                pe.matmul(o[:, P:2 * P], da_PT[:, P:2 * P], da_v[:, 0, e], start=True, stop=False)
                ends(pe.matmul(o[:, P:2 * P], da_PT[:, 2 * P:3 * P], da_v[:, 1, e], start=False, stop=True), f"dao{h}")

            def y_turn(kp):
                o = claim(f"yT{kp}", (3, 7, 4, 3, 7, 7, 7, 4)[kp])
                for i in range(2):
                    for t in range(TOK):
                        k = 2 * kp + i
                        mm = turn(o[:, i * SEQ + t * P:i * SEQ + (t + 1) * P], ssd_y[:, t, k * P:(k + 1) * P])
                ends(mm, f"yT{kp}")

            for i in range(16):
                if i < 8:
                    token_block(f"z{i}", zb + i, 256, hT_hi, hT_lo)
                    if i == 0:
                        for j in range(12):
                            wait_read(pe, f"qkv{j}")
                else:
                    feature_block(f"gate{i - 8}", gb + i - 8, 2, hT_hi, hT_lo)
                if i >= 13:
                    if i == 13:
                        pe.wait_ge(S("ssd_yn"), 8)
                    y_turn(i - 9)
                if i % 2 == 0:
                    if i:
                        da_turn(i // 2 - 1)
                    da_scores(i // 2)
                elif i > 1:
                    da_out(i // 2 - 1)
            da_turn(DA_HEADS - 1)
            y_turn(7)
            y_turn(0)
            y_turn(1)
            da_out(DA_HEADS - 1)
            y_turn(2)
            y_turn(3)
            y_order = [*range(8, 16), *range(8)]

            def ssd_block(i):
                b = FIRST["ssd_out"] + i
                hi, lo = weights(b, 16, P)
                o = claim(f"ssd{i}", b % 3, b)
                for n, k in enumerate(y_order):
                    if i == 0 and k % 2 == 0:
                        wait_read(pe, f"yT{k // 2}")
                    c_hi, c_lo = (hT_hi, hT_lo) if k < 8 else (y2_hi, y2_lo)
                    mm = product(o[:, 0:SEQ], hi[:, k, :], lo[:, k, :], c_hi[:, k % 8, :], c_lo[:, k % 8, :], n == 0, n == 15)
                mm.then_inc(block_done, 1)

            for i in range(8):
                ssd_block(i)
                if i == 4:
                    pe.wait_ge(S("da_on"), 2)
                    for hp in range(4):
                        o = claim(f"oT{hp}", 3 + hp)
                        for j in range(2):
                            for t in range(TOK):
                                mm = turn(o[:, j * SEQ + t * P:j * SEQ + (t + 1) * P], da_o[:, 2 * hp + j, t, :])
                        ends(mm, f"oT{hp}")
            for hp in range(4):
                wait_read(pe, f"oT{hp}")
            def filter_hidden(i):
                o = claim(f"hid{i}", 7)
                if i == 0:
                    pe.wait_ge(S("filter_in"), 4 * 16)
                    mm = pe.matmul(o[0:FILTER_HIDDEN, 0:SEQ], w_f12[0:FILTER_EMB, 0, :], emb[:, :], start=True, stop=True)
                else:
                    pe.wait_ge(S("hid_sin"), 1)
                    mm = pe.matmul(o[0:FILTER_HIDDEN, 0:SEQ], w_f12[:, 1, :], hid[:, 1, :], start=True, stop=True)
                ends(mm, f"hid{i}")

            def filter_taps(i):
                t, c = divmod(i, 4)
                if i == 0:
                    pe.wait_ge(S("hid_sin"), 2)
                o = claim(f"taps{i}", 3 + i % 4)
                ends(pe.matmul(o[:], hid[:, 3, t * P:(t + 1) * P], w_f3[:, c * HY:(c + 1) * HY], start=True, stop=True),
                     f"taps{i}")

            def filter_spectrum(i, bank):
                n, f = divmod(i, 4)
                if i == 0:
                    pe.wait_ge(S("kfil_bias"), 2)
                    pe.wait_ge(S("dft_f_in"), 16)
                o = claim(f"spec{i}", bank)
                for way in range(2):
                    for t in range(TOK):
                        mm = pe.matmul(o[:], dft_f[:, way, t, f * P:(f + 1) * P],
                                       kfil[:, t, (2 * n + way) * HY:(2 * n + way + 1) * HY],
                                       start=way == 0 and t == 0, stop=way == 1 and t == 1)
                ends(mm, f"spec{i}")

            for i in range(4):
                b = FIRST["attn_out"] + i
                if i < 3:
                    feature_block(f"attn{i}", b, 2, o_hi, o_lo)
                else:
                    feature_block("attn3.0", b, 1, o_hi, o_lo, last=False)
                    feature_block("attn3.1", b, 1, o_hi, o_lo, bank=6, at=P)
                if i == 1:
                    filter_hidden(0)

            def mixed_ready(k):
                if k % 2 == 0 or k == 7:
                    pe.wait_ge(S("mixed_lo"), k // 2 + 1 + (k == 7))

            for i in range(4):
                token_block(f"mix{i}", FIRST["mix_out"] + i, 256, mixed_hi, mixed_lo, ready=None if i else mixed_ready)
                if i == 0:
                    filter_hidden(1)
            for i in range(8):
                filter_taps(i)

            norm_turn(3, xa_xn)
            for i in range(8):
                wait_read(pe, f"kv{i}")

            def xa_scores(h):
                wait_read(pe, f"xaq{h}")
                o = claim(f"xas{h}", 3 + h % 2)
                for q in range(2):
                    for kk in range(2):
                        k = 2 * h + kk
                        mm = pe.matmul(o[:, q * SEQ:(q + 1) * SEQ], xa_q[:, k, q * P:(q + 1) * P], xa_k[:, k, :],
                                       start=kk == 0, stop=kk == 1)
                ends(mm, f"xas{h}")

            def xa_turn(h):
                pe.wait_ge(S("xa_P"), 2 * h + 2)
                o = claim(f"xaT{h}", 5)
                for kb in range(2):
                    for q in range(2):
                        mm = turn(o[:, kb * SEQ + q * P:kb * SEQ + (q + 1) * P], xa_p[:, h % 2, q, kb * P:(kb + 1) * P])
                ends(mm, f"xaT{h}")

            def xa_out(h):
                wait_read(pe, f"xaT{h}")
                o = claim(f"xao{h}", 6)
                for f in range(2):
                    for kb in range(2):
                        mm = pe.matmul(o[:, f * SEQ:(f + 1) * SEQ], xa_v[:, kb, (2 * h + f) * P:(2 * h + f + 1) * P],
                                       xa_PT[:, kb, :], start=kb == 0, stop=kb == 1)
                ends(mm, f"xao{h}")

            for i in range(XA_HEADS):
                feature_block(f"xaq{i}", FIRST["xa_q"] + i, 2, hT_hi, hT_lo, ready=None if i else norm_done(3))
                if i >= 3:
                    xa_out(i - 3)
                if i >= 2:
                    xa_turn(i - 2)
                if i >= 1:
                    xa_scores(i - 1)
            xa_scores(3)
            xa_out(1)
            xa_turn(2)

            def xo_ready(k):
                if k == 4:
                    xa_out(2)
                    xa_turn(3)
                elif k == 6:
                    xa_out(3)
                if k % 2 == 0:
                    wait_read(pe, f"xao{k // 2}")

            for i in range(4):
                token_block(f"xo{i}", FIRST["xa_o"] + i, 256, xa_hi, xa_lo, ready=None if i else xo_ready)

            for i in range(3):
                filter_spectrum(i, (3, 4, 5)[i])
            norm_turn(4, ffn[2]["xn"])
            ffn_part(2, 4)
            for i in range(4):
                filter_spectrum(4 + i, (0, 1, 2, 7)[i])

            norm_turn(5, sec_xn)
            token_block("cq0", FIRST["cq"], 256, hT_hi, hT_lo, ready=norm_done(5))
            token_block("ckv", FIRST["ckv"], 256, hT_hi, hT_lo)
            token_block("cq1", FIRST["cq_rope"], P + QK_ROPE, hT_hi, hT_lo)
            for i in range(4):
                feature_block(f"zz{i}", FIRST["z_hy"] + i, 2, hT_hi, hT_lo)
                if i == 2:
                    pe.wait_ge(S("c_ready"), 4)
                    for k in range(5):
                        if k % 2 == 0:
                            o = claim(f"cT{k // 2}", 3 + k // 2)
                        for t in range(TOK):
                            src = cq[:, t, k * P:(k + 1) * P] if k < 3 else ckv[:, t, (k - 3) * P:(k - 2) * P]
                            mm = turn(o[:, k % 2 * SEQ + t * P:k % 2 * SEQ + (t + 1) * P], src)
                        if k % 2 or k == 4:
                            ends(mm, f"cT{k // 2}")
            for k in range(3):
                wait_read(pe, f"cT{k}")

            def token_wide(key, b, kt, width, a_hi, a_lo, at):
                hi, lo = weights(b, kt, width)
                for t in range(TOK):
                    for h in range(0, width, 512):
                        n = min(512, width - h)
                        o = claim(f"{key}.{t}.{h}", at[t * (width // 512 or 1) + h // 512], b)
                        for k in range(kt):
                            mm = product(o[:, 0:n], a_hi[:, k, t * P:(t + 1) * P], a_lo[:, k, t * P:(t + 1) * P],
                                         hi[:, k, h:h + n], lo[:, k, h:h + n], k == 0, k == kt - 1)
                mm.then_inc(block_done, 1)

            uq, ukv = FIRST["uq"], FIRST["ukv"]
            token_wide("uq0", uq, 3, 512, cq_hi, cq_lo, (6, 7))
            token_wide("uq1", uq + 1, 3, 256, cq_hi, cq_lo, (3, 4))
            token_wide("ukv", ukv, 2, 1024, ckv_hi, ckv_lo, (5, 6, 7, 3))

            def hyena_turn(n):
                if n == 0:
                    wait_read(pe, "hy0")
                    wait_read(pe, "hy1")
                for t in range(TOK):
                    o = claim(f"uT{n}.{t}", 6 + t)
                    for c in range(HY_TILES):
                        if n and c % 2 == 0:
                            wait_read(pe, f"yt0.{c // 2}")
                        mm = turn(o[:, c * P:(c + 1) * P], hyF[:, c, t * P:(t + 1) * P])
                    ends(mm, f"uT{n}.{t}")

            def hyena_ahead(n, f):
                if n == 0 and f == 0:
                    pe.wait_ge(S("dft_ab_in"), 32)
                for t in range(TOK):
                    wait_read(pe, f"uT{n}.{t}")
                for i in (f, f + 2):
                    o = claim(f"uf{n}.{i}", 6 + i // 2)
                    for t in range(TOK):
                        mm = pe.matmul(o[:], dft_a[:, t, i * P:(i + 1) * P], uT[:, t, :], start=t == 0, stop=t == 1)
                    ends(mm, f"uf{n}.{i}")

            def hyena_back(n):
                pe.wait_ge(S("hy_yf"), 4 * (n + 1))
                for cp in range(2):
                    o = claim(f"yt{n}.{cp}", 6 + cp)
                    for i in range(2):
                        c = 2 * cp + i
                        for f in range(4):
                            mm = pe.matmul(o[:, i * SEQ:(i + 1) * SEQ], spec[:, n, f, c * P:(c + 1) * P], dft_b[:, f, :],
                                           start=f == 0, stop=f == 3)
                    ends(mm, f"yt{n}.{cp}")

            def head_turn(s):
                pe.wait_ge(S("mla_qk"), s + 1)
                for hp in range(4):
                    o = claim(f"mT{s}.{hp}", (3, 4, 5, 7)[hp])
                    for i in range(2):
                        for t in range(TOK):
                            mm = turn(o[0:QK_DIM, i * SEQ + t * P:i * SEQ + (t + 1) * P], mq[:, s, t, 2 * hp + i, :])
                    ends(mm, f"mT{s}.{hp}")

            def mla_scores(h):
                for s in range(2):
                    wait_read(pe, f"mT{s}.{h // 2}")
                o = claim(f"ms{h}", 3)
                for q in range(2):
                    mm = pe.matmul(o[:, q * SEQ:(q + 1) * SEQ], mqT[:, 0, h, q * P:(q + 1) * P], mqT[:, 1, h, :],
                                   start=True, stop=True)
                ends(mm, f"ms{h}")

            def mla_turn(h):
                pe.wait_ge(S("m_P"), 2 * h + 2)
                o = claim(f"mPT{h}", 4)
                for kb in range(2):
                    for q in range(2):
                        mm = turn(o[:, kb * SEQ + q * P:kb * SEQ + (q + 1) * P], m_p[:, h % 2, q, kb * P:(kb + 1) * P])
                ends(mm, f"mPT{h}")

            def mla_out(h):
                wait_read(pe, f"mPT{h}")
                if h % 2 == 0:
                    claim(f"mo{h // 2}", 5)
                r = slice(h % 2 * V_DIM, (h % 2 + 1) * V_DIM)
                for kb in range(2):
                    mm = pe.matmul(banks[5][r, 0:SEQ], mv[:, kb, h, :], m_PT[:, kb, :], start=kb == 0, stop=kb == 1)
                if h % 2:
                    ends(mm, f"mo{h // 2}")

            def wide_out(key, b, hi, lo, at, ready=None):
                feature_block(f"{key}.0", b, 2, hi, lo, HY_TILES, 512, bank=at[0], last=False, ready=ready)
                feature_block(f"{key}.1", b, 2, hi, lo, HY_TILES, 512, bank=at[1], at=256)

            for i in range(6):
                if i == 5:
                    head_turn(0)
                feature_block(f"hy{i}", FIRST["hy"] + i, 2, hT_hi, hT_lo)
            hyena_turn(0)
            for i in range(MLA_HEADS + 2):
                if i < 8:
                    feature_block(f"gg{i}", FIRST["gate2"] + i, 2, hT_hi, hT_lo)
                if i == 0:
                    head_turn(1)
                    hyena_ahead(0, 0)
                if i >= 2:
                    mla_out(i - 2)
                if i == 8:
                    pe.wait_ge(S("hy_lo"), 4)
                if i >= 8:
                    wide_out(f"hyo{i - 8}", FIRST["hy_out"] + i - 8, hy_hi, hy_lo, ((0, 1), (2, 6))[i - 8])
                if 1 <= i <= MLA_HEADS:
                    mla_turn(i - 1)
                if i < MLA_HEADS:
                    mla_scores(i)
                if i == 1:
                    hyena_ahead(0, 1)
                elif i in (2, 6):
                    hyena_back(i // 4)
                elif i == 3:
                    hyena_turn(1)
                elif i in (4, 5):
                    hyena_ahead(1, i - 4)

            def at_ready(k):
                pe.wait_ge(S("at_lo"), k + 1)

            for i in range(2):
                wide_out(f"ato{i}", FIRST["at_out"] + i, at_hi, at_lo, ((7, 3), (4, 5))[i], None if i else at_ready)

            def fin_ready(k):
                if k % 2 == 0:
                    pe.wait_ge(S("fin_lo"), k // 2 + 1)

            for i in range(4):
                token_block(f"out{i}", FIRST["out"] + i, 256, hT_hi, hT_lo, bank=(0, 1, 2, 6)[i], ready=None if i else fin_ready)

        @block.scalar
        def _(act):
            rounded = [0]
            step = [0]

            def link(ins):
                step[0] += 1
                ins.then_inc(S("scalar_step"), 1)
                act.wait_ge(S("scalar_step"), step[0])

            def round_block(b, turn=0):
                act.wait_ge(w_landed[b % RING], 16 * (b // RING + 1 + turn))
                if b >= STAGES:
                    act.wait_ge(block_done, b - STAGES + 1 + TURN * turn)
                act.activation(w_hi[b % STAGES][:], w_raw[b % RING][:], ACT.Copy).then_inc(w_hi_in, 1)

            def round_to(n):
                for b in range(rounded[0], min(n, NBLOCK)):
                    round_block(b)
                rounded[0] = max(rounded[0], min(n, NBLOCK))

            def after(b):
                round_to(b + 1 + STAGES)

            def copy(key, dst, src):
                read(act.activation(dst, src, ACT.Copy), key)

            def two(bank, n=2):
                return bank[:].rearrange("p (t c) -> p t c", t=n)

            def norm_squares(src, junk):
                act.activation(junk[:, 0, :], src[:, 0, :], ACT.Square, accum_out=ssq[:, 0:1]).then_inc(S("norm_ssq"), 1)

            def norm_high(n, gain, hi):
                for kp in range(KD // 2):
                    o = full(act, f"norm{n}.{kp}")
                    for kk in range(2):
                        k = 2 * kp + kk
                        ins = act.activation(hi[:, k, :], o[:, kk * SEQ:(kk + 1) * SEQ], ACT.Copy, scale=col(gain, k))
                    ins.then_inc(S("norm_hi"), 1)

            def post_gain(i, name):
                if i:
                    act.wait_ge(S("x_ready"), X_READY[i - 1] - 1)
                act.dma_start(post_g[:], a[name].partition_broadcast(P)[:, 0, :]).then_inc(S("post_g_in"), 16)

            def ffn_part(n):
                f = ffn[n]

                def gate(j, turn=0):
                    o = full(act, f"up{n}.{j}", turn)
                    if j >= 2:
                        wait_read(act, f"up{n}.{j - 2}", turn)
                    act.activation(f["gate"][:, j % 2, :], o[:, 0:SEQ], ACT.Silu).then_inc(S("ffn_gate"), 1)

                def high(j, turn=0):
                    if j >= 2:
                        act.wait_ge(block_done, down_at(n, j // 2 - 1) + 1 + TURN * turn)
                    wait_read(act, f"up{n}.{j}", turn)
                    act.activation(f["hi"][:, j % 2, :], f["act"][:, j % 2, :], ACT.Copy).then_inc(S("ffn_hi"), 1)

                for j in range(2):
                    gate(j)
                    after(up_at(n, j))
                    high(j)
                gate(2)
                after(up_at(n, 2))
                after(down_at(n, 0))
                high(2)
                gate(3)
                after(up_at(n, 3))
                high(3)
                if n == 1:
                    act.wait_ge(S("mem_in"), 16)
                    norm_squares(mem_xn, mem_junk)
                with act.Fori(0, PAIR_TURNS) as turn:
                    b = up_at(n, 4) + STAGES
                    gate(4, turn)
                    round_block(b, turn)
                    round_block(b + 1, turn)
                    high(4, turn)
                    gate(5, turn)
                    round_block(b + 2, turn)
                    high(5, turn)
                rounded[0] += TURN * PAIR_TURNS
                if n == 1:
                    norm_high(1, "mem_norm_g", mem_hi)
                else:
                    spectrum(3)
                after(down_at(n, PAIRS - 1))
                for i in range(4):
                    o = full(act, f"down{n}.{i}")
                    if i >= 2:
                        wait_read(act, f"down{n}.{i}")
                    if i:
                        act.wait_ge(S("post_ssq"), (0 if n == 1 else POST_SSQ[2]) + i)
                    act.activation(f["junk"][:], o[:], ACT.Square, accum_out=post_ssq[:, i // 2, i % 2:i % 2 + 1])\
                       .then_inc(S("post_ssq"), 1)

            def out_part(stage, key, i_post, between=None):
                for i in range(4):
                    o = full(act, f"{key}{i}")
                    act.wait_ge(S("post_ssq"), POST_SSQ[i_post - 1] + i)
                    for t in range(TOK):
                        ins = act.activation(post_tmp[:, t * 256:(t + 1) * 256], o[:, t * 256:(t + 1) * 256], ACT.Square,
                                             accum_out=post_ssq[:, t, i:i + 1])
                    ins.then_inc(S("post_ssq"), 1)
                    after(FIRST[stage] + i)
                    if between:
                        between(i)

            act.dma_start(fcols[:], a["fcols"]).then_inc(S("rows_in"), 16)
            act.dma_start(rows[:], a["rows"].partition_broadcast(P)[:, 0, :]).then_inc(S("rows_in"), 16)
            post_gain(0, POST[0])

            act.wait_ge(S("x_in"), 16)
            norm_squares(x, ffn[1]["xn"])
            round_to(1)
            act.wait_ge(S("cols_in"), 16)
            norm_high(0, "ffn1_pre_g", hT_hi)
            round_to(STAGES)
            act.dma_start(mem_xn[:], a["mem"].rearrange("(t p) d -> p t d", p=P)).then_inc(S("mem_in"), 16)
            ffn_part(1)

            for i in range(8):
                if i == 2:
                    act.wait_ge(S("x_ready"), X_READY[0] - 1)
                    norm_squares(x, mix_xn)
                o = full(act, f"kv{i}")
                if i < 4:
                    copy(f"kv{i}", xa_k[:, 2 * i:2 * i + 2, :], two(o))
                else:
                    copy(f"kv{i}", xa_v[:, :, (i - 4) * 256:(i - 3) * 256], two(o))
                after(FIRST["xa_kv"] + i)
                if i == 4:
                    norm_high(2, "mix_pre_g", hT_hi)

            o = full(act, "dt")
            copy("dt", ssd_dtF[:], o[0:SSD_HEADS, 0:SEQ])
            act.activation(strict_r[:], strict, ACT.Copy).then_inc(S("strict_r"), 1)
            after(FIRST["dt"])
            act.wait_ge(S("rows_in"), 32)
            act.activation(ssd_eA[:], row("ssd_A_log"), ACT.Exp).then_inc(S("dt_exp"), 1)

            def time_step(part):
                if part == 0:
                    act.wait_ge(S("dt_abs"), 1)
                    act.activation(ssd_dtt[:, 2], ssd_dtt[:, 1], ACT.Exp).then_inc(S("dt_exp"), 1)
                elif part == 1:
                    act.wait_ge(S("dt_one"), 1)
                    act.activation(ssd_dtt[:, 4], ssd_dtt[:, 3], ACT.Ln).then_inc(S("dt_ln"), 1)
                else:
                    act.wait_ge(S("ssd_A"), 2)
                    act.activation(ssd_A_hi[:], ssd_A[:], ACT.Copy).then_inc(S("ssd_A_hi"), 1)

            for i in range(12):
                wait_read(act, f"xbc{i}")
                dst = ssd_xF[:, i % 2] if i < 8 else (ssd_bF if i < 10 else ssd_cF)[:, 2 * (i % 2):2 * (i % 2) + 2]
                act.activation(dst, ssd_conv[:, i % 2], ACT.Silu).then_inc(S("xbc_silu"), 1)
                after(FIRST["xbc"] + i)
                if i in (2, 4, 6):
                    time_step(i // 2 - 1)
                if 1 <= i <= 10:
                    o = full(act, f"xT{i - 1}")
                    if i <= 8:
                        copy(f"xT{i - 1}", ssd_y[:, :, (i - 1) * 256:i * 256], two(o))
                    else:
                        copy(f"xT{i - 1}", ssd_bT[:, 2 * (i - 9):2 * (i - 9) + 2, :], two(o)[:, 0, :].rearrange("p (c l) -> p c l", c=2))

            for i in range(12):
                o = full(act, f"qkv{i}")
                h = i % 4
                if i < 8:
                    copy(f"qkv{i}", (da_q if i < 4 else da_k)[:, 2 * h:2 * h + 2, :], two(o))
                else:
                    copy(f"qkv{i}", da_v[:, :, h * 256:(h + 1) * 256], two(o))
                after(FIRST["qkv"] + i)
                if i == 0:
                    o = full(act, "sums")
                    act.activation(ssd_ecs[:], o[:, 0:SSD_HEADS], ACT.Exp).then_inc(S("ssd_ecs"), 1)
                    read(act.activation(ssd_decay[:], o[:, SSD_HEADS:2 * SSD_HEADS], ACT.Exp), "sums")
                if 1 <= i <= 8:
                    u = i - 1
                    for q in range(2):
                        o = full(act, f"seg{u}.{q}")
                        if u:
                            act.wait_ge(S("ssd_M"), 2 * (u - 1) + q + 1)
                        read(act.activation(ssd_L[:, q, :], o[:], ACT.Exp), f"seg{u}.{q}")
                    if u < SSD_GROUPS:
                        o = full(act, f"state{u}")
                        copy(f"state{u}", ssd_state[:, u, :], o[:])

            post_gain(1, POST[1])

            act.wait_ge(S("lam_dot"), 2)
            act.activation(da_lam[:, 2:4], da_lam[:, 0:2], ACT.Exp).then_inc(S("lam_exp"), 1)

            def da_exps(h):
                act.wait_ge(S("da_max"), h + 1)
                if h:
                    act.wait_ge(S("da_P"), 2 * h)
                for j in range(2):
                    for q in range(2):
                        c = slice(0, P) if q == 0 else slice(P, P + SEQ)
                        ins = act.activation(da_p[:, j, c], da_s[:, j, c], ACT.Exp, bias=da_st[:, 1, 2 * j + q:2 * j + q + 1],
                                             scale=DA_DIM ** -0.5, accum_out=da_st[:, 2, 2 * j + q:2 * j + q + 1])
                        ins.then_inc(S("da_exp"), 1)

            def da_rows(h):
                o = full(act, f"dao{h}")
                for t in range(TOK):
                    if h or t:
                        act.wait_ge(S("da_ssq"), TOK * h + t)
                    act.activation(da_junk[:], o[:, t * P:(t + 1) * P], ACT.Square, accum_out=da_ssq[:, t, h:h + 1])\
                       .then_inc(S("da_ssq"), 1)
                copy(f"dao{h}", da_o[:, h, :, :], o[:, 0:SEQ].rearrange("p (t c) -> p t c", t=TOK))

            def da_columns(h):
                o = full(act, f"daT{h}")
                copy(f"daT{h}", da_PT[:], o[:, 0:384])

            def y_columns(k):
                return (hT_hi, hT_lo) if k < 8 else (y2_hi, y2_lo)

            def y_high(kp):
                o = full(act, f"yT{kp}")
                for i in range(2):
                    k = 2 * kp + i
                    ins = act.activation(y_columns(k)[0][:, k % 8, :], o[:, i * SEQ:(i + 1) * SEQ], ACT.Copy,
                                         scale=col("ssd_norm_g", k))
                ins.then_inc(S("y_hi"), 1)

            for i in range(16):
                if i >= 13:
                    y_high(i - 9)
                if i % 2 == 0:
                    if i:
                        da_columns(i // 2 - 1)
                    da_exps(i // 2)
                elif i > 1:
                    da_rows(i // 2 - 1)
                if i < 15:
                    after(FIRST["z"] + i)
                if i == 7:
                    for j in range(8):
                        wait_read(act, f"z{j}")
                    for t in range(TOK):
                        act.activation(ssd_z[:, t, :], ssd_z[:, t, :], ACT.Silu).then_inc(S("z_silu"), 1)
                if i in (9, 10):
                    t = i - 9
                    act.wait_ge(S("ssd_yg"), t + 1)
                    for g in range(SSD_GROUPS):
                        act.activation(ssd_z[:, t, g * 512:(g + 1) * 512], ssd_y[:, t, g * 512:(g + 1) * 512], ACT.Square,
                                       accum_out=ssd_ssq[:, t, g:g + 1]).then_inc(S("ssd_ssq"), 1)
            da_columns(DA_HEADS - 1)
            y_high(7)
            y_high(0)
            y_high(1)
            after(FIRST["z"] + 15)
            y_high(2)
            y_high(3)
            da_rows(DA_HEADS - 1)
            for i in range(8):
                wait_read(act, f"gate{i}")
            for c in (1, 0):
                act.activation(mix_gate[:, 8 * c:8 * c + 8, :], mix_gate[:, 8 * c:8 * c + 8, :], ACT.Sigmoid)\
                   .then_inc(S("mix_gate"), 1)
            act.wait_ge(S("sub_g"), 1)
            for i in range(8):
                after(FIRST["ssd_out"] + i)
                if i == 4:
                    for hp in range(4):
                        o = full(act, f"oT{hp}")
                        act.activation(o_hi[:, 2 * hp:2 * hp + 2, :], two(o), ACT.Copy, scale=sub_g[:, 0:1]).then_inc(S("o_hi"), 1)
            act.dma_start(w_f12[0:FILTER_EMB, 0, :], a["w_f1_2"]).then_inc(S("filter_in"), 16)
            act.dma_start(w_f12[:, 1, :], a["w_f2_2"]).then_inc(S("filter_in"), 16)
            act.dma_start(emb[:], a["c_emb"]).then_inc(S("filter_in"), 16)
            act.dma_start(w_f3[:], a["w_f3_2"]).then_inc(S("filter_in"), 16)

            def hidden_sin(i):
                act.wait_ge(S("hid_arg"), i + 1)
                act.activation(hid[:, 2 * i + 1, :], hid[:, 2 * i, :], ACT.Sin).then_inc(S("hid_sin"), 1)

            for i, c in enumerate(MIXED):
                act.wait_ge(S("mixed"), i + 1)
                act.activation(mixed_hi[:, c, :], mg[:, c, :], ACT.Copy).then_inc(S("mixed_hi"), 1)
                if i < 3:
                    after(FIRST["attn_out"] + i)
                if i == 2:
                    hidden_sin(0)
            after(FIRST["attn_out"] + 3)
            act.dma_start(decay[:], a["c_decay"]).then_inc(S("filter_in"), 16)
            act.dma_start(bias_row[:], a["hy_bias"].unsqueeze(0)).then_inc(S("bias_in"), 16)

            def mix_between(i):
                if i == 1:
                    hidden_sin(1)

            out_part("mix_out", "mix", 1, mix_between)

            def taps(i):
                t, c = divmod(i, 4)
                o = full(act, f"taps{i}")
                copy(f"taps{i}", kfil[:, t, c * HY:(c + 1) * HY], o[:])

            def spectrum(i):
                n, f = divmod(i, 4)
                o = full(act, f"spec{i}")
                copy(f"spec{i}", spec[:, n, f, :], o[:])

            for i in range(5):
                taps(i)
            post_gain(2, POST[2])
            norm_squares(x, xa_xn)
            for i in range(5, 8):
                taps(i)
            norm_high(3, "xa_pre_g", hT_hi)

            def xa_exps(h):
                act.wait_ge(S("xa_max"), h + 1)
                o = banks[fills[f"xas{h}"][0]]
                if h >= 2:
                    full(act, f"xaT{h - 2}")
                for q in range(2):
                    ins = act.activation(xa_p[:, h % 2, q, :], o[:, q * SEQ:(q + 1) * SEQ], ACT.Exp, bias=xa_st[:, 1, q:q + 1],
                                         scale=XA_DIM ** -0.5, accum_out=xa_st[:, 2, q:q + 1])
                read(ins, f"xas{h}")

            def xa_columns(h):
                o = full(act, f"xaT{h}")
                copy(f"xaT{h}", xa_PT[:], two(o))

            def xa_high(h):
                o = full(act, f"xao{h}")
                act.activation(xa_hi[:, 2 * h:2 * h + 2, :], two(o), ACT.Copy).then_inc(S("xo_hi"), 1)

            for i in range(XA_HEADS):
                o = full(act, f"xaq{i}")
                copy(f"xaq{i}", xa_q[:, 2 * i:2 * i + 2, :], two(o))
                if i >= 3:
                    xa_high(i - 3)
                if i >= 2:
                    xa_columns(i - 2)
                if i >= 1:
                    xa_exps(i - 1)
                after(FIRST["xa_q"] + i)
            xa_exps(3)
            xa_high(1)
            xa_columns(2)
            xa_high(2)
            xa_columns(3)
            xa_high(3)
            act.dma_start(dft_f[:].rearrange("p w t f -> p (w t f)"), a["c_dft"][:, 0:2048]).then_inc(S("dft_f_in"), 16)
            out_part("xa_o", "xo", 2)

            spectrum(0)
            post_gain(3, POST[3])
            norm_squares(x, ffn[2]["xn"])
            for i in range(1, 3):
                spectrum(i)
            norm_high(4, "ffn2_pre_g", hT_hi)
            ffn_part(2)

            spectrum(4)
            act.wait_ge(S("x_ready"), X_READY[3] - 1)
            norm_squares(x, sec_xn)
            for i in range(5, 8):
                spectrum(i)
            act.dma_start(dft_a[:].rearrange("p t f -> p (t f)"), a["c_dft"][:, 0:1024]).then_inc(S("dft_ab_in"), 16)
            act.dma_start(m_ropeT[:], a["c_rope"]).then_inc(S("rope_in"), 16)
            norm_high(5, "g_norm_2", hT_hi)
            act.dma_start(dft_b[:].rearrange("p f t -> p (f t)"), a["c_dft"][:, 2048:3072]).then_inc(S("dft_ab_in"), 16)

            o = full(act, "cq0")
            copy("cq0", cq[:, :, 0:256], two(o))
            after(FIRST["cq"])
            o = full(act, "ckv")
            copy("ckv", ckv[:], two(o))
            after(FIRST["ckv"])
            o = full(act, "cq1")
            act.activation(cq[:, :, 256:384], two(o)[:, :, 0:P], ACT.Copy).then_inc(S("cq1_in"), 1)
            copy("cq1", k_rope[:], two(o)[:, :, P:P + QK_ROPE])
            for t in range(TOK):
                if t == 0:
                    wait_read(act, "cq0")
                    wait_read(act, "ckv")
                    act.wait_ge(S("cq1_in"), 1)
                else:
                    act.wait_ge(S("c_ssq"), 2)
                act.activation(c_junk[:, 0:Q_LORA], cq[:, t, :], ACT.Square, accum_out=c_ssq[:, 0, t:t + 1]).then_inc(S("c_ssq"), 1)
                act.wait_ge(S("c_ssq"), 2 * t + 1)
                act.activation(c_junk[:, 0:KV_LORA], ckv[:, t, :], ACT.Square, accum_out=c_ssq[:, 1, t:t + 1]).then_inc(S("c_ssq"), 1)
            after(FIRST["cq_rope"])
            for i in range(4):
                o = full(act, f"zz{i}")
                read(act.activation((z_hy if i < 2 else z_at)[:, 2 * (i % 2):2 * (i % 2) + 2, :], two(o), ACT.Silu), f"zz{i}")
                after(FIRST["z_hy"] + i)
                if i == 2:
                    for k in range(5):
                        o = full(act, f"cT{k // 2}")
                        dst = cq_hi[:, k, :] if k < 3 else ckv_hi[:, k - 3, :]
                        g = col("g_cq_2", k) if k < 3 else col("g_ckv_2", k - 3)
                        act.activation(dst, o[:, k % 2 * SEQ:(k % 2 + 1) * SEQ], ACT.Copy, scale=g).then_inc(S("c_hi"), 1)
            for t in range(TOK):
                o = full(act, f"uq0.{t}.0")
                copy(f"uq0.{t}.0", mq_rows[:, 0, t, 0:512], o[:])
            after(FIRST["uq"])
            for t in range(TOK):
                o = full(act, f"uq1.{t}.0")
                copy(f"uq1.{t}.0", mq_rows[:, 0, t, 512:768], o[:, 0:256])
            after(FIRST["uq"] + 1)
            for t in range(TOK):
                for h in range(0, 1024, 512):
                    o = full(act, f"ukv.{t}.{h}")[:].rearrange("p (h c) -> p h c", h=4)
                    heads = slice(h // P, h // P + 4)
                    act.activation(mq[:, 1, t, heads, 0:QK_NOPE], o[:, :, 0:QK_NOPE], ACT.Copy)
                    copy(f"ukv.{t}.{h}", mv[:, t, heads, :], o[:, :, QK_NOPE:])
            after(FIRST["ukv"])

            def centre_tap(i):
                o = full(act, f"hy{i}")
                for c in range(2):
                    ch = 2 * i + c
                    act.activation(hyF[:, ch, :], o[:, c * SEQ:(c + 1) * SEQ], ACT.Identity, scale=col("w_short_2", 3 * ch + 1),
                                   bias=col("b_short_2", ch)).then_inc(S("hy_mid"), 1)

            def hyena_rows(n):
                for t in range(TOK):
                    o = full(act, f"uT{n}.{t}")
                    copy(f"uT{n}.{t}", uT[:, t, :], o[:])

            def head_columns(s):
                for hp in range(4):
                    o = full(act, f"mT{s}.{hp}")
                    copy(f"mT{s}.{hp}", mqT[:, s, 2 * hp:2 * hp + 2, :], o[0:QK_DIM, :].rearrange("p (h c) -> p h c", h=2))

            for i in range(6):
                if i == 5:
                    head_columns(0)
                centre_tap(i)
                after(FIRST["hy"] + i)
            hyena_rows(0)

            def mla_exps(h):
                act.wait_ge(S("m_max"), h + 1)
                o = banks[fills[f"ms{h}"][0]]
                if h >= 2:
                    full(act, f"mPT{h - 2}")
                for q in range(2):
                    ins = act.activation(m_p[:, h % 2, q, :], o[:, q * SEQ:(q + 1) * SEQ], ACT.Exp, bias=m_st[:, 1, q:q + 1],
                                         scale=QK_DIM ** -0.5, accum_out=m_st[:, 2, q:q + 1])
                read(ins, f"ms{h}")

            for i in range(MLA_HEADS + 2):
                if i < 8:
                    o = full(act, f"gg{i}")
                    for c in range(2):
                        ins = act.activation(gate2[:, 2 * i + c, :], o[:, c * SEQ:(c + 1) * SEQ], ACT.Identity,
                                             bias=col("b_gate_2", 2 * i + c))
                    read(ins, f"gg{i}")
                if i == 0:
                    head_columns(1)
                if 1 <= i <= MLA_HEADS:
                    o = full(act, f"mPT{i - 1}")
                    copy(f"mPT{i - 1}", m_PT[:], two(o))
                if i < MLA_HEADS:
                    mla_exps(i)
                if i >= 3 and i % 2:
                    c = (i - 3) // 2
                    wait_read(act, f"mo{c}")
                    act.activation(at_hi[:, c, :], z_at[:, c, :], ACT.Copy).then_inc(S("at_hi"), 1)
                if i == 3:
                    hyena_rows(1)
                if i == 6:
                    for c in range(HY_TILES):
                        wait_read(act, f"yt1.{c // 2}")
                        act.activation(hy_hi[:, c, :], hyF[:, c, :], ACT.Copy).then_inc(S("hy_hi"), 1)
                after(FIRST["gate2"] + i)
                if i >= 8:
                    for j in range(8):
                        wait_read(act, f"gg{j}")
                    c = slice(8 * (i - 8), 8 * (i - 7))
                    act.activation(gate2[:, c, :], gate2[:, c, :], ACT.Sigmoid).then_inc(S("gate2"), 1)
            for i in range(4):
                act.wait_ge(S("fin"), i + 1)
                act.activation(hT_hi[:, 2 * i:2 * i + 2, :], mg2[:, 2 * i:2 * i + 2, :], ACT.Copy).then_inc(S("fin_hi"), 1)
                if i == 0:
                    after(FIRST["at_out"])
            after(NBLOCK - 1)

        @block.vector
        def _(dve):
            step = [0]

            def link(ins):
                step[0] += 1
                ins.then_inc(S("vector_step"), 1)
                dve.wait_ge(S("vector_step"), step[0])

            ts, tt, stt = dve.tensor_scalar, dve.tensor_tensor, dve.scalar_tensor_tensor

            def f32(t):
                return t.bitcast(F32)

            def two(bank, n=2):
                return bank[:].rearrange("p (t c) -> p t c", t=n)

            def inverse_root(dst, sums, n, width, eps):
                v, h, q = (nt[:, i, 0:n] for i in range(3))
                link(ts(v, sums, 1.0 / width, eps, ALU.mult, ALU.add))
                link(ts(dst.bitcast(I32), v.bitcast(I32), -0.5, float(0x5F3759DF), ALU.mult, ALU.add))
                link(tt(h, dst, dst, ALU.mult))
                link(stt(h, h, -0.5, v, ALU.mult, ALU.mult))
                link(stt(dst, h, 1.5, dst, ALU.add, ALU.mult))
                link(tt(h, dst, dst, ALU.mult))
                link(stt(h, h, -1.0, v, ALU.mult, ALU.mult))
                link(ts(q, h, 0.375, 1.25, ALU.mult, ALU.add))
                link(tt(q, q, h, ALU.mult))
                link(stt(dst, q, 1.875, dst, ALU.add, ALU.mult))

            def square_sum(junk, src, acc):
                return dve.tensor_tensor_reduce(junk, src, src, 1.0, 0.0, ALU.mult, ALU.add, acc)

            def norm_rows(n, src, dst, junk):
                link(square_sum(junk[:, 1, :], src[:, 1, :], ssq[:, 1:2]))
                dve.wait_ge(S("norm_ssq"), n + 1)
                inverse_root(rstd[:, 0:2], ssq[:, 0:2], 2, D, EPS)
                for t in range(TOK):
                    ts(dst[:, t, :], src[:, t, :], rstd[:, t:t + 1], None, ALU.mult).then_inc(S("xn_ready"), 1)

            def norm_low(n, gain, hi, lo):
                for kp in range(KD // 2):
                    dve.wait_ge(S("norm_hi"), 4 * n + kp + 1)
                    o = banks[fills[f"norm{n}.{kp}"][0]]
                    for kk in range(2):
                        k = 2 * kp + kk
                        ins = stt(lo[:, k, :], o[:, kk * SEQ:(kk + 1) * SEQ], col(gain, k), f32(hi[:, k, :]),
                                  ALU.mult, ALU.subtract)
                    read(ins, f"norm{n}.{kp}")

            def ffn_part(n):
                f = ffn[n]

                done = FF_TILES * (n - 1)

                def hidden_tile(j, turn=0):
                    dve.wait_ge(S("ffn_gate"), done + j + 1 + 2 * turn)
                    if j >= 2:
                        dve.wait_ge(S("ffn_lo"), done + j - 1 + 2 * turn)
                    o = banks[fills[f"up{n}.{j}"][0]]
                    read(tt(f["act"][:, j % 2, :], o[:, SEQ:2 * SEQ], f["gate"][:, j % 2, :], ALU.mult), f"up{n}.{j}")
                    dve.wait_ge(S("ffn_hi"), done + j + 1 + 2 * turn)
                    tt(f["lo"][:, j % 2, :], f["act"][:, j % 2, :], f32(f["hi"][:, j % 2, :]), ALU.subtract)\
                        .then_inc(S("ffn_lo"), 1)

                for j in range(4):
                    hidden_tile(j)
                if n == 1:
                    dve.wait_ge(S("mem_in"), 16)
                    norm_rows(1, mem_xn, mem_xn, f["xn"])
                with dve.Fori(0, PAIR_TURNS) as turn:
                    hidden_tile(4, turn)
                    hidden_tile(5, turn)
                if n == 1:
                    norm_low(1, "mem_norm_g", mem_hi, mem_lo)
                i_post = 0 if n == 1 else 3
                dve.wait_ge(S("post_g_in"), 16 * (i_post + 1))
                for i in (2, 3, 0, 1):
                    t, h = i // 2, slice(i % 2 * 512, (i % 2 + 1) * 512)
                    key = f"down{n}.{i}"
                    o = full(dve, key)
                    if t == 0:
                        dve.wait_ge(S("post_ssq"), POST_SSQ[i_post] - 3 + i)
                    read(stt(f["xn"][:, t, h], o[:], 0.5, post_g[:, h], ALU.mult, ALU.mult), key)
                dve.wait_ge(S("post_ssq"), POST_SSQ[i_post])
                link(tt(post_sum[:], post_ssq[:, :, 0], post_ssq[:, :, 1], ALU.add))
                residual(i_post, [f"down{n}.{i}" for i in range(4)], f["xn"])

            def residual(i_post, keys, y):
                inverse_root(rstd[:, 2:4], post_sum[:], 2, D, EPS)
                for key in keys:
                    wait_read(dve, key)
                for t in range(TOK):
                    stt(x[:, t, :], y[:, t, :], rstd[:, 2 + t:3 + t], x[:, t, :], ALU.mult, ALU.add).then_inc(S("x_ready"), 1)
                dve.wait_ge(S("x_ready"), X_READY[i_post])

            def out_part(key, i_post, between=None):
                dve.wait_ge(S("post_g_in"), 16 * (i_post + 1))
                for i in range(4):
                    dve.wait_ge(S("post_ssq"), POST_SSQ[i_post - 1] + i + 1)
                    o = banks[fills[f"{key}{i}"][0]]
                    c = slice(i * 256, (i + 1) * 256)
                    read(tt(mg_T[:, :, c], two(o), post_g[:, c].unsqueeze(1).to_broadcast([P, TOK, 256]), ALU.mult), f"{key}{i}")
                    if between:
                        between(i)
                link(dve.tensor_reduce(post_sum[:], post_ssq[:], AX.X, ALU.add))
                residual(i_post, [f"{key}{i}" for i in range(4)], mg_T)

            def each(src, reps):
                return src.unsqueeze(2).to_broadcast([P, src.shape[1], reps])

            dve.wait_ge(S("x_in"), 16)
            norm_rows(0, x, ffn[1]["xn"], ffn[1]["xn"])
            def first_low(b):
                dve.wait_ge(w_hi_in, b + 1)
                h = slice(BLOCK // 2, BLOCK)
                tt(w_lo[b][:, h], w_raw[b][:, h], f32(w_hi[b][:, h]), ALU.subtract).then_inc(S("first_lo"), 1)

            first_low(0)
            dve.wait_ge(S("cols_in"), 16)
            norm_low(0, "ffn1_pre_g", hT_hi, hT_lo)
            first_low(1)
            ffn_part(1)

            norm_rows(2, x, mix_xn, mix_xn)
            norm_low(2, "mix_pre_g", hT_hi, hT_lo)
            dve.wait_ge(S("rows_in"), 32)
            def causal_conv(key, i, dst, w, b, first, taps):
                o = full(dve, key)
                for c in range(2):
                    ch = first + c
                    u, v = o[:, c * SEQ:(c + 1) * SEQ], dst[:, c, :]
                    link(ts(v, u, col(w, taps * ch + taps - 1), col(b, ch), ALU.mult, ALU.add))
                    for j in range(1, taps):
                        ins = stt(v[:, j:SEQ], u[:, 0:SEQ - j], col(w, taps * ch + taps - 1 - j), v[:, j:SEQ], ALU.mult, ALU.add)
                        if c == 0 or j < taps - 1:
                            link(ins)
                read(ins, key)

            def time_step(part):
                e, u, ln, c5 = ssd_dtt[:, 2], ssd_dtt[:, 3], ssd_dtt[:, 4], ssd_dtt[:, 5]
                if part == 0:
                    o = full(dve, "dtT")
                    read(tt(ssd_dtt[:, 0].rearrange("p (t h) -> p t h", t=TOK),
                            o[:, 0:TOK * SSD_HEADS].rearrange("p (t h) -> p t h", t=TOK),
                            row("ssd_dt_bias").unsqueeze(1).to_broadcast([P, TOK, SSD_HEADS]), ALU.add), "dtT")
                    wait_read(dve, "dtT")
                    link(ts(ssd_dtt[:, 1], ssd_dtt[:, 0], -1.0, None, ALU.mult))
                    tt(ssd_dtt[:, 1], ssd_dtt[:, 1], ssd_dtt[:, 0], ALU.min).then_inc(S("dt_abs"), 1)
                elif part == 1:
                    dve.wait_ge(S("dt_exp"), 2)
                    ts(u, e, 1.0, None, ALU.add).then_inc(S("dt_one"), 1)
                    dve.wait_ge(S("dt_one"), 1)
                    link(ts(c5, u, -1.0, None, ALU.add))
                    link(tt(c5, e, c5, ALU.subtract))
                    link(dve.reciprocal(ssd_dtt[:, 1], u))
                    link(tt(c5, c5, ssd_dtt[:, 1], ALU.mult))
                elif part == 2:
                    dve.wait_ge(S("dt_ln"), 1)
                    link(tt(ln, ln, c5, ALU.add))
                    link(stt(ssd_dt[:].rearrange("p t h -> p (t h)"), ssd_dtt[:, 0], 0.0, ln, ALU.max, ALU.add))
                    for t in range(TOK):
                        stt(ssd_A[:, t, :], ssd_dt[:, t, :], -1.0, ssd_eA[:], ALU.mult, ALU.mult).then_inc(S("ssd_A"), 1)
                else:
                    dve.wait_ge(S("ssd_A"), 2)
                    dve.wait_ge(S("ssd_A_hi"), 1)
                    link(tt(ssd_A_lo[:], ssd_A[:], f32(ssd_A_hi[:]), ALU.subtract))

            for i in range(12):
                if i >= 2:
                    dve.wait_ge(S("xbc_silu"), i - 1)
                causal_conv(f"xbc{i}", i, ssd_conv[:, i % 2], "ssd_conv_w", "ssd_conv_b", 2 * i, SSD_CONV)
                if i % 2 and i < 8:
                    time_step(i // 2)

            def ssd_inputs(c):
                tt(ssd_xdt[:].rearrange("p (h d) -> p h d", d=64), ssd_y[:, c, :].rearrange("p (h d) -> p h d", d=64),
                   each(ssd_dt[:, c, :], 64), ALU.mult).then_inc(S("ssd_xdt"), 1)

            def ssd_steps(u):
                c, g = divmod(u, SSD_GROUPS)
                for q in range(2):
                    h = 8 * g + 4 * q
                    for u_A, A in ((ssd_uA_hi, f32(ssd_A_hi[:])), (ssd_uA_lo, ssd_A_lo[:])):
                        ins = tt(u_A[:, q, :].rearrange("p (h l) -> p h l", h=4), upper.unsqueeze(1).to_broadcast([P, 4, P]),
                                 each(A[:, c, h:h + 4], P), ALU.mult)
                    ins.then_inc(S("ssd_uA"), 1)

            def ssd_rows(u):
                c, g = divmod(u, SSD_GROUPS)
                ys = ssd_y[:, c, g * 512:(g + 1) * 512]
                yh, th = ys.rearrange("p (h d) -> p h d", d=64), ssd_t[:].rearrange("p (h d) -> p h d", d=64)
                link(tt(th, yh, each(row("ssd_D")[:, 8 * g:8 * g + 8], 64), ALU.mult))
                o = full(dve, f"diag{u}")
                if c == 0:
                    read(tt(ys, o[:], ssd_t[:], ALU.add), f"diag{u}")
                    wait_read(dve, f"diag{u}")
                else:
                    read(tt(ys, o[:], ssd_t[:], ALU.add), f"diag{u}")
                    wait_read(dve, f"diag{u}")
                    o = full(dve, f"yoff{g}")
                    read(tt(th, o[:].rearrange("p (h d) -> p h d", d=64), each(ssd_ecs[:, 8 * g:8 * g + 8], 64), ALU.mult),
                         f"yoff{g}")
                    wait_read(dve, f"yoff{g}")
                    link(tt(ys, ys, ssd_t[:], ALU.add))

            for i in range(10):
                wait_read(dve, f"xT{i}")
            ssd_inputs(0)
            ssd_steps(0)
            dve.wait_ge(S("ssd_xdt"), 1)
            wait_read(dve, "sums")
            tt(ssd_xdd[:].rearrange("p (h d) -> p h d", d=64), ssd_xdt[:].rearrange("p (h d) -> p h d", d=64),
               each(ssd_decay[:], 64), ALU.mult).then_inc(S("ssd_xdd"), 1)
            dve.wait_ge(S("ssd_ecs"), 1)
            for i in range(1, 10):
                if i <= 8:
                    u = i - 1
                    if u:
                        dve.wait_ge(S("ssd_M"), 2 * u)
                    o = full(dve, f"cb{u}")
                    read(tt(ssd_cb[:], o[:, 0:P], upper, ALU.mult), f"cb{u}")
                    wait_read(dve, f"cb{u}")
                if i >= 2:
                    ssd_rows(i - 2)
                if i == 5:
                    ssd_inputs(1)
                if i <= 8:
                    for q in range(2):
                        wait_read(dve, f"seg{u}.{q}")
                        tt(ssd_M[:, q, :].rearrange("p (h l) -> p h l", h=4), ssd_L[:, q, :].rearrange("p (h l) -> p h l", h=4),
                           ssd_cb[:].unsqueeze(1).to_broadcast([P, 4, P]), ALU.mult).then_inc(S("ssd_M"), 1)
                    if u < 7:
                        ssd_steps(u + 1)

            for j in range(2):
                dve.tensor_tensor_reduce(da_junk2[:, j, :], row(f"da_lambda_q{j + 1}"), row(f"da_lambda_k{j + 1}"), 1.0, 0.0,
                                         ALU.mult, ALU.add, da_lam[:, j:j + 1]).then_inc(S("lam_dot"), 1)
            ts(sub_g[:], col("da_subln_g"), 1.0 - LAM_INIT, None, ALU.mult).then_inc(S("sub_g"), 1)
            dve.wait_ge(S("lam_exp"), 1)
            link(tt(da_lam[:, 0:1], da_lam[:, 3:4], da_lam[:, 2:3], ALU.subtract))
            link(ts(da_lam[:, 0:1], da_lam[:, 0:1], -LAM_INIT, None, ALU.add))

            def da_max(h):
                for j in range(2):
                    key = f"das{h}.{j}"
                    o = full(dve, key)
                    read(tt(da_s[:, j, :], o[:, 0:384], causal, ALU.add), key)
                for j in range(2):
                    wait_read(dve, f"das{h}.{j}")
                st = da_st[:, 0, :].rearrange("p (j q) -> p j q", j=2)
                link(dve.tensor_reduce(st[:, :, 0], da_s[:, :, 0:P], AX.X, ALU.max))
                link(dve.tensor_reduce(st[:, :, 1], da_s[:, :, P:P + SEQ], AX.X, ALU.max))
                ts(da_st[:, 1, :], da_st[:, 0, :], -DA_DIM ** -0.5, None, ALU.mult).then_inc(S("da_max"), 1)

            def da_probs(h):
                dve.wait_ge(S("da_exp"), 4 * h + 4)
                link(dve.reciprocal(da_st[:, 3, :], da_st[:, 2, :]))
                link(ts(da_st[:, 3, 2:4], da_st[:, 3, 2:4], da_lam[:, 0:1], None, ALU.mult))
                if h:
                    full(dve, f"daT{h - 1}")
                for q in range(2):
                    c = slice(0, P) if q == 0 else slice(P, P + SEQ)
                    link(ts(da_P[:, c], da_p[:, 0, c], da_st[:, 3, q:q + 1], None, ALU.mult))
                    stt(da_P[:, c], da_p[:, 1, c], da_st[:, 3, 2 + q:3 + q], da_P[:, c], ALU.mult, ALU.add)\
                        .then_inc(S("da_P"), 1)

            def gate_bias(key, i, dst, b):
                o = full(dve, key)
                for c in range(2):
                    ins = ts(dst[:, 2 * i + c, :], o[:, c * SEQ:(c + 1) * SEQ], col(b, 2 * i + c), None, ALU.add)
                read(ins, key)

            def y_low(kp):
                dve.wait_ge(S("y_hi"), Y_TURNS.index(kp) + 1)
                o = banks[fills[f"yT{kp}"][0]]
                for i in range(2):
                    k = 2 * kp + i
                    hi, lo = (hT_hi, hT_lo) if k < 8 else (y2_hi, y2_lo)
                    ins = stt(lo[:, k % 8, :], o[:, i * SEQ:(i + 1) * SEQ], col("ssd_norm_g", k), f32(hi[:, k % 8, :]),
                              ALU.mult, ALU.subtract)
                read(ins, f"yT{kp}")

            for i in range(16):
                if i < 8:
                    o = full(dve, f"z{i}")
                    read(dve.tensor_copy(ssd_z[:, :, i * 256:(i + 1) * 256], two(o)), f"z{i}")
                else:
                    gate_bias(f"gate{i - 8}", i - 8, mix_gate, "b_gate")
                if i >= 13:
                    y_low(i - 9)
                if i % 2 == 0:
                    da_max(i // 2)
                    da_probs(i // 2)
                if i == 8:
                    for t in range(TOK):
                        dve.wait_ge(S("z_silu"), t + 1)
                        tt(ssd_y[:, t, :], ssd_y[:, t, :], ssd_z[:, t, :], ALU.mult).then_inc(S("ssd_yg"), 1)
                if i == 11:
                    dve.wait_ge(S("ssd_ssq"), TOK * SSD_GROUPS)
                    inverse_root(rstd[:, 0:8], ssd_ssq[:].rearrange("p t g -> p (t g)"), 8, SSD_INNER // SSD_GROUPS, SUB_EPS)
                    for t in range(TOK):
                        for g in range(SSD_GROUPS):
                            c = slice(g * 512, (g + 1) * 512)
                            ts(ssd_y[:, t, c], ssd_y[:, t, c], rstd[:, 4 * t + g:4 * t + g + 1], None, ALU.mult)\
                                .then_inc(S("ssd_yn"), 1)
            y_low(7)

            for kp in range(4):
                y_low(kp)
            wait_read(dve, f"dao{DA_HEADS - 1}")
            dve.wait_ge(S("da_ssq"), TOK * DA_HEADS)
            dve.wait_ge(S("ssd_yn"), TOK * SSD_GROUPS)
            inverse_root(rstd[:], da_ssq[:].rearrange("p t h -> p (t h)"), TOK * DA_HEADS, 2 * DA_DIM, SUB_EPS)
            for t in range(TOK):
                oh = da_o[:, :, t, :]
                tt(oh, oh, each(rstd[:, t * DA_HEADS:(t + 1) * DA_HEADS], P), ALU.mult).then_inc(S("da_on"), 1)
            dve.wait_ge(S("mix_gate"), 1)
            for i in range(8):
                o = full(dve, f"ssd{i}")
                read(tt(mg[:, i, :], o[:, 0:SEQ], mix_gate[:, 8 + i, :], ALU.mult), f"ssd{i}")
                if i == 4:
                    for hp in range(4):
                        dve.wait_ge(S("o_hi"), hp + 1)
                        o = banks[fills[f"oT{hp}"][0]]
                        c = slice(2 * hp, 2 * hp + 2)
                        read(stt(o_lo[:, c, :], two(o), sub_g[:, 0:1], f32(o_hi[:, c, :]), ALU.mult, ALU.subtract), f"oT{hp}")
            dve.wait_ge(S("mix_gate"), 2)
            for i in range(8):
                wait_read(dve, f"ssd{i}")
            def hidden_arg(i):
                arg, turns, r = hid[:, 2 * i, :], fil_t[:, 0, :], fil_t[:, 1, :]
                o = full(dve, f"hid{i}")
                read(ts(arg, o[0:FILTER_HIDDEN, 0:SEQ], fcols[:, 2 * i:2 * i + 1], fcols[:, 2 * i + 1:2 * i + 2], ALU.add, ALU.mult),
                     f"hid{i}")
                wait_read(dve, f"hid{i}")
                link(ts(turns, arg, 1.0 / (2 * math.pi), ROUND, ALU.mult, ALU.add))
                link(ts(turns, turns, -ROUND, None, ALU.add))
                link(stt(r, turns, -TURN_HI, arg, ALU.mult, ALU.add))
                link(stt(r, turns, -TURN_MID, r, ALU.mult, ALU.add))
                link(stt(r, turns, -TURN_LO, r, ALU.mult, ALU.add))
                ts(arg, r, PI_BELOW, -PI_BELOW, ALU.min, ALU.max).then_inc(S("hid_arg"), 1)

            for i, c in enumerate(MIXED):
                key = f"attn{i}" if i < 3 else f"attn3.{i - 3}"
                o = full(dve, key)
                n = c.stop - c.start
                read(tt(mix_gate[:, c, :], o[:, 0:n * SEQ].rearrange("p (t c) -> p t c", t=n), mix_gate[:, c, :], ALU.mult), key)
                wait_read(dve, key)
                tt(mg[:, c, :], mg[:, c, :], mix_gate[:, c, :], ALU.add).then_inc(S("mixed"), 1)
                dve.wait_ge(S("mixed_hi"), i + 1)
                tt(mixed_lo[:, c, :], mg[:, c, :], f32(mixed_hi[:, c, :]), ALU.subtract).then_inc(S("mixed_lo"), 1)
                if i == 2:
                    hidden_arg(0)

            def mix_between(i):
                if i == 0:
                    hidden_arg(1)

            out_part("mix", 1, mix_between)

            norm_rows(3, x, xa_xn, xa_xn)
            norm_low(3, "xa_pre_g", hT_hi, hT_lo)

            def softmax_max(key, st, scale, sem):
                o = full(dve, key)
                link(dve.tensor_reduce(st[:, 0, :], two(o), AX.X, ALU.max))
                ts(st[:, 1, :], st[:, 0, :], -scale, None, ALU.mult).then_inc(S(sem), 1)

            def softmax_scale(key, st, p, sem):
                wait_read(dve, key)
                link(dve.reciprocal(st[:, 3, :], st[:, 2, :]))
                for q in range(2):
                    ts(p[:, q, :], p[:, q, :], st[:, 3, q:q + 1], None, ALU.mult).then_inc(S(sem), 1)

            def filter_decay():
                for i in range(8):
                    wait_read(dve, f"taps{i}")
                dve.wait_ge(S("filter_in"), 5 * 16)
                for t in range(TOK):
                    k = kfil[:, t, :].rearrange("p (c d) -> p c d", c=4)
                    ins = tt(k, k, decay[:, t, :].unsqueeze(1).to_broadcast([P, 4, HY]), ALU.mult)
                link(ins)
                dve.wait_ge(S("bias_in"), 16)
                for n in range(2):
                    k = kfil[0:1, 0, 2 * n * HY:(2 * n + 1) * HY]
                    tt(k, k, bias_row[:, n, :], ALU.add).then_inc(S("kfil_bias"), 1)

            def xa_max(h):
                softmax_max(f"xas{h}", xa_st, XA_DIM ** -0.5, "xa_max")

            def xa_scale(h):
                softmax_scale(f"xas{h}", xa_st, xa_p[:, h % 2], "xa_P")

            def xa_low(h):
                dve.wait_ge(S("xo_hi"), h + 1)
                o = banks[fills[f"xao{h}"][0]]
                read(tt(xa_lo[:, 2 * h:2 * h + 2, :], two(o), f32(xa_hi[:, 2 * h:2 * h + 2, :]), ALU.subtract), f"xao{h}")

            filter_decay()
            for i in range(1, XA_HEADS):
                if i >= 3:
                    xa_low(i - 3)
                xa_max(i - 1)
                xa_scale(i - 1)
            xa_max(3)
            xa_low(1)
            xa_scale(3)
            xa_low(2)
            xa_low(3)
            out_part("xo", 2)

            norm_rows(4, x, ffn[2]["xn"], ffn[2]["xn"])
            norm_low(4, "ffn2_pre_g", hT_hi, hT_lo)
            ffn_part(2)

            norm_rows(5, x, sec_xn, sec_xn)
            norm_low(5, "g_norm_2", hT_hi, hT_lo)

            dve.wait_ge(S("c_ssq"), 4)
            inverse_root(rstd[:, 4:6], c_ssq[:, 0, :], 2, Q_LORA, EPS)
            inverse_root(rstd[:, 6:8], c_ssq[:, 1, :], 2, KV_LORA, EPS)
            for t in range(TOK):
                ts(cq[:, t, :], cq[:, t, :], rstd[:, 4 + t:5 + t], None, ALU.mult).then_inc(S("c_ready"), 1)
                ts(ckv[:, t, :], ckv[:, t, :], rstd[:, 6 + t:7 + t], None, ALU.mult).then_inc(S("c_ready"), 1)

            for k in range(5):
                dve.wait_ge(S("c_hi"), min(2 * (k // 2) + 2, 5))
                o = banks[fills[f"cT{k // 2}"][0]]
                hi, lo, g = (cq_hi[:, k, :], cq_lo[:, k, :], col("g_cq_2", k)) if k < 3 else \
                    (ckv_hi[:, k - 3, :], ckv_lo[:, k - 3, :], col("g_ckv_2", k - 3))
                ins = stt(lo, o[:, k % 2 * SEQ:(k % 2 + 1) * SEQ], g, f32(hi), ALU.mult, ALU.subtract)
                if k % 2 or k == 4:
                    read(ins, f"cT{k // 2}")

            dve.wait_ge(S("rope_in"), 16)

            def head_norm(s):
                r = mq[:, s].rearrange("p t h d -> p (t h) d")
                n = TOK * MLA_HEADS
                sq = msq[:].rearrange("p t h d -> p (t h) d")
                link(tt(sq, r, r, ALU.mult))
                link(dve.tensor_reduce(m_ssq[:], sq, AX.X, ALU.add))
                inverse_root(rstd[:], m_ssq[:], n, QK_DIM, EPS)
                link(tt(r, r, each(rstd[:], QK_DIM), ALU.mult))
                g = row("g_qn_2" if s == 0 else "g_kn_2")
                link(tt(r, r, g.unsqueeze(1).to_broadcast([P, n, QK_DIM]), ALU.mult))

            def head_turn(s):
                for t in range(TOK):
                    cos, sin = (m_ropeT[:, t, i * 16:(i + 1) * 16].unsqueeze(1).to_broadcast([P, MLA_HEADS, 16]) for i in range(2))
                    a1, a2 = mq[:, s, t, :, 64:80], mq[:, s, t, :, 80:96]
                    parts = [m_t[:, i, t] for i in range(4)]
                    tt(parts[0], a1, cos, ALU.mult)
                    tt(parts[1], a2, sin, ALU.mult)
                    tt(parts[2], a1, sin, ALU.mult)
                    link(tt(parts[3], a2, cos, ALU.mult))
                    link(tt(a1, parts[0], parts[1], ALU.subtract))
                    ins = tt(a2, parts[2], parts[3], ALU.add)
                    if t == 0:
                        link(ins)
                ins.then_inc(S("mla_qk"), 1)

            def centred_conv(i):
                key = f"hy{i}"
                dve.wait_ge(S("hy_mid"), 2 * i + 2)
                o = banks[fills[key][0]]
                for c in range(2):
                    ch = 2 * i + c
                    u, v = o[:, c * SEQ:(c + 1) * SEQ], hyF[:, ch, :]
                    link(stt(v[:, 1:SEQ], u[:, 0:SEQ - 1], col("w_short_2", 3 * ch), v[:, 1:SEQ], ALU.mult, ALU.add))
                    ins = stt(v[:, 0:SEQ - 1], u[:, 1:SEQ], col("w_short_2", 3 * ch + 2), v[:, 0:SEQ - 1], ALU.mult, ALU.add)
                read(ins, key)

            for t in range(TOK):
                wait_read(dve, f"uq0.{t}.0")
                wait_read(dve, f"uq1.{t}.0")
            head_norm(0)
            head_turn(0)
            for t in range(TOK):
                for h in (0, 512):
                    wait_read(dve, f"ukv.{t}.{h}")
            wait_read(dve, "cq1")
            for t in range(TOK):
                ins = dve.tensor_copy(mq[:, 1, t, :, QK_NOPE:], k_rope[:, t, :].unsqueeze(1).to_broadcast([P, MLA_HEADS, QK_ROPE]))
            link(ins)
            centred_conv(0)
            centred_conv(1)
            head_norm(1)
            centred_conv(2)
            head_turn(1)
            for i in range(3, 6):
                centred_conv(i)
            for j in range(8):
                wait_read(dve, f"spec{j}")
            for i in range(6):
                wait_read(dve, f"hy{i}")

            def hyena_product(n, f):
                kr, ki = spec[:, n, f, :], spec[:, n, f + 2, :]
                if n or f:
                    dve.wait_ge(S("hy_yf"), 4 * n + 2 * f)
                ur, ui = full(dve, f"uf{n}.{f}"), full(dve, f"uf{n}.{f + 2}")
                tt(yt[:, 0, :], ui[:], ki, ALU.mult)
                read(tt(yt[:, 1, :], ui[:], kr, ALU.mult), f"uf{n}.{f + 2}")
                wait_read(dve, f"uf{n}.{f + 2}")
                tt(ki, ur[:], ki, ALU.mult)
                read(tt(kr, ur[:], kr, ALU.mult), f"uf{n}.{f}")
                wait_read(dve, f"uf{n}.{f}")
                tt(kr, kr, yt[:, 0, :], ALU.subtract).then_inc(S("hy_yf"), 1)
                tt(ki, ki, yt[:, 1, :], ALU.add).then_inc(S("hy_yf"), 1)

            def hyena_gate(n):
                for cp in range(2):
                    key = f"yt{n}.{cp}"
                    o = full(dve, key)
                    k = 4 * (n + 1) + 2 * cp
                    read(tt(hyF[:, 2 * cp:2 * cp + 2, :], two(o), hyF[:, k:k + 2, :], ALU.mult), key)

            def softmax_rows(h):
                softmax_max(f"ms{h}", m_st, QK_DIM ** -0.5, "m_max")
                softmax_scale(f"ms{h}", m_st, m_p[:, h % 2], "m_P")

            def at_low(c):
                dve.wait_ge(S("at_hi"), c + 1)
                tt(at_lo[:, c, :], z_at[:, c, :], f32(at_hi[:, c, :]), ALU.subtract).then_inc(S("at_lo"), 1)

            def fin_low(i):
                dve.wait_ge(S("fin_hi"), i + 1)
                tt(hT_lo[:, 2 * i:2 * i + 2, :], mg2[:, 2 * i:2 * i + 2, :], f32(hT_hi[:, 2 * i:2 * i + 2, :]), ALU.subtract)\
                    .then_inc(S("fin_lo"), 1)

            def wide_gate(i, first):
                for p in range(2):
                    key = f"{'hyo' if first else 'ato'}{i}.{p}"
                    o = full(dve, key)
                    k = 4 * i + 2 * p
                    m, g = mg2[:, k:k + 2, :], gate2[:, (0 if first else 8) + k:(0 if first else 8) + k + 2, :]
                    if first:
                        read(tt(m, two(o), g, ALU.mult), key)
                    else:
                        read(tt(g, two(o), g, ALU.mult), key)
                        wait_read(dve, key)
                        tt(m, m, g, ALU.add).then_inc(S("fin"), 1)
                        if 2 * i + p:
                            fin_low(2 * i + p - 1)

            for i in range(MLA_HEADS + 2):
                c = (i - 3) // 2
                if i >= 3 and i % 2:
                    o = full(dve, f"mo{c}")
                    read(tt(z_at[:, c, :], o[:, 0:SEQ], z_at[:, c, :], ALU.mult), f"mo{c}")
                if i < MLA_HEADS:
                    softmax_rows(i)
                if i >= 3 and i % 2:
                    at_low(c)
                if i in (0, 1, 4, 5):
                    hyena_product(i // 4, i % 4)
                elif i in (2, 6):
                    hyena_gate(i // 4)
                elif i == 3:
                    link(tt(hyF[:, 8:12, :], hyF[:, 8:12, :], z_hy[:], ALU.mult))
                if i == 6:
                    for j in range(HY_TILES):
                        dve.wait_ge(S("hy_hi"), j + 1)
                        tt(hy_lo[:, j, :], hyF[:, j, :], f32(hy_hi[:, j, :]), ALU.subtract).then_inc(S("hy_lo"), 1)
                if i == 8:
                    dve.wait_ge(S("gate2"), 1)
                if i >= 8:
                    wide_gate(i - 8, True)
            dve.wait_ge(S("gate2"), 2)
            for i in range(2):
                for p in range(2):
                    wait_read(dve, f"hyo{i}.{p}")
            for i in range(2):
                wide_gate(i, False)
            fin_low(3)
            for i in range(4):
                o = full(dve, f"out{i}")
                c = slice(i * 256, (i + 1) * 256)
                tt(x[:, :, c], two(o), x[:, :, c], ALU.add).then_inc(S("out_ready"), 1)

        @block.gpsimd
        def _(pool):
            def low_half(b, slot, stage):
                pool.wait_ge(w_hi_in, b + 1)
                pool.tensor_tensor(w_lo[stage][:], w_raw[slot][:], w_hi[stage][:].bitcast(F32), ALU.subtract)\
                    .then_inc(w_lo_in, 1)

            h = slice(0, BLOCK // 2)
            for b in range(2):
                pool.wait_ge(w_hi_in, b + 1)
                pool.tensor_tensor(w_lo[b][:, h], w_raw[b][:, h], w_hi[b][:, h].bitcast(F32), ALU.subtract).then_inc(w_lo_in, 1)
            low_half(2, 2, 2)
            with pool.Fori(1, NBLOCK // RING) as turn:
                for i in range(RING):
                    low_half(turn * RING + i, i, i)

        @block.sync
        def _(sp):
            sp.dma_start(x[:], a["x"].rearrange("(t p) d -> p t d", p=P)).then_inc(S("x_in"), 16)
            for b in range(RING):
                sp.dma_start(w_raw[b][:], a["w"][b]).then_inc(w_landed[b], 16)
                if b == 0:
                    sp.dma_start(square[:], a["c_square"]).then_inc(S("square_in"), 16)
                    sp.dma_start(cols[:], a["cols"]).then_inc(S("cols_in"), 16)
            sp.wait_ge(S("first_lo"), 2)
            with sp.Fori(1, NBLOCK // RING) as turn:
                for i in range(RING):
                    sp.wait_ge(w_lo_in, (turn - 1) * RING + i + 1)
                    sp.dma_start(w_raw[i][:], a["w"][bass.ds(turn * RING + i, 1)].rearrange("b p c -> p (b c)"))\
                        .then_inc(w_landed[i], 16)
            for i in range(4):
                sp.wait_ge(S("out_ready"), i + 1)
                c = slice(i * 256, (i + 1) * 256)
                sp.dma_start(out.rearrange("(t p) d -> p t d", p=P)[:, :, c], x[:, :, c]).then_inc(S("out_in"), 16)
            sp.wait_ge(S("out_in"), 64)


def kernel(**inputs):
    import concourse.bacc as bacc
    from concourse.bass_utils import run_bass_kernel_spmd

    given = {name: np.asarray(value) for name, value in inputs.items()}
    arrays = {"x": given["x"][0], "mem": given["mem"][0]}

    stream = np.zeros((NBLOCK, P, BLOCK), np.float32)
    for n, (_, w, first, kt, columns) in enumerate(BLOCKS):
        rows = given[w][0][first:first + kt * P].reshape(kt, P, -1).transpose(1, 0, 2)
        width = sum(c for _, c in columns)
        part = stream[n, :, 0:kt * width].reshape(P, kt, width)
        at = 0
        for c, m in columns:
            part[:, :, at:at + m] = rows[:, :, c:c + m]
            at += m
    arrays["w"] = stream

    def over_partitions(v):
        v = v.reshape(-1, v.shape[-1])
        return v.reshape(v.shape[0], -1, P).transpose(2, 1, 0).reshape(P, -1)

    arrays["cols"] = np.concatenate([over_partitions(given[n][0]) for n in COLS], axis=1)
    arrays["rows"] = np.concatenate([given[n][0].reshape(1, -1) for n in ROWS], axis=1)
    arrays["fcols"] = np.stack([given[n][0] for n in ("b_f1_2", "freq_1_2", "b_f2_2", "freq_2_2")], axis=1)
    for n in POST + ["w_f1_2", "w_f2_2", "w_f3_2"]:
        arrays[n] = given[n][0].reshape(1, -1) if n in POST else given[n][0]
    arrays["hy_bias"] = given["hy_bias_2"][0]
    arrays.update(shape_constants())
    arrays = {n: np.ascontiguousarray(v) for n, v in arrays.items()}

    nc = bacc.Bacc("TRN2", target_bir_lowering=False, num_devices=1)
    a = {n: nc.dram_tensor(f"in_{n}", v.shape, mybir.dt.from_np(v.dtype), kind="ExternalInput").ap()
         for n, v in arrays.items()}
    out = nc.dram_tensor("out", (SEQ, D), F32, kind="ExternalOutput").ap()
    program(nc, a, out)
    r = run_bass_kernel_spmd(nc, [{f"in_{n}": v for n, v in arrays.items()}], core_ids=[0])
    return r.results[0]["out"].reshape(1, SEQ, D)
```
